# Optimizing a Trainium2 kernel written in Bass

```python
import jax, jax.numpy as jnp
from jax import lax
import numpy as np

D_MODEL = 1024
BATCH = 1
SEQ = 1024
DEPTH = 1
DEC_BATCH = 1
DEC_SEQ = 32
PAST_LEN = 128

CHUNK = 64
PLE_DIM = 256
MIX_WIDTH = D_MODEL
CONV_CH = MIX_WIDTH // 2
POOL_CH = MIX_WIDTH - CONV_CH
CONV_K = 31
POOL_WINDOWS = (2, 4, 8, 16)
N_POOL_GROUPS = len(POOL_WINDOWS)
POOL_GROUP = POOL_CH // N_POOL_GROUPS
POOL_HIST = max(POOL_WINDOWS) - 1
IN_COLS = 2 * CONV_CH + POOL_CH
N_EXPERT_GROUPS = 4
EXPERTS_PER_GROUP = 8
N_EXPERTS = N_EXPERT_GROUPS * EXPERTS_PER_GROUP
TOP_K = 2
D_EXPERT = D_MODEL // 2
DISPATCH_BLOCK = 128
EPS = 1e-6

kernel_name = "hybrid_conv_pool_hmoe_stream_step"

def rmsnorm(x, g):
    xf = x.astype(jnp.float32)
    y = xf * lax.rsqrt(jnp.mean(xf * xf, axis=-1, keepdims=True) + EPS)
    return (y * g.astype(jnp.float32)).astype(x.dtype)

def layernorm(x, g, b):
    xf = x.astype(jnp.float32)
    mu = jnp.mean(xf, axis=-1, keepdims=True)
    xc = xf - mu
    y = xc * lax.rsqrt(jnp.mean(xc * xc, axis=-1, keepdims=True) + EPS)
    return (y * g.astype(jnp.float32) + b.astype(jnp.float32)).astype(x.dtype)

def causal_dwconv(a_ext, w, b):
    y = lax.conv_general_dilated(
        a_ext, w.astype(a_ext.dtype)[:, None, :], window_strides=(1,), padding='VALID',
        dimension_numbers=('NWC', 'WIO', 'NWC'), feature_group_count=a_ext.shape[-1])
    return y + b.astype(a_ext.dtype)

def multiscale_pool(u_ext, pos0, w_lin, scale):
    n, L, C = u_ext.shape
    T = L - POOL_HIST
    uf = u_ext.astype(jnp.float32)
    cs = jnp.concatenate([jnp.zeros((n, 1, C), jnp.float32), jnp.cumsum(uf, axis=1)], axis=1)
    pos = pos0 + jnp.arange(T)
    outs = []
    for g, w in enumerate(POOL_WINDOWS):
        sl = slice(g * POOL_GROUP, (g + 1) * POOL_GROUP)
        wsum = cs[:, POOL_HIST + 1:POOL_HIST + 1 + T, sl] - cs[:, POOL_HIST + 1 - w:POOL_HIST + 1 - w + T, sl]
        cnt = jnp.minimum(w, pos + 1).astype(jnp.float32)[None, :, None]
        outs.append(wsum / cnt - uf[:, POOL_HIST:, sl])
    pooled = jnp.stack(outs, axis=2)
    mixed = jnp.einsum('ntgc,gcd->ntgd', pooled, w_lin.astype(jnp.float32)).reshape(n, T, C)
    return (mixed * scale.astype(jnp.float32)).astype(u_ext.dtype)

def hier_moe(h, w_rg, b_rg, w_re, b_re, w_gate, w_up, w_down):
    T, D = h.shape
    hf = h.astype(jnp.float32)
    g_logits = hf @ w_rg.astype(jnp.float32) + b_rg.astype(jnp.float32)
    g_prob = jax.nn.softmax(g_logits, axis=-1)
    g_sel = jnp.argmax(g_logits, axis=-1)
    g_w = jnp.take_along_axis(g_prob, g_sel[:, None], axis=1)
    e_logits = (hf @ w_re.astype(jnp.float32) + b_re.astype(jnp.float32)).reshape(T, N_EXPERT_GROUPS, EXPERTS_PER_GROUP)
    e_logits = jnp.take_along_axis(e_logits, g_sel[:, None, None], axis=1)[:, 0]
    e_val, e_idx = lax.top_k(e_logits, TOP_K)
    gate = (jax.nn.softmax(e_val, axis=-1) * g_w).reshape(-1)
    eid = (g_sel[:, None] * EXPERTS_PER_GROUP + e_idx).reshape(-1)
    tok = jnp.broadcast_to(jnp.arange(T)[:, None], (T, TOP_K)).reshape(-1)
    A = T * TOP_K
    order = jnp.argsort(eid)
    eid_s, tok_s, gate_s = eid[order], tok[order], gate[order]
    counts = jnp.zeros((N_EXPERTS,), jnp.int32).at[eid].add(1)
    start = jnp.cumsum(counts) - counts
    padded = (counts + DISPATCH_BLOCK - 1) // DISPATCH_BLOCK * DISPATCH_BLOCK
    pend = jnp.cumsum(padded)
    pstart = pend - padded
    slot = pstart[eid_s] + jnp.arange(A) - start[eid_s]
    n_blocks = (A + N_EXPERTS * (DISPATCH_BLOCK - 1) + DISPATCH_BLOCK - 1) // DISPATCH_BLOCK
    slot_tok = jnp.zeros((n_blocks * DISPATCH_BLOCK,), jnp.int32).at[slot].set(tok_s)
    blk_e = jnp.minimum(jnp.searchsorted(pend, jnp.arange(n_blocks) * DISPATCH_BLOCK, side='right'), N_EXPERTS - 1)
    xb = h[slot_tok].reshape(n_blocks, DISPATCH_BLOCK, D)

    def expert_block(args):
        xe, e = args
        hid = jax.nn.silu(xe @ w_gate[e]) * (xe @ w_up[e])
        return hid @ w_down[e]

    yb = lax.map(expert_block, (xb, blk_e)).reshape(-1, D)
    contrib = yb[slot] * gate_s[:, None].astype(h.dtype)
    return jnp.zeros_like(h).at[tok_s].add(contrib)

def trunk(x, p, conv_hist, pool_hist, pos0, params):
    (g_mix, w_in, w_dw, b_dw, g_conv_ln, b_conv_ln, w_pw, b_pw, w_pool, pool_scale, w_out,
     g_ffn, w_route_group, b_route_group, w_route_expert, b_route_expert,
     w_exp_gate, w_exp_up, w_exp_down, g_ple, w_ple_gate, b_ple_gate, w_ple_proj, g_final) = params
    n, T, D = x.shape
    conv_new, pool_new = [], []
    for i in range(DEPTH):
        h = rmsnorm(x, g_mix[i])
        z = h @ w_in[i]
        a = z[..., :CONV_CH] * jax.nn.sigmoid(z[..., CONV_CH:2 * CONV_CH])
        u = z[..., 2 * CONV_CH:]
        a_ext = jnp.concatenate([conv_hist[i].astype(a.dtype), a], axis=1)
        u_ext = jnp.concatenate([pool_hist[i].astype(u.dtype), u], axis=1)
        conv_new.append(a_ext[:, -(CONV_K - 1):])
        pool_new.append(u_ext[:, -POOL_HIST:])
        c = jax.nn.silu(layernorm(causal_dwconv(a_ext, w_dw[i], b_dw[i]), g_conv_ln[i], b_conv_ln[i]))
        o_a = c @ w_pw[i] + b_pw[i]
        o_b = multiscale_pool(u_ext, pos0, w_pool[i], pool_scale[i])
        x = x + jnp.concatenate([o_a, o_b], axis=-1) @ w_out[i]
        h2 = rmsnorm(x, g_ffn[i])
        x = x + hier_moe(h2.reshape(n * T, D), w_route_group[i], b_route_group[i], w_route_expert[i],
                         b_route_expert[i], w_exp_gate[i], w_exp_up[i], w_exp_down[i]).reshape(n, T, D)
        gate = jax.nn.sigmoid(rmsnorm(x, g_ple[i]) @ w_ple_gate[i] + b_ple_gate[i])
        x = x + gate * (p[i].astype(x.dtype) @ w_ple_proj[i])
    return rmsnorm(x, g_final), jnp.stack(conv_new), jnp.stack(pool_new)

def setup_inputs(seed: int = 0) -> dict:
    key = jax.random.key(seed)
    ks = iter(jax.random.split(key, 40))
    f32 = jnp.float32

    def nrm(shape, scale):
        return jax.random.normal(next(ks), shape, f32) * scale

    def gain(shape):
        return 1.0 + 0.01 * jax.random.normal(next(ks), shape, f32)

    return {
        "x_prompt": nrm((BATCH, SEQ, D_MODEL), 1.0),
        "x_sample": nrm((DEC_BATCH, DEC_SEQ, D_MODEL), 1.0),
        "state_conv": nrm((DEPTH, DEC_BATCH, CONV_K - 1, CONV_CH), 0.5),
        "state_pool": nrm((DEPTH, DEC_BATCH, POOL_HIST, POOL_CH), 0.5),
        "p_prompt": nrm((DEPTH, BATCH, SEQ, PLE_DIM), 1.0),
        "p_sample": nrm((DEPTH, DEC_BATCH, DEC_SEQ, PLE_DIM), 1.0),
        "g_mix": gain((DEPTH, D_MODEL)),
        "w_in": nrm((DEPTH, D_MODEL, IN_COLS), D_MODEL ** -0.5),
        "w_dw": nrm((DEPTH, CONV_K, CONV_CH), CONV_K ** -0.5),
        "b_dw": nrm((DEPTH, CONV_CH), 0.02),
        "g_conv_ln": gain((DEPTH, CONV_CH)),
        "b_conv_ln": nrm((DEPTH, CONV_CH), 0.02),
        "w_pw": nrm((DEPTH, CONV_CH, CONV_CH), CONV_CH ** -0.5),
        "b_pw": nrm((DEPTH, CONV_CH), 0.02),
        "w_pool": nrm((DEPTH, N_POOL_GROUPS, POOL_GROUP, POOL_GROUP), POOL_GROUP ** -0.5),
        "pool_scale": 1.0 + 0.1 * jax.random.normal(next(ks), (DEPTH, POOL_CH), f32),
        "w_out": nrm((DEPTH, MIX_WIDTH, D_MODEL), MIX_WIDTH ** -0.5),
        "g_ffn": gain((DEPTH, D_MODEL)),
        "w_route_group": nrm((DEPTH, D_MODEL, N_EXPERT_GROUPS), D_MODEL ** -0.5),
        "b_route_group": nrm((DEPTH, N_EXPERT_GROUPS), 0.01),
        "w_route_expert": nrm((DEPTH, D_MODEL, N_EXPERTS), D_MODEL ** -0.5),
        "b_route_expert": nrm((DEPTH, N_EXPERTS), 0.01),
        "w_exp_gate": nrm((DEPTH, N_EXPERTS, D_MODEL, D_EXPERT), D_MODEL ** -0.5),
        "w_exp_up": nrm((DEPTH, N_EXPERTS, D_MODEL, D_EXPERT), D_MODEL ** -0.5),
        "w_exp_down": nrm((DEPTH, N_EXPERTS, D_EXPERT, D_MODEL), D_EXPERT ** -0.5),
        "g_ple": gain((DEPTH, D_MODEL)),
        "w_ple_gate": nrm((DEPTH, D_MODEL, D_MODEL), D_MODEL ** -0.5),
        "b_ple_gate": nrm((DEPTH, D_MODEL), 0.02),
        "w_ple_proj": nrm((DEPTH, PLE_DIM, D_MODEL), PLE_DIM ** -0.5),
        "g_final": gain((D_MODEL,)),
    }

def reference(x_prompt, x_sample, state_conv, state_pool, p_prompt, p_sample,
              g_mix, w_in, w_dw, b_dw, g_conv_ln, b_conv_ln, w_pw, b_pw, w_pool, pool_scale, w_out,
              g_ffn, w_route_group, b_route_group, w_route_expert, b_route_expert,
              w_exp_gate, w_exp_up, w_exp_down, g_ple, w_ple_gate, b_ple_gate, w_ple_proj, g_final):
    assert x_sample.shape[1] <= CHUNK
    params = (g_mix, w_in, w_dw, b_dw, g_conv_ln, b_conv_ln, w_pw, b_pw, w_pool, pool_scale, w_out,
              g_ffn, w_route_group, b_route_group, w_route_expert, b_route_expert,
              w_exp_gate, w_exp_up, w_exp_down, g_ple, w_ple_gate, b_ple_gate, w_ple_proj, g_final)
    nb = x_prompt.shape[0]
    zero_conv = jnp.zeros((DEPTH, nb, CONV_K - 1, CONV_CH), x_prompt.dtype)
    zero_pool = jnp.zeros((DEPTH, nb, POOL_HIST, POOL_CH), x_prompt.dtype)
    y_prompt, conv_p, pool_p = trunk(x_prompt, p_prompt, zero_conv, zero_pool, 0, params)
    y_sample, conv_s, pool_s = trunk(x_sample, p_sample, state_conv, state_pool, PAST_LEN, params)
    return (y_prompt, y_sample, conv_p, pool_p, conv_s, pool_s)


_drawn_inputs = setup_inputs


def setup_inputs(seed=0):
    import zlib

    import numpy as np

    out = dict(_drawn_inputs(seed))
    spreads = {}
    factors = {'g_mix': 18.466,
     'g_conv_ln': 32.461,
     'b_conv_ln': 18.303,
     'b_route_group': 19.754,
     'b_route_expert': 50.24,
     'g_ple': 200.0,
     'b_ple_gate': 200.0,
     'g_final': 200.0,
     'state_pool': 14.784,
     'b_dw': 5.055,
     'b_pw': 8.0,
     'g_ffn': 8.0,
     'p_prompt': 3.3,
     'p_sample': 3.255,
     'w_ple_gate': 4.699,
     'w_ple_proj': 3.289}
    for name, (base, spread) in spreads.items():
        noise = np.random.default_rng([zlib.crc32(name.encode()), seed]).standard_normal(out[name].shape)
        drawn = base * np.exp(spread * noise) if base else spread * noise
        out[name] = __import__('jax').numpy.asarray(drawn.astype(out[name].dtype))
    for name, factor in factors.items():
        out[name] = (out[name] * factor).astype(out[name].dtype)
    return out
```

```python
from contextlib import ExitStack

import concourse.bass as bass
from concourse import mybir

F32, F32R = mybir.dt.float32, mybir.dt.float32r
BF16, I32 = mybir.dt.bfloat16, mybir.dt.int32
ACT, ALU, AX = mybir.ActivationFunctionType, mybir.AluOpType, mybir.AxisListType

P = 128
D, SEQ, DEC, CH = 1024, 1024, 32, 512
PLE, TAPS, POOL_HIST, POOL_GROUPS = 256, 31, 15, 4
CONV_HIST = TAPS - 1
GROUPS, PER_GROUP, D_EXP = 4, 8, 512
EXPERTS = GROUPS * PER_GROUP
EPS = 1e-6

KD = D // P
KE = D_EXP // P
KC = CH // P
GAP = 32
SAMPLE = SEQ + GAP
TILES = (SAMPLE + DEC + P - 1) // P
ROWS = TILES * P
CHUNKS = 3
CHUNK = 364
COLS = CHUNKS * CHUNK
assert COLS >= SAMPLE + DEC and CHUNK <= 512 and GAP >= CONV_HIST

P_BDW, P_GLN, P_BLN, P_BPW, P_SCALE = TAPS, TAPS + 1, TAPS + 2, TAPS + 3, TAPS + 4
P_CHIST = TAPS + 5
P_PHIST = P_CHIST + CONV_HIST
P_ALL = P_PHIST + POOL_HIST

MAX_BLOCKS = (SEQ + DEC + P - 1) // P
MAX_EXTRA = 2 * (SEQ + DEC) // P
ITEMS = EXPERTS + MAX_EXTRA
RANKS = TILES * P
TABLE = EXPERTS * RANKS + 2 * P
PIECE = 2048


def split_views(t):
    return t[:].bitcast(F32)


def matmul3(pe, out, x_hi, x_lo, w_hi, w_lo, start, stop):
    pe.matmul(out, x_hi, w_hi, start=start, stop=False)
    pe.matmul(out, x_hi, w_lo, start=False, stop=False)
    return pe.matmul(out, x_lo, w_hi, start=False, stop=stop)


class Shared:
    pass


def constants_and_norm(nc, S, x_prompt, x_sample, state_conv, state_pool, g_mix, w_dw, b_dw,
                       g_conv_ln, b_conv_ln, b_pw, pool_scale):
    with ExitStack() as ctx:
        sb = lambda n, s, d=F32: ctx.enter_context(nc.sbuf_tensor(n, s, d))
        sem = lambda n: S.stack.enter_context(nc.semaphore(n))
        x = [sb(f"x_in{j}", [P, D]) for j in range(3)]
        xn = [sb(f"x_norm{j}", [P, D]) for j in range(3)]
        gain = sb("g_mix_rows", [P, D])
        ss, ms, rstd = sb("ss1", [P, 3]), sb("ms1", [P, 3]), sb("rstd1", [P, 3])
        rows = sb("param_rows", [P_ALL, CH])
        ps_t = [ctx.enter_context(nc.psum_tensor(f"ps_t{j}", [P, KD, P], F32)) for j in range(3)]
        ps_par = ctx.enter_context(nc.psum_tensor("ps_par", [P, KC, P_ALL], F32))
        x_loaded = [sem(f"x_loaded{j}") for j in range(3)]
        par_loaded, gain_loaded = sem("par_loaded"), sem("gain_loaded")
        const_set, ident_ready = sem("const_set"), sem("ident_ready")
        squared, mean_ready, rstd_ready = sem("squared"), sem("mean_ready"), sem("rstd_ready")
        norm_ready, turned, hi_ready, lo_ready = sem("norm_ready"), sem("turned"), sem("h_hi_ready"), sem("h_lo_ready")
        par_turned, par_ready = sem("par_turned"), sem("par_ready")
        with nc.Block() as block:

            @block.sync
            def _(sp):
                for t in range(TILES):
                    if t >= 3:
                        sp.wait_ge(norm_ready, t - 2)
                    if t < TILES - 1:
                        sp.dma_start(x[t % 3][:, :], x_prompt[0, t * P:(t + 1) * P, :]).then_inc(x_loaded[t % 3], 16)
                    else:
                        sp.dma_start(x[t % 3][GAP:GAP + DEC, :], x_sample[0]).then_inc(x_loaded[t % 3], 16)

            @block.gpsimd
            def _(pool):
                pool.memset(S.ident[:, :], 0.0).then_inc(const_set, 1)
                pool.wait_ge(const_set, 1)
                pool.affine_select(out=S.ident[:, :], in_=S.ident[:, :], compare_op=ALU.not_equal, fill=1.0,
                                   base=0, pattern=[[-1, P]], channel_multiplier=1).then_inc(ident_ready, 1)
                pool.memset(S.ones[:, :], 1.0)
                pool.memset(S.zero[:, :], 0.0)
                pool.memset(S.minus_half[:, :], -0.5).then_inc(const_set, 1)
                pool.wait_ge(const_set, 2)
                with pool.Fori(0, TILES // 3) as it:
                    pool.wait_ge(mean_ready, it + 2)
                    pool.tensor_tensor(rstd[:, :], ms[:, :], S.minus_half[:, 0:3], ALU.pow).then_inc(rstd_ready, 1)

            @block.scalar
            def _(act):
                act.dma_start(gain[:, :], g_mix[0].partition_broadcast(P)).then_inc(gain_loaded, 16)
                for at, part in ((0, w_dw[0]), (P_BDW, b_dw), (P_GLN, g_conv_ln), (P_BLN, b_conv_ln),
                                 (P_BPW, b_pw), (P_SCALE, pool_scale), (P_CHIST, state_conv[0, 0]),
                                 (P_PHIST, state_pool[0, 0])):
                    act.dma_start(rows[at:at + part.shape[0], :], part).then_inc(par_loaded, 16)
                with act.Fori(0, TILES // 3) as it:
                    act.wait_ge(mean_ready, it + 1)
                    for j in range(3):
                        act.wait_ge(x_loaded[j], it * 16 + 16)
                        act.activation(xn[j][:, :], x[j][:, :], ACT.Square, accum_out=ss[:, j:j + 1]).then_inc(squared, 1)
                    for j in range(3):
                        act.wait_ge(turned, it * 3 + (j + 1))
                        act.activation(S.h_hi[:, :, bass.ds(it * (3 * P) + j * P, P)], ps_t[j][:, :, :], ACT.Copy)\
                           .then_inc(hi_ready, 1)
                act.wait_ge(par_turned, 1)
                act.activation(S.par[:, :, :], ps_par[:, :, :], ACT.Copy).then_inc(par_ready, 1)

            @block.vector
            def _(dve):
                dve.sem_inc(mean_ready, 1)
                dve.wait_ge(gain_loaded, 16)
                with dve.Fori(0, TILES // 3) as it:
                    dve.wait_ge(squared, it * 3 + 3)
                    dve.tensor_scalar(ms[:, :], ss[:, :], 1.0 / D, EPS, ALU.mult, ALU.add).then_inc(mean_ready, 1)
                    dve.wait_ge(rstd_ready, it + 1)
                    for j in range(3):
                        dve.scalar_tensor_tensor(xn[j][:, :], x[j][:, :], rstd[:, j:j + 1], gain[:, :],
                                                 ALU.mult, ALU.mult).then_inc(norm_ready, 1)
                    for j in range(3):
                        dve.wait_ge(hi_ready, it * 3 + (j + 1))
                        cols = bass.ds(it * (3 * P) + j * P, P)
                        dve.tensor_tensor(S.h_lo[:, :, cols], ps_t[j][:, :, :], S.h_hi[:, :, cols].bitcast(F32),
                                          ALU.subtract).then_inc(lo_ready, 1)

            @block.tensor
            def _(pe):
                pe.wait_ge(ident_ready, 1)
                pe.wait_ge(par_loaded, 8 * 16)
                for c in range(KC):
                    last = pe.transpose(ps_par[:, c, :], rows[:, c * P:(c + 1) * P], S.ident[0:P_ALL, 0:P_ALL])
                last.then_inc(par_turned, 1)
                with pe.Fori(0, TILES // 3) as it:
                    for j in range(3):
                        pe.wait_ge(norm_ready, it * 3 + (j + 1))
                        for k in range(KD):
                            last = pe.transpose(ps_t[j][:, k, :], xn[j][:, k * P:(k + 1) * P], S.ident[:, :])
                        last.then_inc(turned, 1)


def in_projection_conv_pool(nc, S, w_in, w_pw, w_pool):
    PARTS = 3
    A_PAD, U_PAD = CONV_HIST, POOL_HIST
    with ExitStack() as ctx:
        sb = lambda n, s, d=F32: ctx.enter_context(nc.sbuf_tensor(n, s, d))
        sem = lambda n: S.stack.enter_context(nc.semaphore(n))
        raw = [sb(f"w_in_raw{s}", [P, KD, P]) for s in range(PARTS)]
        w_hi = [sb(f"w_in_hi{s}", [P, KD, P], F32R) for s in range(PARTS)]
        w_lo = [sb(f"w_in_lo{s}", [P, KD, P], F32R) for s in range(PARTS)]
        a_ext, u_ext = sb("a_ext", [P, A_PAD + COLS]), sb("u_ext", [P, U_PAD + COLS])
        sums = [sb(f"window_sum{i}", [P, U_PAD + COLS]) for i in range(2)]
        sig = sb("sigmoid_gate", [P, CHUNKS, CHUNK])
        inv = sb("inv_count", [P, POOL_GROUPS, 16])
        count = sb("count", [P, 16])
        tail = sb("state_tail", [P, KC, 90])
        state_rows = sb("state_rows", [90, CH])
        bank = [ctx.enter_context(nc.psum_tensor(f"z_bank{b}", [P, 512], F32)) for b in range(8)]
        a_bank, g_bank, u_bank = bank[0:3], bank[3:6], [bank[6], bank[7], bank[3]]
        raw_loaded = [sem(f"w_in_loaded{s}") for s in range(PARTS)]
        w_hi_ready = [sem(f"w_in_hi_ready{s}") for s in range(PARTS)]
        w_split = [sem(f"w_in_split{s}") for s in range(PARTS)]
        z_ready = [sem(f"z_ready{s}") for s in range(PARTS)]
        sig_ready, a_ready, a_whole, conv_step = sem("sig_ready"), sem("a_ready"), sem("a_whole"), sem("conv_step")
        u_ready, group_done, pool_step = sem("u_ready"), sem("group_done"), sem("pool_step")
        padded, inv_step, tail_turned, tail_ready = sem("padded"), sem("inv_step"), sem("tail_turned"), sem("tail_ready")
        state_stored, y_cleared = sem("state_stored"), sem("y_cleared")
        w_view = w_in[0].rearrange("(k p) n -> p k n", p=P)
        with nc.Block() as block:

            @block.sync
            def _(sp):
                def load(c, s):
                    sp.dma_start(raw[s][:, :, :], w_view[:, :, bass.ds(c * P + s * CH, P)]).then_inc(raw_loaded[s], 16)

                for s in range(PARTS):
                    load(0, s)
                with sp.Fori(1, KC) as c:
                    for s in range(PARTS):
                        sp.wait_ge(w_split[s], c)
                        load(c, s)
                sp.dma_start(S.w_pw[:, :, :], w_pw[0].rearrange("(k p) n -> p k n", p=P)).then_inc(S.mix_w_loaded, 16)
                sp.dma_start(S.w_pool[:, :, :], w_pool[0].rearrange("g c d -> c g d")).then_inc(S.mix_w_loaded, 16)
                with sp.Fori(EXPERTS, ITEMS) as i:
                    sp.dma_start(S.y_rows[bass.ds(i * P, P), :].rearrange("p (j n) -> p j n", n=P),
                                 S.zero[:, :].unsqueeze(1).to_broadcast([P, KD, P])).then_inc(y_cleared, 16)
                sp.wait_ge(tail_ready, 1)
                for at, n, out in ((0, CONV_HIST, S.conv_p), (CONV_HIST, CONV_HIST, S.conv_s),
                                   (2 * CONV_HIST, POOL_HIST, S.pool_p), (2 * CONV_HIST + POOL_HIST, POOL_HIST, S.pool_s)):
                    sp.dma_start(out[0, 0], state_rows[at:at + n, :]).then_inc(state_stored, 16)
                sp.wait_ge(state_stored, 4 * 16)
                sp.wait_ge(y_cleared, 16 * (ITEMS - EXPERTS))

            @block.scalar
            def _(act):
                def take_hi(c, s):
                    act.wait_ge(raw_loaded[s], c * 16 + 16)
                    act.activation(w_hi[s][:, :, :], raw[s][:, :, :], ACT.Copy).then_inc(w_hi_ready[s], 1)

                def gates(c):
                    for n in range(CHUNKS):
                        act.wait_ge(z_ready[1], c * CHUNKS + (n + 1))
                        act.activation(sig[:, n, :], g_bank[n][:, 0:CHUNK], ACT.Sigmoid).then_inc(sig_ready, 1)

                def us(c):
                    act.wait_ge(group_done, c + 1)
                    for n in range(CHUNKS):
                        act.wait_ge(z_ready[2], c * CHUNKS + (n + 1))
                        act.activation(u_ext[:, U_PAD + n * CHUNK:U_PAD + (n + 1) * CHUNK], u_bank[n][:, 0:CHUNK],
                                       ACT.Copy).then_inc(u_ready, 1)

                act.sem_inc(u_ready, CHUNKS)
                for s in range(PARTS):
                    take_hi(0, s)
                act.wait_ge(padded, 3)
                with act.Fori(0, KC - 1) as c:
                    act.wait_ge(z_ready[0], c * CHUNKS + CHUNKS)
                    take_hi(c + 1, 0)
                    gates(c)
                    take_hi(c + 1, 1)
                    us(c)
                    take_hi(c + 1, 2)
                gates(KC - 1)
                us(KC - 1)
                act.wait_ge(tail_turned, 1)
                act.activation(state_rows[:, :], bank[0][0:90, :], ACT.Copy).then_inc(tail_ready, 1)

            @block.gpsimd
            def _(pool):
                steps = [0]

                def step(ins):
                    steps[0] += 1
                    ins.then_inc(pool_step, 1)
                    pool.wait_ge(pool_step, steps[0])

                def take_lo(c, s):
                    pool.wait_ge(w_hi_ready[s], c + 1)
                    pool.tensor_tensor(w_lo[s][:, :, :], raw[s][:, :, :], w_hi[s][:, :, :].bitcast(F32),
                                       ALU.subtract).then_inc(w_split[s], 1)

                pool.sem_inc(group_done, 1)
                pool.memset(a_ext[:, 0:A_PAD], 0.0).then_inc(padded, 1)
                pool.memset(u_ext[:, 0:U_PAD], 0.0).then_inc(padded, 1)
                pool.memset(sums[0][:, 0:16], 0.0)
                pool.memset(sums[1][:, 0:16], 0.0).then_inc(padded, 1)
                pool.iota(count[:, :], pattern=[[1, 16]], base=1, channel_multiplier=0,
                          allow_small_or_imprecise_dtypes=True).then_inc(inv_step, 1)
                for s in range(PARTS):
                    take_lo(0, s)
                pool.wait_ge(inv_step, 2 + POOL_GROUPS)
                for c in range(KC):
                    if c + 1 < KC:
                        for s in range(PARTS):
                            take_lo(c + 1, s)
                    pool.wait_ge(a_whole, c + 1)
                    pool.tensor_copy(tail[:, c, 0:CONV_HIST], a_ext[:, SEQ:SEQ + CONV_HIST])
                    pool.tensor_copy(tail[:, c, CONV_HIST:2 * CONV_HIST],
                                     a_ext[:, SAMPLE + DEC:SAMPLE + DEC + CONV_HIST])
                    pool.wait_ge(u_ready, (c + 2) * CHUNKS)
                    step(pool.tensor_copy(u_ext[:, SAMPLE:SAMPLE + POOL_HIST], S.par[:, c, P_PHIST:P_ALL]))
                    pool.tensor_copy(tail[:, c, 2 * CONV_HIST:2 * CONV_HIST + POOL_HIST], u_ext[:, SEQ:SEQ + POOL_HIST])
                    pool.tensor_copy(tail[:, c, 2 * CONV_HIST + POOL_HIST:90],
                                     u_ext[:, SAMPLE + DEC:SAMPLE + DEC + POOL_HIST])
                    src = u_ext
                    for i in range(c + 1):
                        d = 1 << i
                        first = 2 * d - 1
                        dst = sums[i % 2]
                        step(pool.tensor_tensor(dst[:, first:], src[:, first:], src[:, first - d:U_PAD + COLS - d], ALU.add))
                        src = dst
                    mean = sums[(c + 1) % 2]
                    pool.tensor_tensor(mean[:, U_PAD:U_PAD + 16], src[:, U_PAD:U_PAD + 16], inv[:, c, :], ALU.mult)
                    step(pool.tensor_scalar(mean[:, U_PAD + 16:], src[:, U_PAD + 16:], 1.0 / (2 << c), None, ALU.mult))
                    pool.tensor_tensor(S.pooled[:, c, :], mean[:, U_PAD:], u_ext[:, U_PAD:], ALU.subtract)\
                        .then_inc(group_done, 1)

            @block.vector
            def _(dve):
                dve.sem_inc(a_ready, CHUNKS)
                dve.wait_ge(inv_step, 1)
                for g in range(POOL_GROUPS):
                    dve.tensor_scalar(inv[:, g, :], count[:, :], float(2 << g), None, ALU.min).then_inc(inv_step, 1)
                dve.wait_ge(inv_step, 1 + POOL_GROUPS)
                dve.reciprocal(inv[:, :, :], inv[:, :, :]).then_inc(inv_step, 1)
                dve.wait_ge(padded, 1)
                with dve.Fori(0, KC) as c:
                    dve.wait_ge(group_done, c + 1)
                    for n in range(CHUNKS):
                        dve.wait_ge(sig_ready, c * CHUNKS + (n + 1))
                        dve.tensor_tensor(a_ext[:, A_PAD + n * CHUNK:A_PAD + (n + 1) * CHUNK], a_bank[n][:, 0:CHUNK],
                                          sig[:, n, :], ALU.mult).then_inc(a_ready, 1)
                    dve.wait_ge(a_ready, c * CHUNKS + 2 * CHUNKS)
                    dve.tensor_copy(a_ext[:, SAMPLE:SAMPLE + CONV_HIST],
                                    S.par[:, bass.ds(c, 1), P_CHIST:P_PHIST]).then_inc(a_whole, 1)
                    dve.wait_ge(a_whole, c + 1)
                    out = S.conv[:, bass.ds(c, 1), :]
                    dve.tensor_scalar(out, a_ext[:, 0:COLS], S.par[:, bass.ds(c, 1), 0:1],
                                      S.par[:, bass.ds(c, 1), P_BDW:P_BDW + 1], ALU.mult, ALU.add).then_inc(conv_step, 1)
                    for k in range(1, TAPS):
                        dve.wait_ge(conv_step, c * TAPS + k)
                        dve.scalar_tensor_tensor(out, a_ext[:, k:k + COLS], S.par[:, bass.ds(c, 1), k:k + 1], out,
                                                 ALU.mult, ALU.add).then_inc(conv_step, 1)
                    dve.wait_ge(conv_step, c * TAPS + TAPS)

            @block.tensor
            def _(pe):
                with pe.Fori(0, KC) as c:
                    for s, banks in ((0, a_bank), (1, g_bank), (2, u_bank)):
                        pe.wait_ge(w_split[s], c + 1)
                        for n in range(CHUNKS):
                            if s == 0:
                                pe.wait_ge(a_ready, c * CHUNKS + (n + 1))
                            if s == 1 and n == 0:
                                pe.wait_ge(u_ready, c * CHUNKS + CHUNKS)
                            if s == 2 and n == 2:
                                pe.wait_ge(sig_ready, c * CHUNKS + 1)
                            cols = slice(n * CHUNK, (n + 1) * CHUNK)
                            for k in range(KD):
                                last = matmul3(pe, banks[n][:, 0:CHUNK], w_hi[s][:, k, :], w_lo[s][:, k, :],
                                               S.h_hi[:, k, cols], S.h_lo[:, k, cols], k == 0, k == KD - 1)
                            last.then_inc(z_ready[s], 1)
                pe.wait_ge(group_done, KC + 1)
                for c in range(KC):
                    last = pe.transpose(bank[0][0:90, c * P:(c + 1) * P], tail[:, c, :], S.ident[:, :])
                last.then_inc(tail_turned, 1)


def mixer_outputs(nc, S, w_out):
    with ExitStack() as ctx:
        sb = lambda n, s, d=F32: ctx.enter_context(nc.sbuf_tensor(n, s, d))
        sem = lambda n: S.stack.enter_context(nc.semaphore(n))
        sq = sb("conv_sq", [P, KC, COLS])
        var, rstd = sb("conv_var", [P, CHUNKS, CHUNK]), sb("conv_rstd", [P, CHUNKS, CHUNK])
        root, fix = sb("conv_root", [P, CHUNKS, CHUNK]), sb("conv_fix", [P, CHUNKS, CHUNK])
        raw = [sb(f"w_out_raw{i}", [P, 2, D]) for i in range(2)]
        bank = [ctx.enter_context(nc.psum_tensor(f"mix_bank{b}", [P, 512], F32)) for b in range(8)]
        raw_loaded = [sem(f"w_out_loaded{i}") for i in range(2)]
        w_hi_ready, w_lo_ready = sem("w_out_hi_ready"), sem("w_out_lo_ready")
        sum_ready, centred, sq_ready = sem("sum_ready"), sem("centred"), sem("sq_ready")
        varsum_ready, var_ready, rstd_ready, root_ready = sem("varsum_ready"), sem("var_ready"), sem("conv_rstd_step"), sem("root_ready")
        scaled, c_ready, o_ready, o_left = sem("scaled"), sem("c_ready"), sem("o_product"), sem("o_left")
        cols = [slice(n * CHUNK, (n + 1) * CHUNK) for n in range(CHUNKS)]
        outs = [(KC + g, n) for g in range(KC) for n in range(CHUNKS)] + [(c, n) for n in range(CHUNKS) for c in range(KC)]
        o_bank = lambda i: bank[3 + i % 5][:, 0:CHUNK]
        w_view = w_out[0].rearrange("(k p) n -> p k n", p=P)
        with nc.Block() as block:

            @block.sync
            def _(sp):
                for i in range(KD // 2):
                    if i >= 2:
                        sp.wait_ge(w_lo_ready, i - 1)
                    sp.dma_start(raw[i % 2][:, :, :], w_view[:, 2 * i:2 * i + 2, :]).then_inc(raw_loaded[i % 2], 16)

            @block.gpsimd
            def _(pool):
                def take_lo(i):
                    pool.wait_ge(w_hi_ready, i + 1)
                    pool.tensor_tensor(S.wo_lo[:, 2 * i:2 * i + 2, :], raw[i % 2][:, :, :],
                                       S.wo_hi[:, 2 * i:2 * i + 2, :].bitcast(F32), ALU.subtract).then_inc(w_lo_ready, 1)

                pool.memset(S.o[:, :, COLS:ROWS], 0.0)
                for i in range(KD // 2):
                    take_lo(i)

            @block.scalar
            def _(act):
                def take_hi(i):
                    act.wait_ge(raw_loaded[i % 2], 16 * (i // 2) + 16)
                    act.activation(S.wo_hi[:, 2 * i:2 * i + 2, :], raw[i % 2][:, :, :], ACT.Copy).then_inc(w_hi_ready, 1)

                def leave(i):
                    act.wait_ge(o_ready, i + 1)
                    block_of, n = outs[i]
                    if block_of >= KC:
                        g = block_of - KC
                        act.activation(S.o[:, block_of, cols[n]], o_bank(i), ACT.Copy, scale=S.par[:, g, P_SCALE:P_SCALE + 1])\
                           .then_inc(o_left, 1)
                    else:
                        act.activation(S.o[:, block_of, cols[n]], o_bank(i), ACT.Identity,
                                       bias=S.par[:, block_of, P_BPW:P_BPW + 1]).then_inc(o_left, 1)

                take_hi(0)
                take_hi(1)
                for n in range(CHUNKS):
                    act.wait_ge(centred, n + 1)
                    act.activation(sq[:, :, cols[n]], S.conv[:, :, cols[n]], ACT.Square).then_inc(sq_ready, 1)
                for i in range(KC * CHUNKS):
                    leave(i)
                    if i in (2 * CHUNKS + 1, 2 * CHUNKS + 2, 2 * CHUNKS + 3):
                        n = i - 2 * CHUNKS - 1
                        act.wait_ge(var_ready, n + 1)
                        act.activation(root[:, n, :], var[:, n, :], ACT.Sqrt).then_inc(root_ready, 1)
                for n in range(CHUNKS):
                    act.wait_ge(scaled, n + 1)
                    for c in range(KC):
                        act.activation(S.conv[:, c, cols[n]], S.conv[:, c, cols[n]], ACT.Silu,
                                       bias=S.par[:, c, P_BLN:P_BLN + 1], scale=S.par[:, c, P_GLN:P_GLN + 1])\
                           .then_inc(c_ready, 1)
                    if n >= 1:
                        for i in range(KC):
                            leave(KC * CHUNKS + (n - 1) * KC + i)
                for i in range(KC):
                    leave(KC * CHUNKS + (CHUNKS - 1) * KC + i)
                for i in range(2, KD // 2):
                    take_hi(i)

            @block.vector
            def _(dve):
                steps = [0]

                def step(ins):
                    steps[0] += 1
                    ins.then_inc(rstd_ready, 1)
                    dve.wait_ge(rstd_ready, steps[0])

                for n in range(CHUNKS):
                    dve.wait_ge(sum_ready, n + 1)
                    dve.scalar_tensor_tensor(S.conv[:, :, cols[n]],
                                             bank[n][:, 0:CHUNK].unsqueeze(1).to_broadcast([P, KC, CHUNK]), -1.0 / CH,
                                             S.conv[:, :, cols[n]], ALU.mult, ALU.add).then_inc(centred, 1)
                for n in range(CHUNKS):
                    dve.wait_ge(varsum_ready, n + 1)
                    dve.tensor_scalar(var[:, n, :], bank[n][:, 0:CHUNK], 1.0 / CH, EPS, ALU.mult, ALU.add)\
                       .then_inc(var_ready, 1)
                for n in range(CHUNKS):
                    dve.wait_ge(root_ready, n + 1)
                    step(dve.reciprocal(rstd[:, n, :], root[:, n, :]))
                    step(dve.tensor_tensor(fix[:, n, :], rstd[:, n, :], rstd[:, n, :], ALU.mult))
                    step(dve.scalar_tensor_tensor(fix[:, n, :], fix[:, n, :], -0.5, var[:, n, :], ALU.mult, ALU.mult))
                    step(dve.scalar_tensor_tensor(rstd[:, n, :], fix[:, n, :], 1.5, rstd[:, n, :], ALU.add, ALU.mult))
                    dve.tensor_tensor(S.conv[:, :, cols[n]], S.conv[:, :, cols[n]],
                                      rstd[:, n, :].unsqueeze(1).to_broadcast([P, KC, CHUNK]), ALU.mult).then_inc(scaled, 1)

            @block.tensor
            def _(pe):
                for n in range(CHUNKS):
                    for c in range(KC):
                        last = pe.matmul(bank[n][:, 0:CHUNK], S.ones[:, :], S.conv[:, c, cols[n]],
                                         start=(c == 0), stop=(c == KC - 1))
                    last.then_inc(sum_ready, 1)
                pe.wait_ge(S.mix_w_loaded, 32)
                i = 0
                for g in range(KC):
                    for n in range(CHUNKS):
                        if i >= 5:
                            pe.wait_ge(o_left, i - 4)
                        pe.matmul(o_bank(i), S.w_pool[:, g, :], S.pooled[:, g, cols[n]], start=True, stop=True)\
                          .then_inc(o_ready, 1)
                        i += 1
                        if g == 1:
                            pe.wait_ge(sq_ready, n + 1)
                            for c in range(KC):
                                last = pe.matmul(bank[n][:, 0:CHUNK], S.ones[:, :], sq[:, c, cols[n]],
                                                 start=(c == 0), stop=(c == KC - 1))
                            last.then_inc(varsum_ready, 1)
                for n in range(CHUNKS):
                    pe.wait_ge(c_ready, KC * (n + 1))
                    for c in range(KC):
                        pe.wait_ge(o_left, i - 4)
                        for k in range(KC):
                            last = pe.matmul(o_bank(i), S.w_pw[:, k, c * P:(c + 1) * P], S.conv[:, k, cols[n]],
                                             start=(k == 0), stop=(k == KC - 1))
                        last.then_inc(o_ready, 1)
                        i += 1


def out_projection(nc, S, x_prompt, x_sample, g_ffn, w_rg, w_re):
    HALF = KD // 2
    with ExitStack() as ctx:
        sb = lambda n, s, d=F32: ctx.enter_context(nc.sbuf_tensor(n, s, d))
        sem = lambda n: S.stack.enter_context(nc.semaphore(n))
        x, x2, h2, junk, gain = (sb(n, [P, D]) for n in ("x_res", "x2_tile", "h2_tile", "sq_junk4", "g_ffn_rows"))
        o_hi, o_lo = sb("o_hi", [P, KD, P], F32R), sb("o_lo", [P, KD, P], F32R)
        h2_t = sb("h2_t", [P, KD, P])
        w_route = sb("w_route", [P, KD, GROUPS + EXPERTS])
        ss, ms, rstd = sb("ss4", [P, 1]), sb("ms4", [P, 1]), sb("rstd4", [P, 1])
        ps = [ctx.enter_context(nc.psum_tensor(f"ps_out{h}", [P, 512], F32)) for h in range(2)]
        ps_t = ctx.enter_context(nc.psum_tensor("ps_h2t", [P, KD, P], F32))
        x_loaded, gain_loaded, route_loaded = sem("x_loaded4"), sem("gain_loaded4"), sem("route_loaded")
        hi_ready, lo_ready = [sem(f"o_hi_ready{i}") for i in range(2)], [sem(f"o_lo_ready{i}") for i in range(2)]
        used, added = [sem(f"o_used{i}") for i in range(2)], sem("added")
        squared, mean_ready, rstd_ready, h2_ready = sem("squared4"), sem("mean4"), sem("rstd_ready4"), sem("h2_ready")
        turned, h2t_ready = sem("h2_turned"), sem("h2t_ready")
        x2_stored, h2_stored = sem("x2_stored"), sem("h2_stored")
        with nc.Block() as block:

            @block.sync
            def _(sp):
                def store(t):
                    sp.wait_ge(added, t + 2)
                    sp.dma_start(S.x2_rows[bass.ds(t * P, P), :], x2[:, :]).then_inc(x2_stored, 16)

                def store_h(t):
                    sp.wait_ge(h2_ready, t + 1)
                    sp.dma_start(S.h2_rows[bass.ds(t * P, P), :], h2[:, :]).then_inc(h2_stored, 16)

                sp.sem_inc(x2_stored, 16)
                sp.sem_inc(h2_stored, 16)
                sp.dma_start(x[:, :], x_prompt[0, 0:P, :]).then_inc(x_loaded, 16)
                with sp.Fori(0, TILES - 2) as t:
                    store(t)
                    sp.dma_start(x[:, :], x_prompt[0, bass.ds(t * P + P, P), :]).then_inc(x_loaded, 16)
                    store_h(t)
                store(TILES - 2)
                sp.dma_start(x[GAP:GAP + DEC, :], x_sample[0]).then_inc(x_loaded, 16)
                store_h(TILES - 2)
                store(TILES - 1)
                store_h(TILES - 1)
                sp.wait_ge(x2_stored, 16 * (TILES + 1))
                sp.wait_ge(h2_stored, 16 * (TILES + 1))

            @block.gpsimd
            def _(pool):
                with pool.Fori(0, TILES) as t:
                    pool.wait_ge(mean_ready, t + 1)
                    pool.tensor_tensor(rstd[:, :], ms[:, :], S.minus_half[:, 0:1], ALU.pow).then_inc(rstd_ready, 1)

            @block.scalar
            def _(act):
                act.dma_start(gain[:, :], g_ffn[0].partition_broadcast(P)).then_inc(gain_loaded, 16)
                act.dma_start(w_route[:, :, 0:GROUPS], w_rg[0].rearrange("(k p) n -> p k n", p=P)).then_inc(route_loaded, 16)
                act.dma_start(w_route[:, :, GROUPS:], w_re[0].rearrange("(k p) n -> p k n", p=P)).then_inc(route_loaded, 16)

                def take_hi(t, i):
                    ks = slice(i * HALF, (i + 1) * HALF)
                    act.activation(o_hi[:, ks, :], S.o[:, ks, bass.ds(t * P, P)], ACT.Copy).then_inc(hi_ready[i], 1)

                def next_hi(t):
                    for i in range(2):
                        act.wait_ge(used[i], t)
                        take_hi(t, i)

                def square(t):
                    if type(t) is not int or t > 0:
                        act.wait_ge(squared, t)
                    act.wait_ge(added, t + 2)
                    act.activation(junk[:, :], x2[:, :], ACT.Square, accum_out=ss[:, :]).then_inc(squared, 1)

                def leave(t):
                    act.wait_ge(turned, t + 2)
                    act.activation(h2_t[:, :, :], ps_t[:, :, :], ACT.Copy).then_inc(h2t_ready, 1)

                take_hi(0, 0)
                take_hi(0, 1)
                next_hi(1)
                square(0)
                with act.Fori(1, TILES - 1) as t:
                    next_hi(t + 1)
                    square(t)
                    leave(t - 1)
                square(TILES - 1)
                leave(TILES - 2)
                leave(TILES - 1)

            @block.vector
            def _(dve):
                def take_lo(t, i):
                    ks = slice(i * HALF, (i + 1) * HALF)
                    dve.wait_ge(hi_ready[i], t + 1)
                    dve.tensor_tensor(o_lo[:, ks, :], S.o[:, ks, bass.ds(t * P, P)], o_hi[:, ks, :].bitcast(F32),
                                      ALU.subtract).then_inc(lo_ready[i], 1)

                def add(t):
                    dve.wait_ge(x_loaded, t * 16 + 16)
                    dve.wait_ge(x2_stored, t * 16 + 16)
                    dve.wait_ge(used[1], t + 1)
                    dve.tensor_tensor(x2[:, 0:512], ps[0][:, :], x[:, 0:512], ALU.add)
                    dve.tensor_tensor(x2[:, 512:D], ps[1][:, :], x[:, 512:D], ALU.add).then_inc(added, 1)

                def norm(t):
                    dve.wait_ge(squared, t + 1)
                    dve.tensor_scalar(ms[:, :], ss[:, :], 1.0 / D, EPS, ALU.mult, ALU.add).then_inc(mean_ready, 1)
                    dve.wait_ge(rstd_ready, t + 1)
                    dve.wait_ge(h2_stored, t * 16 + 16)
                    dve.wait_ge(turned, t + 1)
                    dve.scalar_tensor_tensor(h2[:, :], x2[:, :], rstd[:, :], gain[:, :], ALU.mult, ALU.mult)\
                       .then_inc(h2_ready, 1)
                    dve.wait_ge(h2_ready, t + 1)

                dve.sem_inc(added, 1)
                dve.wait_ge(gain_loaded, 16)
                take_lo(0, 0)
                take_lo(0, 1)
                with dve.Fori(0, TILES - 1) as t:
                    take_lo(t + 1, 0)
                    add(t)
                    take_lo(t + 1, 1)
                    norm(t)
                add(TILES - 1)
                norm(TILES - 1)

            @block.tensor
            def _(pe):
                def products(t):
                    pe.wait_ge(added, t + 1)
                    for i in range(2):
                        pe.wait_ge(lo_ready[i], t + 1)
                        for k in range(i * HALF, (i + 1) * HALF):
                            for h in range(2):
                                half = slice(h * 512, (h + 1) * 512)
                                last = matmul3(pe, ps[h][:, :], o_hi[:, k, :], o_lo[:, k, :], S.wo_hi[:, k, half],
                                               S.wo_lo[:, k, half], k == 0, k == KD - 1)
                        last.then_inc(used[i], 1)

                def turn(t):
                    pe.wait_ge(h2_ready, t + 1)
                    for k in range(KD):
                        last = pe.transpose(ps_t[:, k, :], h2[:, k * P:(k + 1) * P], S.ident[:, :])
                    last.then_inc(turned, 1)

                def route(t):
                    pe.wait_ge(h2t_ready, t + 1)
                    for k in range(KD):
                        last = pe.matmul(S.ps_route[:, bass.ds(t, 1), :], h2_t[:, k, :], w_route[:, k, :],
                                         start=(k == 0), stop=(k == KD - 1))
                    last.then_inc(S.routed, 1)

                pe.sem_inc(turned, 1)
                products(0)
                products(1)
                turn(0)
                pe.wait_ge(route_loaded, 32)
                with pe.Fori(2, TILES) as t:
                    products(t)
                    route(t - 2)
                    turn(t - 1)
                route(TILES - 2)
                turn(TILES - 1)
                route(TILES - 1)


def routing(nc, S, b_rg, b_re):
    T, E, G, C8 = TILES, EXPERTS, GROUPS, PER_GROUP
    with ExitStack() as ctx:
        sb = lambda n, s, d=F32: ctx.enter_context(nc.sbuf_tensor(n, s, d))
        sem = lambda n: S.stack.enter_context(nc.semaphore(n))
        bias = sb("route_bias", [P, G + E])
        lg = sb("logits", [P, T, G + E])
        idx = sb("iota_experts", [P, E])
        valid = sb("valid_rows", [P, T])
        dump, first_row = sb("dump_rows", [P, 2, T]), sb("first_rows", [P, 2, T])
        tok = sb("token_rows", [P, T], I32)
        tri = sb("earlier", [P, P], BF16)
        ones_b = sb("ones_b", [P, P], BF16)
        zero = sb("zero_table", [P, TABLE // P], I32)
        a9, b9, gsel, gw = (sb(n, [P, T]) for n in ("a9", "b9", "gsel", "gw"))
        g4, g4b = sb("g4", [P, T, G]), sb("g4b", [P, T, G])
        e32, esel, e8, e8b = sb("e32", [P, T, G, C8]), sb("esel", [P, T, C8]), sb("e8", [P, T, C8]), sb("e8b", [P, T, C8])
        m1, m2 = sb("m1", [P, T]), sb("m2", [P, T])
        eid = sb("eid", [P, 2, T])
        oh = [sb(f"onehot{k}", [P, T, E]) for k in range(2)]
        ohs = sb("onehot_sum", [P, T, E], BF16)
        tot, base, rank = sb("tile_totals", [P, T, E]), sb("tile_base", [P, T + 1, E]), sb("rank", [P, T, E])
        t32 = sb("t32", [P, T, E])
        over, cum, cum2 = sb("over", [P, E]), sb("cum", [P, E]), sb("cum2", [P, E])
        rk, osk, blk, item, s18 = (sb(n, [P, 2, T]) for n in ("rk", "osk", "blk", "item", "s18"))
        scatter_i = sb("scatter_rows", [P, 2, T], I32)
        x16, y16, c16 = sb("x16", [P, MAX_EXTRA, E]), sb("y16", [P, MAX_EXTRA, E]), sb("c16", [P, MAX_EXTRA, 1])
        j16, r16, q16, n1 = sb("j16", [P, MAX_EXTRA]), sb("r16", [P, MAX_EXTRA]), sb("q16", [P, MAX_EXTRA]), sb("n1", [P, 1])
        r32 = sb("r32", [P, E])
        ps_rank = ctx.enter_context(nc.psum_tensor("ps_rank", [P, T, E], F32))
        ps_tot = ctx.enter_context(nc.psum_tensor("ps_tot", [P, T, E], F32))
        bias_loaded, made, cleared, exp_ready = sem("bias_loaded"), sem("tables_made"), sem("table_cleared"), sem("exp_ready")
        chain, to_exp, to_rank, ranked = sem("route_chain"), sem("to_exp"), sem("to_rank"), sem("ranked")
        rows_ready, scattered = sem("rows_ready"), sem("scattered")
        bc = lambda ap, shape: ap.to_broadcast(shape)
        with nc.Block() as block:

            @block.sync
            def _(sp):
                sp.dma_start(bias[:, 0:G], b_rg[0].partition_broadcast(P)).then_inc(bias_loaded, 16)
                sp.dma_start(bias[:, G:], b_re[0].partition_broadcast(P)).then_inc(bias_loaded, 16)
                sp.wait_ge(made, 1)
                sp.dma_start(S.table.rearrange("(p n) o -> p (n o)", p=P), zero[:, :]).then_inc(cleared, 16)

            @block.gpsimd
            def _(pool):
                pool.memset(zero[:, :], 0).then_inc(made, 1)
                pool.iota(idx[:, :], pattern=[[1, E]], base=0, channel_multiplier=0, allow_small_or_imprecise_dtypes=True)
                pool.iota(j16[:, :], pattern=[[1, MAX_EXTRA]], base=0, channel_multiplier=0,
                          allow_small_or_imprecise_dtypes=True)
                pool.iota(tok[:, :], pattern=[[P, T]], base=0, channel_multiplier=1)
                pool.iota(r32[:, :], pattern=[[RANKS, E]], base=0, channel_multiplier=0, allow_small_or_imprecise_dtypes=True)
                pool.memset(valid[:, :], 1.0)
                pool.memset(tri[:, :], 1.0)
                pool.memset(dump[:, :, 0:T - 1], 0.0)
                pool.iota(dump[:, :, T - 1], pattern=[[P, 2]], base=E * RANKS, channel_multiplier=1,
                          allow_small_or_imprecise_dtypes=True)
                pool.memset(first_row[:, :, 0:T - 1], 0.0)
                pool.iota(first_row[:, :, T - 1], pattern=[[0, 2]], base=0, channel_multiplier=1,
                          allow_small_or_imprecise_dtypes=True)
                pool.memset(ones_b[:, :], 1.0).then_inc(made, 1)
                pool.wait_ge(made, 2)
                pool.affine_select(out=valid[:, T - 1:T], in_=valid[:, T - 1:T], compare_op=ALU.is_ge, fill=0.0,
                                   base=-GAP, pattern=[[0, 1]], channel_multiplier=1).then_inc(made, 1)
                pool.wait_ge(made, 3)
                pool.affine_select(out=valid[:, T - 1:T], in_=valid[:, T - 1:T], compare_op=ALU.is_ge, fill=0.0,
                                   base=GAP + DEC - 1, pattern=[[0, 1]], channel_multiplier=-1)
                pool.affine_select(out=tri[:, :], in_=tri[:, :], compare_op=ALU.is_gt, fill=0.0,
                                   base=0, pattern=[[1, P]], channel_multiplier=-1).then_inc(made, 1)
                pool.wait_ge(cleared, 16)
                pool.wait_ge(rows_ready, 1)
                for k in range(2):
                    for t in range(T):
                        pool.indirect_dma_start(out=S.table[:, :],
                                                out_offset=bass.IndirectOffsetOnAxis(ap=scatter_i[:, k, t:t + 1], axis=0),
                                                in_=tok[:, t:t + 1], in_offset=None).then_inc(scattered, 16)
                pool.wait_ge(scattered, 2 * T * 16)

            @block.scalar
            def _(act):
                act.wait_ge(to_exp, 1)
                act.activation(g4[:, :, :], g4[:, :, :], ACT.Exp).then_inc(exp_ready, 1)
                act.wait_ge(to_exp, 2)
                act.activation(m2[:, :], m2[:, :], ACT.Exp).then_inc(exp_ready, 1)

            @block.tensor
            def _(pe):
                pe.wait_ge(made, 4)
                pe.wait_ge(to_rank, 1)
                pe.matmul(ps_tot[:, :, :], ones_b[:, :], ohs[:, :, :], start=True, stop=True)
                pe.matmul(ps_rank[:, :, :], tri[:, :], ohs[:, :, :], start=True, stop=True).then_inc(ranked, 1)

            @block.vector
            def _(dve):
                links = [0]

                def step(ins):
                    links[0] += 1
                    ins.then_inc(chain, 1)
                    dve.wait_ge(chain, links[0])

                tt = lambda o, a, b, op: step(dve.tensor_tensor(o, a, b, op))
                ts = lambda o, a, s1, s2, o1, o2=None: step(
                    dve.tensor_scalar(o, a, s1, s2, o1) if o2 is None else dve.tensor_scalar(o, a, s1, s2, o1, o2))
                red = lambda o, a, op: step(dve.tensor_reduce(o, a, AX.X, op))

                def argfirst(out, values, best, n, work):
                    tt(work, values, bc(best.unsqueeze(2), [P, T, n]), ALU.is_equal)
                    step(dve.scalar_tensor_tensor(work, bc(idx[:, 0:n].unsqueeze(1), [P, T, n]), -float(E), work,
                                                  ALU.add, ALU.mult))
                    red(out, work, ALU.min)
                    ts(out, out, float(E), None, ALU.add)

                dve.wait_ge(made, 4)
                dve.wait_ge(bias_loaded, 32)
                dve.wait_ge(S.routed, T)
                tt(lg[:, :, :], S.ps_route[:, :, :], bc(bias[:, :].unsqueeze(1), [P, T, G + E]), ALU.add)
                red(a9[:, :], lg[:, :, 0:G], ALU.max)
                argfirst(gsel[:, :], lg[:, :, 0:G], a9[:, :], G, g4[:, :, :])
                tt(g4[:, :, :], lg[:, :, 0:G], bc(a9[:, :].unsqueeze(2), [P, T, G]), ALU.subtract)
                dve.sem_inc(to_exp, 1)
                tt(g4b[:, :, :], bc(idx[:, 0:G].unsqueeze(1), [P, T, G]), bc(gsel[:, :].unsqueeze(2), [P, T, G]), ALU.is_equal)
                tt(e32[:, :, :, :], lg[:, :, G:].rearrange("p t (g e) -> p t g e", g=G),
                   bc(g4b[:, :, :].unsqueeze(3), [P, T, G, C8]), ALU.mult)
                tt(esel[:, :, :], e32[:, :, 0, :], e32[:, :, 1, :], ALU.add)
                tt(esel[:, :, :], esel[:, :, :], e32[:, :, 2, :], ALU.add)
                tt(esel[:, :, :], esel[:, :, :], e32[:, :, 3, :], ALU.add)
                red(m1[:, :], esel[:, :, :], ALU.max)
                argfirst(eid[:, 0, :], esel[:, :, :], m1[:, :], C8, e8[:, :, :])
                tt(e8[:, :, :], bc(idx[:, 0:C8].unsqueeze(1), [P, T, C8]), bc(eid[:, 0, :].unsqueeze(2), [P, T, C8]),
                   ALU.is_equal)
                step(dve.scalar_tensor_tensor(e8b[:, :, :], e8[:, :, :], -1e30, esel[:, :, :], ALU.mult, ALU.add))
                red(m2[:, :], e8b[:, :, :], ALU.max)
                argfirst(eid[:, 1, :], e8b[:, :, :], m2[:, :], C8, e8[:, :, :])
                tt(m2[:, :], m2[:, :], m1[:, :], ALU.subtract)
                dve.sem_inc(to_exp, 1)
                for k in range(2):
                    step(dve.scalar_tensor_tensor(eid[:, k, :], gsel[:, :], float(C8), eid[:, k, :], ALU.mult, ALU.add))
                    step(dve.scalar_tensor_tensor(eid[:, k, :], eid[:, k, :], 1.0, valid[:, :], ALU.add, ALU.mult))
                    ts(eid[:, k, :], eid[:, k, :], -1.0, None, ALU.add)
                    tt(oh[k][:, :, :], bc(idx[:, :].unsqueeze(1), [P, T, E]), bc(eid[:, k, :].unsqueeze(2), [P, T, E]),
                       ALU.is_equal)
                tt(ohs[:, :, :], oh[0][:, :, :], oh[1][:, :, :], ALU.add)
                dve.sem_inc(to_rank, 1)
                dve.wait_ge(exp_ready, 2)
                red(gw[:, :], g4[:, :, :], ALU.add)
                step(dve.reciprocal(gw[:, :], gw[:, :]))
                ts(a9[:, :], m2[:, :], 1.0, None, ALU.add)
                step(dve.reciprocal(a9[:, :], a9[:, :]))
                tt(S.gate[:, 0, :], a9[:, :], gw[:, :], ALU.mult)
                tt(S.gate[:, 1, :], S.gate[:, 0, :], m2[:, :], ALU.mult)
                dve.wait_ge(ranked, 1)
                step(dve.tensor_copy(tot[:, :, :], ps_tot[:, :, :]))
                step(dve.memset(base[:, 0, :], 0.0))
                for t in range(T):
                    tt(base[:, t + 1, :], base[:, t, :], tot[:, t, :], ALU.add)
                tt(rank[:, :, :], ps_rank[:, :, :], base[:, 0:T, :], ALU.add)
                for k in range(2):
                    tt(t32[:, :, :], oh[k][:, :, :], rank[:, :, :], ALU.mult)
                    red(rk[:, k, :], t32[:, :, :], ALU.add)
                step(dve.scalar_tensor_tensor(s18[:, :, :], eid[:, :, :], float(RANKS), rk[:, :, :], ALU.mult, ALU.add))
                v2 = bc(valid[:, :].unsqueeze(1), [P, 2, T])
                tt(s18[:, :, :], s18[:, :, :], v2, ALU.mult)
                tt(s18[:, :, :], s18[:, :, :], dump[:, :, :], ALU.add)
                tt(item[:, :, :], dump[:, :, :], v2, ALU.mult)
                tt(s18[:, :, :], s18[:, :, :], item[:, :, :], ALU.subtract)
                step(dve.tensor_copy(scatter_i[:, :, :], s18[:, :, :]))
                dve.sem_inc(rows_ready, 1)
                total = base[:, T, :]
                ts(over[:, :], total, float(P), None, ALU.is_gt)
                for m in range(2, MAX_BLOCKS):
                    step(dve.scalar_tensor_tensor(over[:, :], total, float(m * P), over[:, :], ALU.is_gt, ALU.add))
                src, dst, d = over, cum, 1
                while d < E:
                    tt(dst[:, d:], src[:, d:], src[:, 0:E - d], ALU.add)
                    step(dve.tensor_copy(dst[:, 0:d], src[:, 0:d]))
                    src, dst, d = dst, (cum2 if dst is cum else cum), 2 * d
                incl = src
                ts(n1[:, :], incl[:, E - 1:E], 1.0, float(E), ALU.max, ALU.add)
                step(dve.tensor_copy(S.n_items[:, 0:1], n1[:, :]))
                ts(n1[:, :], n1[:, :], -1.0, None, ALU.add)
                step(dve.tensor_copy(S.n_items[:, 1:2], n1[:, :]))
                shape = [P, MAX_EXTRA, E]
                tt(x16[:, :, :], bc(incl[:, :].unsqueeze(1), shape), bc(j16[:, :].unsqueeze(2), shape), ALU.is_le)
                red(r16[:, :], x16[:, :, :], ALU.add)
                ts(r16[:, :], r16[:, :], float(E - 1), None, ALU.min)
                step(dve.tensor_copy(S.item_expert[:, E:], r16[:, :]))
                step(dve.tensor_copy(S.item_expert[:, 0:E], idx[:, :]))
                tt(y16[:, :, :], x16[:, :, :], bc(incl[:, :].unsqueeze(1), shape), ALU.mult)
                red(q16[:, :], y16[:, :, :], ALU.max)
                tt(q16[:, :], j16[:, :], q16[:, :], ALU.subtract)
                ts(q16[:, :], q16[:, :], 1.0, float(P), ALU.add, ALU.mult)
                step(dve.scalar_tensor_tensor(q16[:, :], r16[:, :], float(RANKS), q16[:, :], ALU.mult, ALU.add))
                ts(q16[:, :], q16[:, :], float(E * RANKS - P), None, ALU.min)
                step(dve.tensor_copy(S.item_row[:, E:], q16[:, :]))
                step(dve.tensor_copy(S.item_row[:, 0:E], r32[:, :]))
                tt(over[:, :], incl[:, :], over[:, :], ALU.subtract)
                for k in range(2):
                    tt(t32[:, :, :], oh[k][:, :, :], bc(over[:, :].unsqueeze(1), [P, T, E]), ALU.mult)
                    red(osk[:, k, :], t32[:, :, :], ALU.add)
                ts(blk[:, :, :], rk[:, :, :], float(P), None, ALU.is_ge)
                for m in range(2, MAX_BLOCKS):
                    step(dve.scalar_tensor_tensor(blk[:, :, :], rk[:, :, :], float(m * P), blk[:, :, :], ALU.is_ge, ALU.add))
                tt(osk[:, :, :], osk[:, :, :], blk[:, :, :], ALU.add)
                tt(osk[:, :, :], osk[:, :, :], eid[:, :, :], ALU.subtract)
                ts(osk[:, :, :], osk[:, :, :], float(E - 1), None, ALU.add)
                ts(item[:, :, :], blk[:, :, :], 0.0, None, ALU.is_gt)
                tt(item[:, :, :], item[:, :, :], osk[:, :, :], ALU.mult)
                tt(item[:, :, :], item[:, :, :], eid[:, :, :], ALU.add)
                tt(item[:, :, :], item[:, :, :], blk[:, :, :], ALU.subtract)
                step(dve.scalar_tensor_tensor(s18[:, :, :], item[:, :, :], float(P), rk[:, :, :], ALU.mult, ALU.add))
                tt(s18[:, :, :], s18[:, :, :], v2, ALU.mult)
                tt(item[:, :, :], first_row[:, :, :], v2, ALU.mult)
                tt(item[:, :, :], first_row[:, :, :], item[:, :, :], ALU.subtract)
                tt(s18[:, :, :], s18[:, :, :], item[:, :, :], ALU.add)
                step(dve.tensor_copy(S.out_row[:, :, :], s18[:, :, :]))


def experts(nc, S, w_gate, w_up, w_down):
    GATE, UP, DOWN = (0, 1), (2, 3), (4, 5)
    with ExitStack() as ctx:
        sb = lambda n, s, d=F32: ctx.enter_context(nc.sbuf_tensor(n, s, d))
        sem = lambda n: S.stack.enter_context(nc.semaphore(n))
        raw = [sb(f"w_raw{s}", [P, PIECE]) for s in range(6)]
        w_hi = [sb(f"w_hi{s}", [P, PIECE], F32R) for s in range(6)]
        w_lo = [sb(f"w_lo{s}", [P, PIECE], F32R) for s in range(6)]
        ids = sb("token_ids", [P, 1], I32)
        x = sb("x_tokens", [P, D])
        x_hi, x_lo = sb("xt_hi", [P, KD, P], F32R), sb("xt_lo", [P, KD, P], F32R)
        act_g, hid = sb("act_gate", [P, D_EXP]), sb("hidden", [P, D_EXP])
        h_hi, h_lo = sb("ht_hi", [P, KE, P], F32R), sb("ht_lo", [P, KE, P], F32R)
        y = sb("y_tile", [P, D])
        psum = lambda n, s: ctx.enter_context(nc.psum_tensor(n, s, F32))
        ps_x, ps_g, ps_u, ps_h, ps_y = (psum("ps_x", [P, KD, P]), psum("ps_g", [P, D_EXP]), psum("ps_u", [P, D_EXP]),
                                        psum("ps_h", [P, KE, P]), psum("ps_y", [P, D]))
        raw_loaded, w_hi_ready, w_split, w_used = ([sem(f"{n}{s}") for s in range(6)] for n in
                                                   ("raw_loaded", "w_hi_ready", "w_split", "w_used"))
        ids_loaded, x_gathered, x_turned, xh_ready, xl_ready = (sem(n) for n in (
            "ids_loaded", "x_gathered", "x_turned", "xh_ready", "xl_ready"))
        silu_ready, hid_ready, hid_turned, hh_ready, hl_ready = (sem(n) for n in (
            "silu_ready", "hid_ready", "hid_turned", "hh_ready", "hl_ready"))
        y_left, y_stored = sem("y_left"), sem("y_stored")
        number = lambda eng: eng.value_load(S.n_items[0:1, 0:1], min_val=EXPERTS + 1, max_val=ITEMS)
        final_of = lambda eng: eng.value_load(S.n_items[0:1, 1:2], min_val=EXPERTS, max_val=ITEMS - 1)
        kgu = PIECE // D_EXP
        kdn = PIECE // D
        with nc.Block() as block:

            @block.sync
            def _(sp):
                end = final_of(sp)
                for s in range(6):
                    sp.sem_inc(w_split[s], 1)

                def load(i, slots):
                    e = sp.value_load(S.item_expert[0:1, bass.ds(i, 1)], min_val=0, max_val=EXPERTS - 1)
                    for s in slots:
                        w, cols = ((w_gate, D_EXP), (w_up, D_EXP), (w_down, D))[s // 2]
                        half = w.shape[2] // 2
                        src = w[0, bass.ds(e, 1), (s % 2) * half:(s % 2 + 1) * half, :].rearrange(
                            "o (k p) n -> p (o k) n", p=P)
                        sp.wait_ge(w_split[s], i + 1)
                        sp.dma_start(raw[s][:, :].rearrange("p (k n) -> p k n", n=cols), src).then_inc(raw_loaded[s], 16)

                load(0, GATE + UP)
                with sp.Fori(0, end) as i:
                    load(i + 1, GATE + UP)
                    load(i, DOWN)
                load(end, DOWN)

            @block.gpsimd
            def _(pool):
                n_items = number(pool)

                def fetch(i, row):
                    pool.dma_start(ids[:, :], S.table[bass.ds(row, P), :]).then_inc(ids_loaded, 16)
                    pool.wait_ge(ids_loaded, i * 16 + 16)

                def gather():
                    pool.indirect_dma_start(out=x[:, :], out_offset=None, in_=S.h2_rows[:, :],
                                            in_offset=bass.IndirectOffsetOnAxis(ap=ids[:, :], axis=0)).then_inc(x_gathered, 16)

                def take_lo(i):
                    pool.wait_ge(w_hi_ready[3], i + 1)
                    pool.tensor_tensor(w_lo[3][:, :], raw[3][:, :], w_hi[3][:, :].bitcast(F32), ALU.subtract)\
                        .then_inc(w_split[3], 1)

                fetch(0, 0)
                gather()
                take_lo(0)
                with pool.Fori(1, n_items) as i:
                    row = pool.value_load(S.item_row[0:1, bass.ds(i, 1)], min_val=0, max_val=EXPERTS * RANKS - P)
                    pool.wait_ge(x_gathered, i * 16)
                    fetch(i, row)
                    pool.wait_ge(x_turned, i)
                    pool.sem_inc(S.waits_met, 1)
                    gather()
                    take_lo(i)

            @block.scalar
            def _(act):
                end = final_of(act)

                def take_hi(i, s, used=True):
                    act.wait_ge(raw_loaded[s], i * 16 + 16)
                    if used:
                        act.wait_ge(w_used[s], i)
                    act.activation(w_hi[s][:, :], raw[s][:, :], ACT.Copy).then_inc(w_hi_ready[s], 1)

                def x_to_hi(i):
                    act.wait_ge(x_turned, i + 1)
                    act.activation(x_hi[:, :, :], ps_x[:, :, :], ACT.Copy).then_inc(xh_ready, 1)

                def leave_y(i):
                    act.wait_ge(w_used[5], i + 1)
                    act.wait_ge(y_stored, i * 16 + 16)
                    act.activation(y[:, :], ps_y[:, :], ACT.Copy).then_inc(y_left, 1)
                    act.wait_ge(y_left, i + 2)
                    act.dma_start(S.y_rows[bass.ds(i * P, P), :], y[:, :]).then_inc(y_stored, 16)

                def iteration(i, first=False, final=False):
                    if not final:
                        take_hi(i + 1, 0)
                        take_hi(i + 1, 1)
                        take_hi(i + 1, 2)
                    act.wait_ge(w_used[1], i + 1)
                    act.activation(act_g[:, :], ps_g[:, :], ACT.Silu).then_inc(silu_ready, 1)
                    if not final:
                        take_hi(i + 1, 3)
                        x_to_hi(i + 1)
                    take_hi(i, 4, used=not first)
                    take_hi(i, 5, used=not first)
                    if not first:
                        leave_y(i - 1)
                    act.wait_ge(hid_turned, i + 1)
                    act.activation(h_hi[:, :, :], ps_h[:, :, :], ACT.Copy).then_inc(hh_ready, 1)

                act.sem_inc(y_left, 1)
                act.sem_inc(y_stored, 16)
                take_hi(0, 0, used=False)
                x_to_hi(0)
                for s in (1, 2, 3):
                    take_hi(0, s, used=False)
                iteration(0, first=True)
                with act.Fori(1, end) as i:
                    iteration(i)
                iteration(end, final=True)
                leave_y(end)
                act.wait_ge(y_stored, end * 16 + 32)
                act.sem_inc(S.waits_met, 1)

            @block.vector
            def _(dve):
                end = final_of(dve)

                def take_lo(i, s):
                    dve.wait_ge(w_hi_ready[s], i + 1)
                    dve.tensor_tensor(w_lo[s][:, :], raw[s][:, :], w_hi[s][:, :].bitcast(F32), ALU.subtract)\
                       .then_inc(w_split[s], 1)

                def x_to_lo(i):
                    dve.wait_ge(xh_ready, i + 1)
                    dve.tensor_tensor(x_lo[:, :, :], ps_x[:, :, :], x_hi[:, :, :].bitcast(F32), ALU.subtract)\
                       .then_inc(xl_ready, 1)

                def iteration(i, final=False):
                    if not final:
                        for s in (0, 1, 2):
                            take_lo(i + 1, s)
                    dve.wait_ge(silu_ready, i + 1)
                    dve.wait_ge(w_used[3], i + 1)
                    dve.tensor_tensor(hid[:, :], ps_u[:, :], act_g[:, :], ALU.mult).then_inc(hid_ready, 1)
                    if not final:
                        x_to_lo(i + 1)
                    take_lo(i, 4)
                    take_lo(i, 5)
                    dve.wait_ge(hh_ready, i + 1)
                    dve.tensor_tensor(h_lo[:, :, :], ps_h[:, :, :], h_hi[:, :, :].bitcast(F32), ALU.subtract)\
                       .then_inc(hl_ready, 1)

                take_lo(0, 0)
                x_to_lo(0)
                for s in (1, 2):
                    take_lo(0, s)
                iteration(0)
                with dve.Fori(1, end) as i:
                    iteration(i)
                iteration(end, final=True)

            @block.tensor
            def _(pe):
                end = final_of(pe)

                def turn_x(i):
                    pe.wait_ge(x_gathered, i * 16 + 16)
                    for k in range(KD):
                        last = pe.transpose(ps_x[:, k, :], x[:, k * P:(k + 1) * P], S.ident[:, :])
                    last.then_inc(x_turned, 1)

                def gate_up(i):
                    pe.wait_ge(xl_ready, i + 1)
                    for slots, ps in ((GATE, ps_g), (UP, ps_u)):
                        for s in slots:
                            pe.wait_ge(w_split[s], i + 2)
                            for j in range(kgu):
                                k = (s % 2) * kgu + j
                                cols = slice(j * D_EXP, (j + 1) * D_EXP)
                                last = matmul3(pe, ps[:, :], x_hi[:, k, :], x_lo[:, k, :], w_hi[s][:, cols],
                                               w_lo[s][:, cols], k == 0, k == KD - 1)
                            last.then_inc(w_used[s], 1)

                def down(i):
                    pe.wait_ge(hl_ready, i + 1)
                    pe.wait_ge(y_left, i + 1)
                    for s in DOWN:
                        pe.wait_ge(w_split[s], i + 2)
                        for j in range(kdn):
                            k = (s % 2) * kdn + j
                            for h in range(2):
                                cols = slice(j * D + h * 512, j * D + (h + 1) * 512)
                                last = matmul3(pe, ps_y[:, h * 512:(h + 1) * 512], h_hi[:, k, :], h_lo[:, k, :],
                                               w_hi[s][:, cols], w_lo[s][:, cols], k == 0, k == KE - 1)
                        last.then_inc(w_used[s], 1)

                def turn_hid(i):
                    pe.wait_ge(hid_ready, i + 1)
                    for k in range(KE):
                        last = pe.transpose(ps_h[:, k, :], hid[:, k * P:(k + 1) * P], S.ident[:, :])
                    last.then_inc(hid_turned, 1)

                turn_x(0)
                gate_up(0)
                turn_x(1)
                turn_hid(0)
                with pe.Fori(1, end) as i:
                    gate_up(i)
                    turn_x(i + 1)
                    down(i - 1)
                    turn_hid(i)
                gate_up(end)
                down(end - 1)
                turn_hid(end)
                down(end)


def embedding_gate(nc, S, p_prompt, p_sample, g_ple, w_ple_gate, b_ple_gate, w_ple_proj, g_final, y_prompt, y_sample):
    KP = PLE // P
    HALF = KD // 2
    with ExitStack() as ctx:
        sb = lambda n, s, d=F32: ctx.enter_context(nc.sbuf_tensor(n, s, d))
        sem = lambda n: S.stack.enter_context(nc.semaphore(n))
        NW = KD // 2 + 1
        raw = [sb(f"ple_raw{i}", [P, 2, D]) for i in range(NW)]
        w_hi, w_lo = sb("ple_hi", [P, 2 * NW, D], F32R), sb("ple_lo", [P, 2 * NW, D], F32R)
        x2, y1, y2, x3, x3b, h3, sgm, x4, out = (sb(n, [P, D]) for n in (
            "x2_in", "y1_in", "y2_in", "x3_tile", "x3_kept", "h3_tile", "sigmoid_ple", "x4_tile", "out_tile"))
        junk1, junk2, g_rows, f_rows, b_rows = (sb(n, [P, D]) for n in ("junk61", "junk62", "g_ple_rows", "g_final_rows", "b_ple_rows"))
        p_in = sb("p_in", [P, PLE])
        h_hi, h_lo = sb("h3t_hi", [P, KD, P], F32R), sb("h3t_lo", [P, KD, P], F32R)
        p_hi, p_lo = sb("pt_hi", [P, KP, P], F32R), sb("pt_lo", [P, KP, P], F32R)
        rows = sb("gather_rows", [P, 2], I32)
        gate = sb("gate_cols", [P, 2])
        ss, ms, rstd = sb("ss6", [P, 2]), sb("ms6", [P, 2]), sb("rstd6", [P, 2])
        psum = lambda n, s: ctx.enter_context(nc.psum_tensor(n, s, F32))
        ps_g, ps_p, ps_h, ps_pt = psum("ps_gate", [P, D]), psum("ps_proj", [P, D]), psum("ps_h3t", [P, KD, P]), psum("ps_pt", [P, KP, P])
        raw_loaded = sem("ple_loaded")
        rows_loaded, w_hi_ready, w_lo_ready = sem("rows_loaded"), sem("ple_hi_ready"), sem("ple_lo_ready")
        x2_loaded, p_loaded, y1_in, y2_in, picked = (sem(n) for n in ("x2_in_loaded", "p_loaded", "y1_gathered", "y2_gathered", "picked"))
        x3_part, x3_ready, x3_kept, h3_ready, turned, p_turned = (sem(n) for n in (
            "x3_part", "x3_ready", "x3_kept_ready", "h3_ready", "h3_turned", "p_turned"))
        hi_ready, lo_ready, p_hi_ready, p_lo_ready = (sem(n) for n in ("h3_hi", "h3_lo", "p_hi_ready", "p_lo_ready"))
        squared, mean_ready, rstd_ready = ([sem(f"{n}{i}") for i in range(2)] for n in ("sq6_", "ms6_", "rstd6_"))
        gates, biased, sig_ready, projected, scaled = (sem(n) for n in ("gates_ready", "biased", "sig6_ready", "projected", "scaled6"))
        x4_ready, out_ready, out_stored = sem("x4_ready"), sem("out_ready"), sem("out_stored")
        gate_view = w_ple_gate[0].rearrange("(k p) n -> p k n", p=P)
        proj_view = w_ple_proj[0].rearrange("(k p) n -> p k n", p=P)
        with nc.Block() as block:

            @block.sync
            def _(sp):
                for i in range(NW):
                    src = gate_view[:, 2 * i:2 * i + 2, :] if i < NW - 1 else proj_view
                    sp.dma_start(raw[i][:, :, :], src).then_inc(raw_loaded, 16)

                def loads(t, p_src, rows_of):
                    sp.wait_ge(x3_part, t)
                    sp.dma_start(x2[:, :], S.x2_rows[bass.ds(t * P, P), :]).then_inc(x2_loaded, 16)
                    sp.wait_ge(p_turned, t)
                    sp.dma_start(p_in[rows_of, :], p_src).then_inc(p_loaded, 16)

                def store(t, dst, rows_of):
                    sp.wait_ge(out_ready, t + 1)
                    sp.dma_start(dst, out[rows_of, :]).then_inc(out_stored, 16)

                whole, sample = slice(0, P), slice(GAP, GAP + DEC)
                sp.sem_inc(out_stored, 16)
                sp.dma_start(x2[:, :], S.x2_rows[0:P, :]).then_inc(x2_loaded, 16)
                sp.dma_start(p_in[:, :], p_prompt[0, 0, 0:P, :]).then_inc(p_loaded, 16)
                loads(1, p_prompt[0, 0, P:2 * P, :], whole)
                with sp.Fori(0, TILES - 3) as t:
                    loads(t + 2, p_prompt[0, 0, bass.ds(t * P + 2 * P, P), :], whole)
                    store(t, y_prompt[0, bass.ds(t * P, P), :], whole)
                loads(TILES - 1, p_sample[0, 0], sample)
                for t in (TILES - 3, TILES - 2):
                    store(t, y_prompt[0, t * P:(t + 1) * P, :], whole)
                store(TILES - 1, y_sample[0], sample)
                sp.wait_ge(out_stored, 16 * (TILES + 1))

            @block.gpsimd
            def _(pool):
                def fetch(t):
                    pool.tensor_copy(rows[:, :], S.out_row[:, :, bass.ds(t, 1)])
                    pool.tensor_copy(gate[:, :], S.gate[:, :, bass.ds(t, 1)]).then_inc(picked, 1)
                    pool.wait_ge(picked, t + 1)
                    pool.sem_inc(S.waits_met, 1)
                    for k, (dst, got) in enumerate(((y1, y1_in), (y2, y2_in))):
                        pool.indirect_dma_start(out=dst[:, :], out_offset=None, in_=S.y_rows[:, :],
                                                in_offset=bass.IndirectOffsetOnAxis(ap=rows[:, k:k + 1], axis=0)).then_inc(got, 16)

                def norm1(t):
                    pool.wait_ge(mean_ready[0], t + 1)
                    pool.tensor_tensor(rstd[:, 0:1], ms[:, 0:1], S.minus_half[:, 0:1], ALU.pow).then_inc(rstd_ready[0], 1)

                def keep(t):
                    pool.wait_ge(x4_ready, t + 1)
                    pool.wait_ge(x3_ready, t + 1)
                    pool.sem_inc(S.waits_met, 1)
                    pool.tensor_copy(x3b[:, :], x3[:, :]).then_inc(x3_kept, 1)

                def norm2(t):
                    pool.wait_ge(mean_ready[1], t + 1)
                    pool.tensor_tensor(rstd[:, 1:2], ms[:, 1:2], S.minus_half[:, 0:1], ALU.pow).then_inc(rstd_ready[1], 1)

                def refetch(t):
                    pool.wait_ge(y1_in, t * 16)
                    pool.wait_ge(y2_in, t * 16)
                    pool.wait_ge(x3_ready, t)
                    pool.sem_inc(S.waits_met, 1)
                    fetch(t)

                fetch(0)
                norm1(0)
                refetch(1)
                keep(0)
                with pool.Fori(0, TILES - 2) as t:
                    norm1(t + 1)
                    refetch(t + 2)
                    norm2(t)
                    keep(t + 1)
                norm1(TILES - 1)
                norm2(TILES - 2)
                keep(TILES - 1)
                norm2(TILES - 1)

            @block.scalar
            def _(act):
                for dst, src in ((g_rows, g_ple[0]), (b_rows, b_ple_gate[0]), (f_rows, g_final)):
                    act.dma_start(dst[:, :], src.partition_broadcast(P)).then_inc(rows_loaded, 16)

                def square(t, j):
                    if type(t) is not int or t > 0:
                        act.wait_ge(squared[j], t)
                    act.wait_ge((x3_ready, x4_ready)[j], t + 1 + j)
                    act.activation((junk1, junk2)[j][:, :], (x3, x4)[j][:, :], ACT.Square, accum_out=ss[:, j:j + 1])\
                       .then_inc(squared[j], 1)

                def to_hi(t):
                    act.wait_ge(turned, t + 1)
                    act.activation(h_hi[:, :, :], ps_h[:, :, :], ACT.Copy).then_inc(hi_ready, 1)
                    act.wait_ge(p_turned, t + 1)
                    if type(t) is not int or t > 0:
                        act.wait_ge(projected, t)
                    act.activation(p_hi[:, :, :], ps_pt[:, :, :], ACT.Copy).then_inc(p_hi_ready, 1)

                def sigmoid(t):
                    act.wait_ge(biased, t + 1)
                    act.activation(sgm[:, :], sgm[:, :], ACT.Sigmoid).then_inc(sig_ready, 1)

                square(0, 0)
                act.wait_ge(raw_loaded, NW * 16)
                for i in range(NW):
                    act.activation(w_hi[:, 2 * i:2 * i + 2, :], raw[i][:, :, :], ACT.Copy).then_inc(w_hi_ready, 1)
                to_hi(0)
                def iteration(t):
                    square(t + 1, 0)
                    sigmoid(t)
                    to_hi(t + 1)
                    square(t, 1)

                iteration(0)
                with act.Fori(1, TILES - 1) as t:
                    iteration(t)
                sigmoid(TILES - 1)
                square(TILES - 1, 1)

            @block.vector
            def _(dve):
                def combine(t):
                    dve.wait_ge(picked, t + 1)
                    dve.wait_ge(x2_loaded, t * 16 + 16)
                    dve.wait_ge(y1_in, t * 16 + 16)
                    if type(t) is not int or t > 0:
                        dve.wait_ge(x3_kept, t)
                    dve.scalar_tensor_tensor(x3[:, :], y1[:, :], gate[:, 0:1], x2[:, :], ALU.mult, ALU.add).then_inc(x3_part, 1)
                    dve.wait_ge(y2_in, t * 16 + 16)
                    dve.wait_ge(x3_part, t + 1)
                    dve.scalar_tensor_tensor(x3[:, :], y2[:, :], gate[:, 1:2], x3[:, :], ALU.mult, ALU.add).then_inc(x3_ready, 1)

                def mean(t, j):
                    dve.wait_ge(squared[j], t + 1)
                    dve.tensor_scalar(ms[:, j:j + 1], ss[:, j:j + 1], 1.0 / D, EPS, ALU.mult, ALU.add).then_inc(mean_ready[j], 1)
                    dve.wait_ge(rstd_ready[j], t + 1)

                def norm(t):
                    mean(t, 0)
                    dve.scalar_tensor_tensor(h3[:, :], x3[:, :], rstd[:, 0:1], g_rows[:, :], ALU.mult, ALU.mult)\
                       .then_inc(h3_ready, 1)

                def to_lo(t):
                    dve.wait_ge(hi_ready, t + 1)
                    dve.tensor_tensor(h_lo[:, :, :], ps_h[:, :, :], h_hi[:, :, :].bitcast(F32), ALU.subtract).then_inc(lo_ready, 1)

                def p_to_lo(t):
                    dve.wait_ge(p_hi_ready, t + 1)
                    dve.tensor_tensor(p_lo[:, :, :], ps_pt[:, :, :], p_hi[:, :, :].bitcast(F32), ALU.subtract).then_inc(p_lo_ready, 1)

                def bias(t):
                    dve.wait_ge(gates, t + 1)
                    dve.tensor_tensor(sgm[:, :], ps_g[:, :], b_rows[:, :], ALU.add).then_inc(biased, 1)

                def finish(t):
                    dve.wait_ge(sig_ready, t + 1)
                    dve.wait_ge(projected, t + 1)
                    dve.tensor_tensor(x4[:, :], ps_p[:, :], sgm[:, :], ALU.mult).then_inc(scaled, 1)
                    dve.wait_ge(scaled, t + 1)
                    dve.wait_ge(x3_kept, t + 1)
                    dve.tensor_tensor(x4[:, :], x4[:, :], x3b[:, :], ALU.add).then_inc(x4_ready, 1)

                def final(t):
                    mean(t, 1)
                    dve.wait_ge(out_stored, t * 16 + 16)
                    dve.scalar_tensor_tensor(out[:, :], x4[:, :], rstd[:, 1:2], f_rows[:, :], ALU.mult, ALU.mult)\
                       .then_inc(out_ready, 1)

                dve.sem_inc(x4_ready, 1)
                combine(0)
                dve.wait_ge(rows_loaded, 48)
                norm(0)
                for i in range(NW):
                    dve.wait_ge(w_hi_ready, i + 1)
                    dve.tensor_tensor(w_lo[:, 2 * i:2 * i + 2, :], raw[i][:, :, :], w_hi[:, 2 * i:2 * i + 2, :].bitcast(F32),
                                      ALU.subtract).then_inc(w_lo_ready, 1)
                to_lo(0)
                p_to_lo(0)
                with dve.Fori(0, TILES - 1) as t:
                    combine(t + 1)
                    norm(t + 1)
                    bias(t)
                    to_lo(t + 1)
                    finish(t)
                    p_to_lo(t + 1)
                    final(t)
                bias(TILES - 1)
                finish(TILES - 1)
                final(TILES - 1)

            @block.tensor
            def _(pe):
                def turn(t):
                    pe.wait_ge(h3_ready, t + 1)
                    for k in range(KD):
                        last = pe.transpose(ps_h[:, k, :], h3[:, k * P:(k + 1) * P], S.ident[:, :])
                    last.then_inc(turned, 1)
                    pe.wait_ge(p_loaded, t * 16 + 16)
                    for k in range(KP):
                        last = pe.transpose(ps_pt[:, k, :], p_in[:, k * P:(k + 1) * P], S.ident[:, :])
                    last.then_inc(p_turned, 1)

                def gate_products(t):
                    pe.wait_ge(lo_ready, t + 1)
                    for k in range(KD):
                        for h in range(2):
                            half = slice(h * 512, (h + 1) * 512)
                            last = matmul3(pe, ps_g[:, half], h_hi[:, k, :], h_lo[:, k, :], w_hi[:, k, half], w_lo[:, k, half],
                                           k == 0, k == KD - 1)
                    last.then_inc(gates, 1)

                def proj_products(t):
                    pe.wait_ge(p_lo_ready, t + 1)
                    for k in range(KP):
                        for h in range(2):
                            half = slice(h * 512, (h + 1) * 512)
                            last = matmul3(pe, ps_p[:, half], p_hi[:, k, :], p_lo[:, k, :], w_hi[:, KD + k, half],
                                           w_lo[:, KD + k, half], k == 0, k == KP - 1)
                    last.then_inc(projected, 1)

                turn(0)
                pe.wait_ge(w_lo_ready, NW)
                with pe.Fori(0, TILES - 1) as t:
                    gate_products(t)
                    turn(t + 1)
                    proj_products(t)
                gate_products(TILES - 1)
                proj_products(TILES - 1)


def build(nc, i, o):
    S = Shared()
    S.x2_rows = nc.dram_tensor("x2_rows", [ROWS, D], F32).ap()
    S.h2_rows = nc.dram_tensor("h2_rows", [ROWS, D], F32).ap()
    S.y_rows = nc.dram_tensor("y_rows", [ITEMS * P, D], F32).ap()
    S.table = nc.dram_tensor("token_table", [TABLE, 1], I32).ap()
    S.conv_p, S.pool_p, S.conv_s, S.pool_s = o["conv_p"], o["pool_p"], o["conv_s"], o["pool_s"]
    with ExitStack() as whole:
        S.stack = whole
        sb = lambda n, s, d=F32, at=whole: at.enter_context(nc.sbuf_tensor(n, s, d))
        S.ident, S.ones, S.minus_half = sb("ident", [P, P]), sb("ones", [P, P]), sb("minus_half", [P, 4])
        S.zero = sb("zero_rows", [P, P])
        S.gate, S.out_row = sb("gates", [P, 2, TILES]), sb("out_rows", [P, 2, TILES], I32)
        S.n_items, S.item_expert, S.item_row = sb("n_items", [P, 2], I32), sb("item_expert", [P, ITEMS], I32), sb("item_row", [P, ITEMS], I32)
        S.mix_w_loaded = whole.enter_context(nc.semaphore("mix_w_loaded"))
        S.waits_met = whole.enter_context(nc.semaphore("waits_met"))
        S.routed = whole.enter_context(nc.semaphore("routed"))
        with ExitStack() as mixer:
            S.par = sb("par", [P, KC, P_ALL], F32, mixer)
            with ExitStack() as front:
                S.conv, S.pooled = sb("conv_out", [P, KC, COLS], F32, front), sb("pooled", [P, KC, COLS], F32, front)
                S.w_pw, S.w_pool = sb("w_pw_sb", [P, KC, CH], F32, front), sb("w_pool_sb", [P, KC, P], F32, front)
                with ExitStack() as hs:
                    S.h_hi, S.h_lo = sb("h_hi", [P, KD, ROWS], F32R, hs), sb("h_lo", [P, KD, ROWS], F32R, hs)
                    constants_and_norm(nc, S, i["x_prompt"], i["x_sample"], i["state_conv"], i["state_pool"], i["g_mix"],
                                       i["w_dw"], i["b_dw"], i["g_conv_ln"], i["b_conv_ln"], i["b_pw"], i["pool_scale"])
                    in_projection_conv_pool(nc, S, i["w_in"], i["w_pw"], i["w_pool"])
                with ExitStack() as back:
                    S.o = sb("o_channels", [P, KD, ROWS], F32, back)
                    S.wo_hi, S.wo_lo = sb("w_out_hi", [P, KD, D], F32R, back), sb("w_out_lo", [P, KD, D], F32R, back)
                    mixer_outputs(nc, S, i["w_out"])
                    S.ps_route = back.enter_context(nc.psum_tensor("ps_route", [P, TILES, GROUPS + EXPERTS], F32))
                    out_projection(nc, S, i["x_prompt"], i["x_sample"], i["g_ffn"], i["w_route_group"], i["w_route_expert"])
                    routing(nc, S, i["b_route_group"], i["b_route_expert"])
        experts(nc, S, i["w_exp_gate"], i["w_exp_up"], i["w_exp_down"])
        embedding_gate(nc, S, i["p_prompt"], i["p_sample"], i["g_ple"], i["w_ple_gate"], i["b_ple_gate"],
                       i["w_ple_proj"], i["g_final"], o["y_prompt"], o["y_sample"])


_OUTS = {
    "y_prompt": (1, SEQ, D), "y_sample": (1, DEC, D), "conv_p": (1, 1, CONV_HIST, CH), "pool_p": (1, 1, POOL_HIST, CH),
    "conv_s": (1, 1, CONV_HIST, CH), "pool_s": (1, 1, POOL_HIST, CH),
}


def kernel(**inputs):
    import numpy as np
    import concourse.bacc as bacc
    from concourse.bass_utils import run_bass_kernel_spmd

    nc = bacc.Bacc("TRN2", target_bir_lowering=False, num_devices=1)
    arrays = {n: np.ascontiguousarray(a) for n, a in inputs.items()}
    ins = {n: nc.dram_tensor(n, a.shape, mybir.dt.from_np(a.dtype), kind="ExternalInput").ap() for n, a in arrays.items()}
    outs = {n: nc.dram_tensor(n, s, F32, kind="ExternalOutput").ap() for n, s in _OUTS.items()}
    build(nc, ins, outs)
    r = run_bass_kernel_spmd(nc, [arrays], core_ids=[0])
    return tuple(r.results[0][n] for n in _OUTS)
```

```python
from contextlib import ExitStack

import concourse.bass as bass
from concourse import mybir

F32, F32R = mybir.dt.float32, mybir.dt.float32r
BF16, I32 = mybir.dt.bfloat16, mybir.dt.int32
ACT, ALU, AX = mybir.ActivationFunctionType, mybir.AluOpType, mybir.AxisListType

P = 128
D, SEQ, DEC, CH = 1024, 1024, 32, 512
PLE, TAPS, POOL_HIST, POOL_GROUPS = 256, 31, 15, 4
POOL_TAPS = 7
CONV_HIST = TAPS - 1
GROUPS, PER_GROUP, D_EXP = 4, 8, 512
EXPERTS = GROUPS * PER_GROUP
EPS = 1e-6

KD = D // P
KE = D_EXP // P
KC = CH // P
GAP = 32
SAMPLE = SEQ + GAP
TILES = (SAMPLE + DEC + P - 1) // P
ROWS = TILES * P
CHUNKS = 3
CHUNK = 364
COLS = CHUNKS * CHUNK
assert COLS >= SAMPLE + DEC and CHUNK <= 512 and GAP >= CONV_HIST

P_BDW, P_GLN, P_BLN, P_BPW, P_SCALE = TAPS, TAPS + 1, TAPS + 2, TAPS + 3, TAPS + 4
P_CHIST = TAPS + 5
P_PHIST = P_CHIST + CONV_HIST
P_ALL = P_PHIST + POOL_HIST

MAX_BLOCKS = (SEQ + DEC + P - 1) // P
MAX_EXTRA = 2 * (SEQ + DEC) // P
ITEMS = EXPERTS + MAX_EXTRA
RANKS = TILES * P
TABLE = EXPERTS * RANKS + 2 * P
PIECE = 2048


def split_views(t):
    return t[:].bitcast(F32)


def matmul3(pe, out, x_hi, x_lo, w_hi, w_lo, start, stop):
    pe.matmul(out, x_hi, w_hi, start=start, stop=False)
    pe.matmul(out, x_hi, w_lo, start=False, stop=False)
    return pe.matmul(out, x_lo, w_hi, start=False, stop=stop)


GATE, UP, DOWN = (0, 1), (2, 3), (4, 5)


def load_piece(eng, S, s, n, src):
    cols = D if s in DOWN else D_EXP
    eng.wait_ge(S.w_split[s], n + 1)
    eng.dma_start(S.w_raw[s].rearrange("p (k n) -> p k n", n=cols), src).then_inc(S.raw_loaded[s], 16)


def expert_piece(S, s, e):
    w = S.w_experts[s // 2]
    half = w.shape[2] // 2
    rows = slice((s % 2) * half, (s % 2 + 1) * half)
    return w[0, e, rows, :].rearrange("o (k p) n -> p (o k) n", p=P)


def piece_hi(act, S, n, s, items):
    act.wait_ge(S.raw_loaded[s], n * 16 + 16)
    if items is not None:
        act.wait_ge(S.w_used[s], items)
    act.activation(S.w_hi[s][:, :], S.w_raw[s], ACT.Copy).then_inc(S.w_hi_ready[s], 1)


def piece_lo(eng, S, n, s):
    eng.wait_ge(S.w_hi_ready[s], n + 1)
    eng.tensor_tensor(S.w_lo[s][:, :], S.w_raw[s], S.w_hi[s][:, :].bitcast(F32), ALU.subtract)\
       .then_inc(S.w_split[s], 1)


class Shared:
    pass


def constants_and_norm(nc, S, x_prompt, x_sample, state_conv, state_pool, g_mix, w_dw, b_dw,
                       g_conv_ln, b_conv_ln, b_pw, pool_scale):
    with ExitStack() as ctx:
        sb = lambda n, s, d=F32: ctx.enter_context(nc.sbuf_tensor(n, s, d))
        sem = lambda n: S.stack.enter_context(nc.semaphore(n))
        x = [sb(f"x_in{j}", [P, D]) for j in range(3)]
        xn = [sb(f"x_norm{j}", [P, D]) for j in range(3)]
        gain = sb("g_mix_rows", [P, D])
        ss, ms, rstd = sb("ss1", [P, 3]), sb("ms1", [P, 3]), sb("rstd1", [P, 3])
        rows = sb("param_rows", [P_ALL, CH])
        ps_t = [ctx.enter_context(nc.psum_tensor(f"ps_t{j}", [P, KD, P], F32)) for j in range(3)]
        ps_par = ctx.enter_context(nc.psum_tensor("ps_par", [P, KC, P_ALL], F32))
        x_loaded = [sem(f"x_loaded{j}") for j in range(3)]
        par_loaded, gain_loaded = sem("par_loaded"), sem("gain_loaded")
        const_set = sem("const_set")
        squared, mean_ready, rstd_ready = sem("squared"), sem("mean_ready"), sem("rstd_ready")
        norm_ready, turned, hi_ready, lo_ready = sem("norm_ready"), sem("turned"), sem("h_hi_ready"), sem("h_lo_ready")
        par_turned, par_ready = sem("par_turned"), sem("par_ready")
        with nc.Block() as block:

            @block.sync
            def _(sp):
                for t in range(TILES):
                    if t >= 3:
                        sp.wait_ge(norm_ready, t - 2)
                    if t < TILES - 1:
                        sp.dma_start(x[t % 3][:, :], x_prompt[0, t * P:(t + 1) * P, :]).then_inc(x_loaded[t % 3], 16)
                    else:
                        sp.dma_start(x[t % 3][GAP:GAP + DEC, :], x_sample[0]).then_inc(x_loaded[t % 3], 16)

            @block.gpsimd
            def _(pool):
                pool.memset(S.ident[:, :], 0.0).then_inc(const_set, 1)
                pool.wait_ge(const_set, 1)
                pool.affine_select(out=S.ident[:, :], in_=S.ident[:, :], compare_op=ALU.not_equal, fill=1.0,
                                   base=0, pattern=[[-1, P]], channel_multiplier=1).then_inc(const_set, 1)
                pool.memset(S.ones[:, :], 1.0)
                pool.memset(S.zero[:, :], 0.0)
                pool.memset(S.minus_half[:, :], -0.5).then_inc(const_set, 1)
                pool.wait_ge(const_set, 3)
                with pool.Fori(0, TILES // 3) as it:
                    pool.wait_ge(mean_ready, it + 2)
                    pool.tensor_tensor(rstd[:, :], ms[:, :], S.minus_half[:, 0:3], ALU.pow).then_inc(rstd_ready, 1)

            @block.scalar
            def _(act):
                act.dma_start(gain[:, :], g_mix[0].partition_broadcast(P)).then_inc(gain_loaded, 16)
                for at, part in ((0, w_dw[0]), (P_BDW, b_dw), (P_GLN, g_conv_ln), (P_BLN, b_conv_ln),
                                 (P_BPW, b_pw), (P_SCALE, pool_scale), (P_CHIST, state_conv[0, 0]),
                                 (P_PHIST, state_pool[0, 0])):
                    act.dma_start(rows[at:at + part.shape[0], :], part).then_inc(par_loaded, 16)
                with act.Fori(0, TILES // 3) as it:
                    act.wait_ge(mean_ready, it + 1)
                    for j in range(3):
                        act.wait_ge(x_loaded[j], it * 16 + 16)
                        act.activation(xn[j][:, :], x[j][:, :], ACT.Square, accum_out=ss[:, j:j + 1]).then_inc(squared, 1)
                    for j in range(3):
                        act.wait_ge(turned, it * 3 + (j + 1))
                        act.activation(S.h_hi[:, :, bass.ds(it * (3 * P) + j * P, P)], ps_t[j][:, :, :], ACT.Copy)\
                           .then_inc(hi_ready, 1)
                act.wait_ge(par_turned, 1)
                act.activation(S.par[:, :, :], ps_par[:, :, :], ACT.Copy).then_inc(par_ready, 1)

            @block.vector
            def _(dve):
                dve.sem_inc(mean_ready, 1)
                dve.wait_ge(gain_loaded, 16)
                with dve.Fori(0, TILES // 3) as it:
                    dve.wait_ge(squared, it * 3 + 3)
                    dve.tensor_scalar(ms[:, :], ss[:, :], 1.0 / D, EPS, ALU.mult, ALU.add).then_inc(mean_ready, 1)
                    dve.wait_ge(rstd_ready, it + 1)
                    for j in range(3):
                        dve.scalar_tensor_tensor(xn[j][:, :], x[j][:, :], rstd[:, j:j + 1], gain[:, :],
                                                 ALU.mult, ALU.mult).then_inc(norm_ready, 1)
                    for j in range(3):
                        dve.wait_ge(hi_ready, it * 3 + (j + 1))
                        cols = bass.ds(it * (3 * P) + j * P, P)
                        dve.tensor_tensor(S.h_lo[:, :, cols], ps_t[j][:, :, :], S.h_hi[:, :, cols].bitcast(F32),
                                          ALU.subtract).then_inc(lo_ready, 1)

            @block.tensor
            def _(pe):
                pe.wait_ge(const_set, 2)
                pe.wait_ge(par_loaded, 8 * 16)
                for c in range(KC):
                    last = pe.transpose(ps_par[:, c, :], rows[:, c * P:(c + 1) * P], S.ident[0:P_ALL, 0:P_ALL])
                last.then_inc(par_turned, 1)
                with pe.Fori(0, TILES // 3) as it:
                    for j in range(3):
                        pe.wait_ge(norm_ready, it * 3 + (j + 1))
                        for k in range(KD):
                            last = pe.transpose(ps_t[j][:, k, :], xn[j][:, k * P:(k + 1) * P], S.ident[:, :])
                        last.then_inc(turned, 1)


def in_projection_conv_pool(nc, S, w_in, w_pw, w_pool):
    PARTS = 3
    A_PAD, U_PAD = CONV_HIST, POOL_HIST
    with ExitStack() as ctx:
        sb = lambda n, s, d=F32: ctx.enter_context(nc.sbuf_tensor(n, s, d))
        sem = lambda n: S.stack.enter_context(nc.semaphore(n))
        raw = [sb(f"w_in_raw{s}", [P, KD, P]) for s in range(PARTS)]
        w_hi = [sb(f"w_in_hi{s}", [P, KD, P], F32R) for s in range(PARTS)]
        w_lo = [sb(f"w_in_lo{s}", [P, KD, P], F32R) for s in range(PARTS)]
        a_ext, u_ext = sb("a_ext", [P, A_PAD + COLS]), sb("u_ext", [P, U_PAD + COLS])
        sums = [sb(f"window_sum{i}", [P, U_PAD + COLS]) for i in range(2)]
        sig = sb("sigmoid_gate", [P, CHUNKS, CHUNK])
        product = [sb(f"tap_product{i}", [P, COLS]) for i in range(2)]
        odd, late = sb("conv_odd_taps", [P, COLS]), sb("conv_late_taps", [P, COLS])
        inv = sb("inv_count", [P, POOL_GROUPS, 16])
        count = sb("count", [P, 16])
        tail = sb("state_tail", [P, KC, 90])
        state_rows = sb("state_rows", [90, CH])
        bank = [ctx.enter_context(nc.psum_tensor(f"z_bank{b}", [P, 512], F32)) for b in range(8)]
        a_bank, g_bank, u_bank = bank[0:3], bank[3:6], [bank[6], bank[7], bank[3]]
        raw_loaded = [sem(f"w_in_loaded{s}") for s in range(PARTS)]
        w_hi_ready = [sem(f"w_in_hi_ready{s}") for s in range(PARTS)]
        w_split = [sem(f"w_in_split{s}") for s in range(PARTS)]
        z_ready = [sem(f"z_ready{s}") for s in range(PARTS)]
        sig_ready, a_ready, a_whole, conv_step = sem("sig_ready"), sem("a_ready"), sem("a_whole"), sem("conv_step")
        u_ready, group_done, pool_step = sem("u_ready"), sem("group_done"), sem("pool_step")
        padded, inv_step, tail_turned, tail_ready = sem("padded"), sem("inv_step"), sem("tail_turned"), sem("tail_ready")
        state_stored, y_cleared = sem("state_stored"), sem("y_cleared")
        tail_read, product_ready, product_added, conv_done = (sem(n) for n in (
            "tail_read", "product_ready", "product_added", "conv_done"))
        w_view = w_in[0].rearrange("(k p) n -> p k n", p=P)
        with nc.Block() as block:

            @block.sync
            def _(sp):
                def load(c, s):
                    sp.dma_start(raw[s][:, :, :], w_view[:, :, bass.ds(c * P + s * CH, P)]).then_inc(raw_loaded[s], 16)

                for s in range(PARTS):
                    load(0, s)
                with sp.Fori(1, KC) as c:
                    for s in range(PARTS):
                        sp.wait_ge(w_split[s], c)
                        load(c, s)
                sp.dma_start(S.w_pw[:, :, :], w_pw[0].rearrange("(k p) n -> p k n", p=P)).then_inc(S.mix_w_loaded, 16)
                sp.dma_start(S.w_pool[:, :, :], w_pool[0].rearrange("g c d -> c g d")).then_inc(S.mix_w_loaded, 16)
                with sp.Fori(EXPERTS, ITEMS) as i:
                    sp.dma_start(S.y_rows[bass.ds(i * P, P), :].rearrange("p (j n) -> p j n", n=P),
                                 S.zero[:, :].unsqueeze(1).to_broadcast([P, KD, P])).then_inc(y_cleared, 16)
                sp.wait_ge(tail_ready, 1)
                for at, n, out in ((0, CONV_HIST, S.conv_p), (CONV_HIST, CONV_HIST, S.conv_s),
                                   (2 * CONV_HIST, POOL_HIST, S.pool_p), (2 * CONV_HIST + POOL_HIST, POOL_HIST, S.pool_s)):
                    sp.dma_start(out[0, 0], state_rows[at:at + n, :]).then_inc(state_stored, 16)
                sp.wait_ge(state_stored, 4 * 16)
                sp.wait_ge(y_cleared, 16 * (ITEMS - EXPERTS))

            @block.scalar
            def _(act):
                def take_hi(c, s):
                    act.wait_ge(raw_loaded[s], c * 16 + 16)
                    act.activation(w_hi[s][:, :, :], raw[s][:, :, :], ACT.Copy).then_inc(w_hi_ready[s], 1)

                def gates(c):
                    for n in range(CHUNKS):
                        act.wait_ge(z_ready[1], c * CHUNKS + (n + 1))
                        act.activation(sig[:, n, :], g_bank[n][:, 0:CHUNK], ACT.Sigmoid).then_inc(sig_ready, 1)

                def us(c):
                    act.wait_ge(group_done, c + 1)
                    for n in range(CHUNKS):
                        act.wait_ge(z_ready[2], c * CHUNKS + (n + 1))
                        act.activation(u_ext[:, U_PAD + n * CHUNK:U_PAD + (n + 1) * CHUNK], u_bank[n][:, 0:CHUNK],
                                       ACT.Copy).then_inc(u_ready, 1)

                def products(c):
                    act.wait_ge(a_whole, c + 1)
                    for j in range(POOL_TAPS):
                        k = TAPS - POOL_TAPS + j
                        act.wait_ge(product_added, c * POOL_TAPS + (j + 1))
                        act.activation(product[j % 2][:, :], a_ext[:, k:k + COLS], ACT.Copy,
                                       scale=S.par[:, bass.ds(c, 1), k:k + 1]).then_inc(product_ready, 1)

                act.sem_inc(product_added, 2)
                act.sem_inc(product_ready, 1)
                act.sem_inc(u_ready, CHUNKS)
                for s in range(PARTS):
                    take_hi(0, s)
                act.wait_ge(padded, 3)
                with act.Fori(0, KC - 1) as c:
                    act.wait_ge(z_ready[0], c * CHUNKS + CHUNKS)
                    take_hi(c + 1, 0)
                    gates(c)
                    take_hi(c + 1, 1)
                    us(c)
                    take_hi(c + 1, 2)
                    products(c)
                gates(KC - 1)
                us(KC - 1)
                products(KC - 1)
                act.wait_ge(tail_turned, 1)
                act.activation(state_rows[:, :], bank[0][0:90, :], ACT.Copy).then_inc(tail_ready, 1)

            @block.gpsimd
            def _(pool):
                steps = [0]

                def step(ins):
                    steps[0] += 1
                    ins.then_inc(pool_step, 1)
                    pool.wait_ge(pool_step, steps[0])

                def take_lo(c, s):
                    pool.wait_ge(w_hi_ready[s], c + 1)
                    pool.tensor_tensor(w_lo[s][:, :, :], raw[s][:, :, :], w_hi[s][:, :, :].bitcast(F32),
                                       ALU.subtract).then_inc(w_split[s], 1)

                def add_products(c):
                    first = c * POOL_TAPS
                    pool.wait_ge(product_ready, first + 2)
                    pool.wait_ge(conv_done, c + 1)
                    pool.tensor_copy(late[:, :], product[0][:, :]).then_inc(product_added, 1)
                    for j in range(1, POOL_TAPS):
                        pool.wait_ge(product_ready, first + j + 2)
                        pool.wait_ge(product_added, first + j + 2)
                        pool.tensor_tensor(late[:, :], late[:, :], product[j % 2][:, :], ALU.add).then_inc(product_added, 1)

                pool.sem_inc(group_done, 1)
                pool.sem_inc(tail_read, 1)
                pool.memset(a_ext[:, 0:A_PAD], 0.0).then_inc(padded, 1)
                pool.memset(u_ext[:, 0:U_PAD], 0.0).then_inc(padded, 1)
                pool.memset(sums[0][:, 0:16], 0.0)
                pool.memset(sums[1][:, 0:16], 0.0).then_inc(padded, 1)
                pool.iota(count[:, :], pattern=[[1, 16]], base=1, channel_multiplier=0,
                          allow_small_or_imprecise_dtypes=True).then_inc(inv_step, 1)
                for s in range(PARTS):
                    take_lo(0, s)
                pool.wait_ge(inv_step, 2 + POOL_GROUPS)
                for c in range(KC):
                    if c + 1 < KC:
                        for s in range(PARTS):
                            take_lo(c + 1, s)
                    pool.wait_ge(a_whole, c + 1)
                    pool.tensor_copy(tail[:, c, 0:CONV_HIST], a_ext[:, SEQ:SEQ + CONV_HIST])
                    pool.tensor_copy(tail[:, c, CONV_HIST:2 * CONV_HIST],
                                     a_ext[:, SAMPLE + DEC:SAMPLE + DEC + CONV_HIST]).then_inc(tail_read, 1)
                    add_products(c)
                    pool.wait_ge(u_ready, (c + 2) * CHUNKS)
                    step(pool.tensor_copy(u_ext[:, SAMPLE:SAMPLE + POOL_HIST], S.par[:, c, P_PHIST:P_ALL]))
                    pool.tensor_copy(tail[:, c, 2 * CONV_HIST:2 * CONV_HIST + POOL_HIST], u_ext[:, SEQ:SEQ + POOL_HIST])
                    pool.tensor_copy(tail[:, c, 2 * CONV_HIST + POOL_HIST:90],
                                     u_ext[:, SAMPLE + DEC:SAMPLE + DEC + POOL_HIST])
                    src = u_ext
                    for i in range(c + 1):
                        d = 1 << i
                        first = 2 * d - 1
                        dst = sums[i % 2]
                        step(pool.tensor_tensor(dst[:, first:], src[:, first:], src[:, first - d:U_PAD + COLS - d], ALU.add))
                        src = dst
                    mean = sums[(c + 1) % 2]
                    pool.tensor_tensor(mean[:, U_PAD:U_PAD + 16], src[:, U_PAD:U_PAD + 16], inv[:, c, :], ALU.mult)
                    step(pool.tensor_scalar(mean[:, U_PAD + 16:], src[:, U_PAD + 16:], 1.0 / (2 << c), None, ALU.mult))
                    pool.tensor_tensor(S.pooled[:, c, :], mean[:, U_PAD:], u_ext[:, U_PAD:], ALU.subtract)\
                        .then_inc(group_done, 1)

            @block.vector
            def _(dve):
                STEPS = TAPS - POOL_TAPS + 1
                dve.sem_inc(a_ready, CHUNKS)
                dve.sem_inc(conv_done, 1)
                dve.wait_ge(inv_step, 1)
                for g in range(POOL_GROUPS):
                    dve.tensor_scalar(inv[:, g, :], count[:, :], float(2 << g), None, ALU.min).then_inc(inv_step, 1)
                dve.wait_ge(inv_step, 1 + POOL_GROUPS)
                dve.reciprocal(inv[:, :, :], inv[:, :, :]).then_inc(inv_step, 1)
                dve.wait_ge(padded, 1)
                with dve.Fori(0, KC) as c:
                    dve.wait_ge(tail_read, c + 1)
                    dve.wait_ge(product_ready, c * POOL_TAPS + 1)
                    for n in range(CHUNKS):
                        dve.wait_ge(sig_ready, c * CHUNKS + (n + 1))
                        dve.tensor_tensor(a_ext[:, A_PAD + n * CHUNK:A_PAD + (n + 1) * CHUNK], a_bank[n][:, 0:CHUNK],
                                          sig[:, n, :], ALU.mult).then_inc(a_ready, 1)
                    dve.wait_ge(a_ready, c * CHUNKS + 2 * CHUNKS)
                    dve.tensor_copy(a_ext[:, SAMPLE:SAMPLE + CONV_HIST],
                                    S.par[:, bass.ds(c, 1), P_CHIST:P_PHIST]).then_inc(a_whole, 1)
                    dve.wait_ge(a_whole, c + 1)
                    even = S.conv[:, bass.ds(c, 1), :]
                    dve.tensor_scalar(even, a_ext[:, 0:COLS], S.par[:, bass.ds(c, 1), 0:1],
                                      S.par[:, bass.ds(c, 1), P_BDW:P_BDW + 1], ALU.mult, ALU.add).then_inc(conv_step, 1)
                    dve.tensor_scalar(odd[:, :], a_ext[:, 1:1 + COLS], S.par[:, bass.ds(c, 1), 1:2],
                                      None, ALU.mult).then_inc(conv_step, 1)
                    for k in range(2, TAPS - POOL_TAPS):
                        out = even if k % 2 == 0 else odd[:, :]
                        dve.wait_ge(conv_step, c * STEPS + k - 1)
                        dve.scalar_tensor_tensor(out, a_ext[:, k:k + COLS], S.par[:, bass.ds(c, 1), k:k + 1], out,
                                                 ALU.mult, ALU.add).then_inc(conv_step, 1)
                    dve.wait_ge(conv_step, c * STEPS + STEPS - 1)
                    dve.tensor_tensor(even, even, odd[:, :], ALU.add).then_inc(conv_step, 1)
                    dve.wait_ge(conv_step, c * STEPS + STEPS)
                    dve.wait_ge(product_added, c * POOL_TAPS + POOL_TAPS + 2)
                    dve.tensor_tensor(even, even, late[:, :], ALU.add).then_inc(conv_done, 1)
                    dve.wait_ge(conv_done, c + 2)

            @block.tensor
            def _(pe):
                with pe.Fori(0, KC) as c:
                    for s, banks in ((0, a_bank), (1, g_bank), (2, u_bank)):
                        pe.wait_ge(w_split[s], c + 1)
                        for n in range(CHUNKS):
                            if s == 0:
                                pe.wait_ge(a_ready, c * CHUNKS + (n + 1))
                            if s == 1 and n == 0:
                                pe.wait_ge(u_ready, c * CHUNKS + CHUNKS)
                            if s == 2 and n == 2:
                                pe.wait_ge(sig_ready, c * CHUNKS + 1)
                            cols = slice(n * CHUNK, (n + 1) * CHUNK)
                            for k in range(KD):
                                last = matmul3(pe, banks[n][:, 0:CHUNK], w_hi[s][:, k, :], w_lo[s][:, k, :],
                                               S.h_hi[:, k, cols], S.h_lo[:, k, cols], k == 0, k == KD - 1)
                            last.then_inc(z_ready[s], 1)
                pe.wait_ge(group_done, KC + 1)
                for c in range(KC):
                    last = pe.transpose(bank[0][0:90, c * P:(c + 1) * P], tail[:, c, :], S.ident[:, :])
                last.then_inc(tail_turned, 1)


def mixer_outputs(nc, S, w_out):
    with ExitStack() as ctx:
        sb = lambda n, s, d=F32: ctx.enter_context(nc.sbuf_tensor(n, s, d))
        sem = lambda n: S.stack.enter_context(nc.semaphore(n))
        sq = sb("conv_sq", [P, KC, COLS])
        var, rstd = sb("conv_var", [P, CHUNKS, CHUNK]), sb("conv_rstd", [P, CHUNKS, CHUNK])
        root, fix = sb("conv_root", [P, CHUNKS, CHUNK]), sb("conv_fix", [P, CHUNKS, CHUNK])
        raw = [sb(f"w_out_raw{i}", [P, 2, D]) for i in range(2)]
        bank = [ctx.enter_context(nc.psum_tensor(f"mix_bank{b}", [P, 512], F32)) for b in range(8)]
        raw_loaded = [sem(f"w_out_loaded{i}") for i in range(2)]
        w_hi_ready, w_lo_ready = sem("w_out_hi_ready"), sem("w_out_lo_ready")
        sum_ready, centred, sq_ready = sem("sum_ready"), sem("centred"), sem("sq_ready")
        varsum_ready, var_ready, rstd_ready, root_ready = sem("varsum_ready"), sem("var_ready"), sem("conv_rstd_step"), sem("root_ready")
        scaled, c_ready, o_ready, o_left = sem("scaled"), sem("c_ready"), sem("o_product"), sem("o_left")
        cols = [slice(n * CHUNK, (n + 1) * CHUNK) for n in range(CHUNKS)]
        outs = [(KC + g, n) for g in range(KC) for n in range(CHUNKS)] + [(c, n) for n in range(CHUNKS) for c in range(KC)]
        o_bank = lambda i: bank[3 + i % 5][:, 0:CHUNK]
        w_view = w_out[0].rearrange("(k p) n -> p k n", p=P)
        with nc.Block() as block:

            @block.sync
            def _(sp):
                for i in range(KD // 2):
                    if i >= 2:
                        sp.wait_ge(w_lo_ready, i - 1)
                    sp.dma_start(raw[i % 2][:, :, :], w_view[:, 2 * i:2 * i + 2, :]).then_inc(raw_loaded[i % 2], 16)

            @block.gpsimd
            def _(pool):
                def take_lo(i):
                    pool.wait_ge(w_hi_ready, i + 1)
                    pool.tensor_tensor(S.wo_lo[:, 2 * i:2 * i + 2, :], raw[i % 2][:, :, :],
                                       S.wo_hi[:, 2 * i:2 * i + 2, :].bitcast(F32), ALU.subtract).then_inc(w_lo_ready, 1)

                pool.memset(S.o[:, :, COLS:ROWS], 0.0)
                for i in range(KD // 2):
                    take_lo(i)

            @block.scalar
            def _(act):
                def take_hi(i):
                    act.wait_ge(raw_loaded[i % 2], 16 * (i // 2) + 16)
                    act.activation(S.wo_hi[:, 2 * i:2 * i + 2, :], raw[i % 2][:, :, :], ACT.Copy).then_inc(w_hi_ready, 1)

                def leave(i):
                    act.wait_ge(o_ready, i + 1)
                    block_of, n = outs[i]
                    if block_of >= KC:
                        g = block_of - KC
                        act.activation(S.o[:, block_of, cols[n]], o_bank(i), ACT.Copy, scale=S.par[:, g, P_SCALE:P_SCALE + 1])\
                           .then_inc(o_left, 1)
                    else:
                        act.activation(S.o[:, block_of, cols[n]], o_bank(i), ACT.Identity,
                                       bias=S.par[:, block_of, P_BPW:P_BPW + 1]).then_inc(o_left, 1)

                take_hi(0)
                take_hi(1)
                for n in range(CHUNKS):
                    act.wait_ge(centred, n + 1)
                    act.activation(sq[:, :, cols[n]], S.conv[:, :, cols[n]], ACT.Square).then_inc(sq_ready, 1)
                for i in range(KC * CHUNKS):
                    leave(i)
                    if i in (2 * CHUNKS + 1, 2 * CHUNKS + 2, 2 * CHUNKS + 3):
                        n = i - 2 * CHUNKS - 1
                        act.wait_ge(var_ready, n + 1)
                        act.activation(root[:, n, :], var[:, n, :], ACT.Sqrt).then_inc(root_ready, 1)
                for n in range(CHUNKS):
                    act.wait_ge(scaled, n + 1)
                    for c in range(KC):
                        act.activation(S.conv[:, c, cols[n]], S.conv[:, c, cols[n]], ACT.Silu,
                                       bias=S.par[:, c, P_BLN:P_BLN + 1], scale=S.par[:, c, P_GLN:P_GLN + 1])\
                           .then_inc(c_ready, 1)
                    if n >= 1:
                        for i in range(KC):
                            leave(KC * CHUNKS + (n - 1) * KC + i)
                for i in range(KC):
                    leave(KC * CHUNKS + (CHUNKS - 1) * KC + i)
                for i in range(2, KD // 2):
                    take_hi(i)

            @block.vector
            def _(dve):
                steps = [0]

                def step(ins):
                    steps[0] += 1
                    ins.then_inc(rstd_ready, 1)
                    dve.wait_ge(rstd_ready, steps[0])

                for n in range(CHUNKS):
                    dve.wait_ge(sum_ready, n + 1)
                    dve.scalar_tensor_tensor(S.conv[:, :, cols[n]],
                                             bank[n][:, 0:CHUNK].unsqueeze(1).to_broadcast([P, KC, CHUNK]), -1.0 / CH,
                                             S.conv[:, :, cols[n]], ALU.mult, ALU.add).then_inc(centred, 1)
                for n in range(CHUNKS):
                    dve.wait_ge(varsum_ready, n + 1)
                    dve.tensor_scalar(var[:, n, :], bank[n][:, 0:CHUNK], 1.0 / CH, EPS, ALU.mult, ALU.add)\
                       .then_inc(var_ready, 1)
                for n in range(CHUNKS):
                    dve.wait_ge(root_ready, n + 1)
                    step(dve.reciprocal(rstd[:, n, :], root[:, n, :]))
                    step(dve.tensor_tensor(fix[:, n, :], rstd[:, n, :], rstd[:, n, :], ALU.mult))
                    step(dve.scalar_tensor_tensor(fix[:, n, :], fix[:, n, :], -0.5, var[:, n, :], ALU.mult, ALU.mult))
                    step(dve.scalar_tensor_tensor(rstd[:, n, :], fix[:, n, :], 1.5, rstd[:, n, :], ALU.add, ALU.mult))
                    dve.tensor_tensor(S.conv[:, :, cols[n]], S.conv[:, :, cols[n]],
                                      rstd[:, n, :].unsqueeze(1).to_broadcast([P, KC, CHUNK]), ALU.mult).then_inc(scaled, 1)

            @block.tensor
            def _(pe):
                for n in range(CHUNKS):
                    for c in range(KC):
                        last = pe.matmul(bank[n][:, 0:CHUNK], S.ones[:, :], S.conv[:, c, cols[n]],
                                         start=(c == 0), stop=(c == KC - 1))
                    last.then_inc(sum_ready, 1)
                pe.wait_ge(S.mix_w_loaded, 32)
                i = 0
                for g in range(KC):
                    for n in range(CHUNKS):
                        if i >= 5:
                            pe.wait_ge(o_left, i - 4)
                        pe.matmul(o_bank(i), S.w_pool[:, g, :], S.pooled[:, g, cols[n]], start=True, stop=True)\
                          .then_inc(o_ready, 1)
                        i += 1
                        if g == 1:
                            pe.wait_ge(sq_ready, n + 1)
                            for c in range(KC):
                                last = pe.matmul(bank[n][:, 0:CHUNK], S.ones[:, :], sq[:, c, cols[n]],
                                                 start=(c == 0), stop=(c == KC - 1))
                            last.then_inc(varsum_ready, 1)
                for n in range(CHUNKS):
                    pe.wait_ge(c_ready, KC * (n + 1))
                    for c in range(KC):
                        pe.wait_ge(o_left, i - 4)
                        for k in range(KC):
                            last = pe.matmul(o_bank(i), S.w_pw[:, k, c * P:(c + 1) * P], S.conv[:, k, cols[n]],
                                             start=(k == 0), stop=(k == KC - 1))
                        last.then_inc(o_ready, 1)
                        i += 1


def out_projection(nc, S, x_prompt, x_sample, g_ffn, w_rg, w_re):
    HALF = KD // 2
    with ExitStack() as ctx:
        sb = lambda n, s, d=F32: ctx.enter_context(nc.sbuf_tensor(n, s, d))
        sem = lambda n: S.stack.enter_context(nc.semaphore(n))
        x, x2, h2, junk, gain = (sb(n, [P, D]) for n in ("x_res", "x2_tile", "h2_tile", "sq_junk4", "g_ffn_rows"))
        o_hi, o_lo = sb("o_hi", [P, KD, P], F32R), sb("o_lo", [P, KD, P], F32R)
        h2_t = sb("h2_t", [P, KD, P])
        w_route = sb("w_route", [P, KD, GROUPS + EXPERTS])
        ss, ms, rstd = sb("ss4", [P, 1]), sb("ms4", [P, 1]), sb("rstd4", [P, 1])
        ps = [ctx.enter_context(nc.psum_tensor(f"ps_out{h}", [P, 512], F32)) for h in range(2)]
        ps_t = ctx.enter_context(nc.psum_tensor("ps_h2t", [P, KD, P], F32))
        x_loaded, gain_loaded, route_loaded = sem("x_loaded4"), sem("gain_loaded4"), sem("route_loaded")
        hi_ready, lo_ready, used, added = sem("o_hi_ready"), sem("o_lo_ready"), sem("o_used"), sem("added")
        squared, mean_ready, rstd_ready, h2_ready = sem("squared4"), sem("mean4"), sem("rstd_ready4"), sem("h2_ready")
        turned, h2t_ready = sem("h2_turned"), sem("h2t_ready")
        x2_stored, h2_stored = sem("x2_stored"), sem("h2_stored")
        with nc.Block() as block:

            @block.sync
            def _(sp):
                def store(t):
                    sp.wait_ge(added, t + 2)
                    sp.dma_start(S.x2_rows[bass.ds(t * P, P), :], x2[:, :]).then_inc(x2_stored, 16)

                def store_h(t):
                    sp.wait_ge(h2_ready, t + 1)
                    sp.dma_start(S.h2_rows[bass.ds(t * P, P), :], h2[:, :]).then_inc(h2_stored, 16)

                sp.sem_inc(x2_stored, 16)
                sp.sem_inc(h2_stored, 16)
                sp.dma_start(x[:, :], x_prompt[0, 0:P, :]).then_inc(x_loaded, 16)
                for s in range(6):
                    sp.sem_inc(S.w_split[s], 1)
                    load_piece(sp, S, s, 0, expert_piece(S, s, slice(0, 1)))
                with sp.Fori(0, TILES - 2) as t:
                    store(t)
                    sp.dma_start(x[:, :], x_prompt[0, bass.ds(t * P + P, P), :]).then_inc(x_loaded, 16)
                    store_h(t)
                store(TILES - 2)
                sp.dma_start(x[GAP:GAP + DEC, :], x_sample[0]).then_inc(x_loaded, 16)
                store_h(TILES - 2)
                store(TILES - 1)
                store_h(TILES - 1)
                sp.wait_ge(x2_stored, 16 * (TILES + 1))
                sp.wait_ge(h2_stored, 16 * (TILES + 1))

            @block.gpsimd
            def _(pool):
                with pool.Fori(0, TILES) as t:
                    pool.wait_ge(mean_ready, t + 1)
                    pool.tensor_tensor(rstd[:, :], ms[:, :], S.minus_half[:, 0:1], ALU.pow).then_inc(rstd_ready, 1)

            @block.scalar
            def _(act):
                act.dma_start(gain[:, :], g_ffn[0].partition_broadcast(P)).then_inc(gain_loaded, 16)
                act.dma_start(w_route[:, :, 0:GROUPS], w_rg[0].rearrange("(k p) n -> p k n", p=P)).then_inc(route_loaded, 16)
                act.dma_start(w_route[:, :, GROUPS:], w_re[0].rearrange("(k p) n -> p k n", p=P)).then_inc(route_loaded, 16)

                def take_hi(t, i):
                    ks = slice(i * HALF, (i + 1) * HALF)
                    act.activation(o_hi[:, ks, :], S.o[:, ks, bass.ds(t * P, P)], ACT.Copy).then_inc(hi_ready, 1)

                def next_hi(t):
                    for i in range(2):
                        act.wait_ge(used, 2 * t + (i - 1))
                        take_hi(t, i)

                def square(t):
                    if type(t) is not int or t > 0:
                        act.wait_ge(squared, t)
                    act.wait_ge(added, t + 2)
                    act.activation(junk[:, :], x2[:, :], ACT.Square, accum_out=ss[:, :]).then_inc(squared, 1)

                def leave(t):
                    act.wait_ge(turned, t + 2)
                    act.activation(h2_t[:, :, :], ps_t[:, :, :], ACT.Copy).then_inc(h2t_ready, 1)

                take_hi(0, 0)
                take_hi(0, 1)
                next_hi(1)
                square(0)
                with act.Fori(1, TILES - 1) as t:
                    next_hi(t + 1)
                    square(t)
                    leave(t - 1)
                square(TILES - 1)
                leave(TILES - 2)
                leave(TILES - 1)

            @block.vector
            def _(dve):
                def take_lo(t, i):
                    ks = slice(i * HALF, (i + 1) * HALF)
                    dve.wait_ge(hi_ready, t * 2 + (i + 1))
                    dve.tensor_tensor(o_lo[:, ks, :], S.o[:, ks, bass.ds(t * P, P)], o_hi[:, ks, :].bitcast(F32),
                                      ALU.subtract).then_inc(lo_ready, 1)

                def add(t):
                    dve.wait_ge(x_loaded, t * 16 + 16)
                    dve.wait_ge(x2_stored, t * 16 + 16)
                    dve.wait_ge(used, t * 2 + 2)
                    dve.tensor_tensor(x2[:, 0:512], ps[0][:, :], x[:, 0:512], ALU.add)
                    dve.tensor_tensor(x2[:, 512:D], ps[1][:, :], x[:, 512:D], ALU.add).then_inc(added, 1)

                def norm(t):
                    dve.wait_ge(squared, t + 1)
                    dve.tensor_scalar(ms[:, :], ss[:, :], 1.0 / D, EPS, ALU.mult, ALU.add).then_inc(mean_ready, 1)
                    dve.wait_ge(rstd_ready, t + 1)
                    dve.wait_ge(h2_stored, t * 16 + 16)
                    dve.wait_ge(turned, t + 1)
                    dve.scalar_tensor_tensor(h2[:, :], x2[:, :], rstd[:, :], gain[:, :], ALU.mult, ALU.mult)\
                       .then_inc(h2_ready, 1)
                    dve.wait_ge(h2_ready, t + 1)

                dve.sem_inc(added, 1)
                dve.wait_ge(gain_loaded, 16)
                take_lo(0, 0)
                take_lo(0, 1)
                with dve.Fori(0, TILES - 1) as t:
                    take_lo(t + 1, 0)
                    add(t)
                    take_lo(t + 1, 1)
                    norm(t)
                add(TILES - 1)
                norm(TILES - 1)

            @block.tensor
            def _(pe):
                def products(t):
                    pe.wait_ge(added, t + 1)
                    for i in range(2):
                        pe.wait_ge(lo_ready, t * 2 + (i + 1))
                        for k in range(i * HALF, (i + 1) * HALF):
                            for h in range(2):
                                half = slice(h * 512, (h + 1) * 512)
                                last = matmul3(pe, ps[h][:, :], o_hi[:, k, :], o_lo[:, k, :], S.wo_hi[:, k, half],
                                               S.wo_lo[:, k, half], k == 0, k == KD - 1)
                        last.then_inc(used, 1)

                def turn(t):
                    pe.wait_ge(h2_ready, t + 1)
                    for k in range(KD):
                        last = pe.transpose(ps_t[:, k, :], h2[:, k * P:(k + 1) * P], S.ident[:, :])
                    last.then_inc(turned, 1)

                def route(t):
                    pe.wait_ge(h2t_ready, t + 1)
                    for k in range(KD):
                        last = pe.matmul(S.ps_route[:, bass.ds(t, 1), :], h2_t[:, k, :], w_route[:, k, :],
                                         start=(k == 0), stop=(k == KD - 1))
                    last.then_inc(S.routed, 1)

                pe.sem_inc(turned, 1)
                products(0)
                products(1)
                turn(0)
                pe.wait_ge(route_loaded, 32)
                with pe.Fori(2, TILES) as t:
                    products(t)
                    route(t - 2)
                    turn(t - 1)
                route(TILES - 2)
                turn(TILES - 1)
                route(TILES - 1)


def routing(nc, S, b_rg, b_re):
    T, E, G, C8 = TILES, EXPERTS, GROUPS, PER_GROUP
    with ExitStack() as ctx:
        sb = lambda n, s, d=F32: ctx.enter_context(nc.sbuf_tensor(n, s, d))
        sem = lambda n: S.stack.enter_context(nc.semaphore(n))
        bias = sb("route_bias", [P, G + E])
        lg = sb("logits", [P, T, G + E])
        idx = sb("iota_experts", [P, E])
        valid = sb("valid_rows", [P, T])
        dump, first_row = sb("dump_rows", [P, 2, T]), sb("first_rows", [P, 2, T])
        tok = sb("token_rows", [P, T], I32)
        tri = sb("earlier", [P, P], BF16)
        ones_b = sb("ones_b", [P, P], BF16)
        zero = sb("zero_table", [P, TABLE // P], I32)
        a9, b9, gsel, gw = (sb(n, [P, T]) for n in ("a9", "b9", "gsel", "gw"))
        g4, g4b = sb("g4", [P, T, G]), sb("g4b", [P, T, G])
        e32, esel, e8, e8b = sb("e32", [P, T, G, C8]), sb("esel", [P, T, C8]), sb("e8", [P, T, C8]), sb("e8b", [P, T, C8])
        m1, m2 = sb("m1", [P, T]), sb("m2", [P, T])
        eid = sb("eid", [P, 2, T])
        oh = [sb(f"onehot{k}", [P, T, E]) for k in range(2)]
        ohs = sb("onehot_sum", [P, T, E], BF16)
        tot, base, rank = sb("tile_totals", [P, T, E]), sb("tile_base", [P, T + 1, E]), sb("rank", [P, T, E])
        t32 = sb("t32", [P, T, E])
        over, cum, cum2 = sb("over", [P, E]), sb("cum", [P, E]), sb("cum2", [P, E])
        rk, osk, item, s18 = (sb(n, [P, 2, T]) for n in ("rk", "osk", "item", "s18"))
        scatter_i = sb("scatter_rows", [P, 2, T], I32)
        ended, ended_at = sb("ended_experts", [P, ITEMS + 1, E]), sb("ended_at", [P, ITEMS + 1, E])
        number, owner, row, n1 = (sb("item_numbers", [P, ITEMS + 1]), sb("item_owners", [P, ITEMS + 1]),
                                  sb("item_rows", [P, ITEMS + 1]), sb("n1", [P, 1]))
        ps_rank = ctx.enter_context(nc.psum_tensor("ps_rank", [P, T, E], F32))
        ps_tot = ctx.enter_context(nc.psum_tensor("ps_tot", [P, T, E], F32))
        bias_loaded, made, cleared, exp_ready = sem("bias_loaded"), sem("tables_made"), sem("table_cleared"), sem("exp_ready")
        chain, to_exp, to_rank, ranked = sem("route_chain"), sem("to_exp"), sem("to_rank"), sem("ranked")
        rows_ready, scattered = sem("rows_ready"), sem("scattered")
        bc = lambda ap, shape: ap.to_broadcast(shape)
        with nc.Block() as block:

            @block.sync
            def _(sp):
                sp.dma_start(bias[:, 0:G], b_rg[0].partition_broadcast(P)).then_inc(bias_loaded, 16)
                sp.dma_start(bias[:, G:], b_re[0].partition_broadcast(P)).then_inc(bias_loaded, 16)
                sp.wait_ge(made, 1)
                sp.dma_start(S.table.rearrange("(p n) o -> p (n o)", p=P), zero[:, :]).then_inc(cleared, 16)
                for s in GATE + UP:
                    load_piece(sp, S, s, 1, expert_piece(S, s, slice(1, 2)))

            @block.gpsimd
            def _(pool):
                pool.memset(zero[:, :], 0).then_inc(made, 1)
                pool.iota(idx[:, :], pattern=[[1, E]], base=0, channel_multiplier=0, allow_small_or_imprecise_dtypes=True)
                pool.iota(number[:, :], pattern=[[1, ITEMS + 1]], base=0, channel_multiplier=0,
                          allow_small_or_imprecise_dtypes=True)
                pool.iota(tok[:, :], pattern=[[P, T]], base=0, channel_multiplier=1)
                pool.memset(valid[:, :], 1.0)
                pool.memset(tri[:, :], 1.0)
                pool.memset(dump[:, :, 0:T - 1], 0.0)
                pool.iota(dump[:, :, T - 1], pattern=[[P, 2]], base=E * RANKS, channel_multiplier=1,
                          allow_small_or_imprecise_dtypes=True)
                pool.memset(first_row[:, :, 0:T - 1], 0.0)
                pool.iota(first_row[:, :, T - 1], pattern=[[0, 2]], base=0, channel_multiplier=1,
                          allow_small_or_imprecise_dtypes=True)
                pool.memset(ones_b[:, :], 1.0).then_inc(made, 1)
                pool.wait_ge(made, 2)
                pool.affine_select(out=valid[:, T - 1:T], in_=valid[:, T - 1:T], compare_op=ALU.is_ge, fill=0.0,
                                   base=-GAP, pattern=[[0, 1]], channel_multiplier=1).then_inc(made, 1)
                pool.wait_ge(made, 3)
                pool.affine_select(out=valid[:, T - 1:T], in_=valid[:, T - 1:T], compare_op=ALU.is_ge, fill=0.0,
                                   base=GAP + DEC - 1, pattern=[[0, 1]], channel_multiplier=-1)
                pool.affine_select(out=tri[:, :], in_=tri[:, :], compare_op=ALU.is_gt, fill=0.0,
                                   base=0, pattern=[[1, P]], channel_multiplier=-1).then_inc(made, 1)
                for s in GATE + UP:
                    piece_lo(pool, S, 0, s)
                pool.wait_ge(cleared, 16)
                pool.wait_ge(rows_ready, 1)
                for k in range(2):
                    for t in range(T):
                        pool.indirect_dma_start(out=S.table[:, :],
                                                out_offset=bass.IndirectOffsetOnAxis(ap=scatter_i[:, k, t:t + 1], axis=0),
                                                in_=tok[:, t:t + 1], in_offset=None).then_inc(scattered, 16)
                pool.wait_ge(scattered, 2 * T * 16)

            @block.scalar
            def _(act):
                for s in GATE + UP:
                    piece_hi(act, S, 0, s, None)
                act.wait_ge(to_exp, 1)
                act.activation(g4[:, :, :], g4[:, :, :], ACT.Exp).then_inc(exp_ready, 1)
                act.wait_ge(to_exp, 2)
                act.activation(m2[:, :], m2[:, :], ACT.Exp).then_inc(exp_ready, 1)

            @block.tensor
            def _(pe):
                pe.wait_ge(made, 4)
                pe.wait_ge(to_rank, 1)
                pe.matmul(ps_tot[:, :, :], ones_b[:, :], ohs[:, :, :], start=True, stop=True)
                pe.matmul(ps_rank[:, :, :], tri[:, :], ohs[:, :, :], start=True, stop=True).then_inc(ranked, 1)

            @block.vector
            def _(dve):
                links = [0]

                def step(ins):
                    links[0] += 1
                    ins.then_inc(chain, 1)
                    dve.wait_ge(chain, links[0])

                tt = lambda o, a, b, op: step(dve.tensor_tensor(o, a, b, op))
                ts = lambda o, a, s1, s2, o1, o2=None: step(
                    dve.tensor_scalar(o, a, s1, s2, o1) if o2 is None else dve.tensor_scalar(o, a, s1, s2, o1, o2))
                red = lambda o, a, op: step(dve.tensor_reduce(o, a, AX.X, op))

                def argfirst(out, values, best, n, work):
                    tt(work, values, bc(best.unsqueeze(2), [P, T, n]), ALU.is_equal)
                    step(dve.scalar_tensor_tensor(work, bc(idx[:, 0:n].unsqueeze(1), [P, T, n]), -float(E), work,
                                                  ALU.add, ALU.mult))
                    red(out, work, ALU.min)
                    ts(out, out, float(E), None, ALU.add)

                dve.wait_ge(made, 4)
                dve.wait_ge(bias_loaded, 32)
                dve.wait_ge(S.routed, T)
                tt(lg[:, :, :], S.ps_route[:, :, :], bc(bias[:, :].unsqueeze(1), [P, T, G + E]), ALU.add)
                red(a9[:, :], lg[:, :, 0:G], ALU.max)
                argfirst(gsel[:, :], lg[:, :, 0:G], a9[:, :], G, g4[:, :, :])
                tt(g4[:, :, :], lg[:, :, 0:G], bc(a9[:, :].unsqueeze(2), [P, T, G]), ALU.subtract)
                dve.sem_inc(to_exp, 1)
                tt(g4b[:, :, :], bc(idx[:, 0:G].unsqueeze(1), [P, T, G]), bc(gsel[:, :].unsqueeze(2), [P, T, G]), ALU.is_equal)
                tt(e32[:, :, :, :], lg[:, :, G:].rearrange("p t (g e) -> p t g e", g=G),
                   bc(g4b[:, :, :].unsqueeze(3), [P, T, G, C8]), ALU.mult)
                tt(esel[:, :, :], e32[:, :, 0, :], e32[:, :, 1, :], ALU.add)
                tt(esel[:, :, :], esel[:, :, :], e32[:, :, 2, :], ALU.add)
                tt(esel[:, :, :], esel[:, :, :], e32[:, :, 3, :], ALU.add)
                red(m1[:, :], esel[:, :, :], ALU.max)
                argfirst(eid[:, 0, :], esel[:, :, :], m1[:, :], C8, e8[:, :, :])
                tt(e8[:, :, :], bc(idx[:, 0:C8].unsqueeze(1), [P, T, C8]), bc(eid[:, 0, :].unsqueeze(2), [P, T, C8]),
                   ALU.is_equal)
                step(dve.scalar_tensor_tensor(e8b[:, :, :], e8[:, :, :], -1e30, esel[:, :, :], ALU.mult, ALU.add))
                red(m2[:, :], e8b[:, :, :], ALU.max)
                argfirst(eid[:, 1, :], e8b[:, :, :], m2[:, :], C8, e8[:, :, :])
                tt(m2[:, :], m2[:, :], m1[:, :], ALU.subtract)
                dve.sem_inc(to_exp, 1)
                for k in range(2):
                    step(dve.scalar_tensor_tensor(eid[:, k, :], gsel[:, :], float(C8), eid[:, k, :], ALU.mult, ALU.add))
                    step(dve.scalar_tensor_tensor(eid[:, k, :], eid[:, k, :], 1.0, valid[:, :], ALU.add, ALU.mult))
                    ts(eid[:, k, :], eid[:, k, :], -1.0, None, ALU.add)
                    tt(oh[k][:, :, :], bc(idx[:, :].unsqueeze(1), [P, T, E]), bc(eid[:, k, :].unsqueeze(2), [P, T, E]),
                       ALU.is_equal)
                tt(ohs[:, :, :], oh[0][:, :, :], oh[1][:, :, :], ALU.add)
                dve.sem_inc(to_rank, 1)
                dve.wait_ge(exp_ready, 2)
                red(gw[:, :], g4[:, :, :], ALU.add)
                step(dve.reciprocal(gw[:, :], gw[:, :]))
                ts(a9[:, :], m2[:, :], 1.0, None, ALU.add)
                step(dve.reciprocal(a9[:, :], a9[:, :]))
                tt(S.gate[:, 0, :], a9[:, :], gw[:, :], ALU.mult)
                tt(S.gate[:, 1, :], S.gate[:, 0, :], m2[:, :], ALU.mult)
                dve.wait_ge(ranked, 1)
                step(dve.tensor_copy(tot[:, :, :], ps_tot[:, :, :]))
                step(dve.memset(base[:, 0, :], 0.0))
                for t in range(T):
                    tt(base[:, t + 1, :], base[:, t, :], tot[:, t, :], ALU.add)
                tt(rank[:, :, :], ps_rank[:, :, :], base[:, 0:T, :], ALU.add)
                for k in range(2):
                    tt(t32[:, :, :], oh[k][:, :, :], rank[:, :, :], ALU.mult)
                    red(rk[:, k, :], t32[:, :, :], ALU.add)
                step(dve.scalar_tensor_tensor(s18[:, :, :], eid[:, :, :], float(RANKS), rk[:, :, :], ALU.mult, ALU.add))
                v2 = bc(valid[:, :].unsqueeze(1), [P, 2, T])
                tt(s18[:, :, :], s18[:, :, :], v2, ALU.mult)
                tt(s18[:, :, :], s18[:, :, :], dump[:, :, :], ALU.add)
                tt(item[:, :, :], dump[:, :, :], v2, ALU.mult)
                tt(s18[:, :, :], s18[:, :, :], item[:, :, :], ALU.subtract)
                step(dve.tensor_copy(scatter_i[:, :, :], s18[:, :, :]))
                dve.sem_inc(rows_ready, 1)
                total = base[:, T, :]
                ts(over[:, :], total, float(P), 1.0, ALU.is_gt, ALU.add)
                for m in range(2, MAX_BLOCKS):
                    step(dve.scalar_tensor_tensor(over[:, :], total, float(m * P), over[:, :], ALU.is_gt, ALU.add))
                src, dst, d = over, cum, 1
                while d < E:
                    tt(dst[:, d:], src[:, d:], src[:, 0:E - d], ALU.add)
                    step(dve.tensor_copy(dst[:, 0:d], src[:, 0:d]))
                    src, dst, d = dst, (cum2 if dst is cum else cum), 2 * d
                incl = src
                step(dve.tensor_copy(S.n_items[:, 0:1], incl[:, E - 1:E]))
                ts(n1[:, :], incl[:, E - 1:E], -1.0, None, ALU.add)
                step(dve.tensor_copy(S.n_items[:, 1:2], n1[:, :]))
                shape = [P, ITEMS + 1, E]
                tt(ended[:, :, :], bc(incl[:, :].unsqueeze(1), shape), bc(number[:, :].unsqueeze(2), shape), ALU.is_le)
                red(owner[:, :], ended[:, :, :], ALU.add)
                step(dve.tensor_copy(S.item_expert[:, :], owner[:, :]))
                tt(ended_at[:, :, :], ended[:, :, :], bc(incl[:, :].unsqueeze(1), shape), ALU.mult)
                red(row[:, :], ended_at[:, :, :], ALU.max)
                tt(row[:, :], number[:, :], row[:, :], ALU.subtract)
                ts(row[:, :], row[:, :], float(P), None, ALU.mult)
                step(dve.scalar_tensor_tensor(row[:, :], owner[:, :], float(RANKS), row[:, :], ALU.mult, ALU.add))
                ts(row[:, :], row[:, :], float(E * RANKS - P), None, ALU.min)
                step(dve.tensor_copy(S.item_row[:, :], row[:, :]))
                tt(over[:, :], incl[:, :], over[:, :], ALU.subtract)
                for k in range(2):
                    tt(t32[:, :, :], oh[k][:, :, :], bc(over[:, :].unsqueeze(1), [P, T, E]), ALU.mult)
                    red(osk[:, k, :], t32[:, :, :], ALU.add)
                step(dve.scalar_tensor_tensor(s18[:, :, :], osk[:, :, :], float(P), rk[:, :, :], ALU.mult, ALU.add))
                tt(s18[:, :, :], s18[:, :, :], v2, ALU.mult)
                tt(item[:, :, :], first_row[:, :, :], v2, ALU.mult)
                tt(item[:, :, :], first_row[:, :, :], item[:, :, :], ALU.subtract)
                tt(s18[:, :, :], s18[:, :, :], item[:, :, :], ALU.add)
                step(dve.tensor_copy(S.out_row[:, :, :], s18[:, :, :]))


def experts(nc, S, ple_gate, ple_proj):
    with ExitStack() as ctx:
        sb = lambda n, s, d=F32: ctx.enter_context(nc.sbuf_tensor(n, s, d))
        sem = lambda n: S.stack.enter_context(nc.semaphore(n))
        w_hi, w_lo, w_split, w_used = S.w_hi, S.w_lo, S.w_split, S.w_used
        next_ids, ids = sb("next_token_ids", [P, 1], I32), sb("token_ids", [P, 1], I32)
        x = sb("x_tokens", [P, D])
        x_hi, x_lo = sb("xt_hi", [P, KD, P], F32R), sb("xt_lo", [P, KD, P], F32R)
        act_g, hid = sb("act_gate", [P, D_EXP]), sb("hidden", [P, D_EXP])
        h_hi, h_lo = sb("ht_hi", [P, KE, P], F32R), sb("ht_lo", [P, KE, P], F32R)
        y = sb("y_tile", [P, D])
        psum = lambda n, s: ctx.enter_context(nc.psum_tensor(n, s, F32))
        ps_x, ps_g, ps_u, ps_h, ps_y = (psum("ps_x", [P, KD, P]), psum("ps_g", [P, D_EXP]), psum("ps_u", [P, D_EXP]),
                                        psum("ps_h", [P, KE, P]), psum("ps_y", [P, D]))
        ids_loaded, x_gathered, x_turned, xh_ready, xl_ready = (sem(n) for n in (
            "ids_loaded", "x_gathered", "x_turned", "xh_ready", "xl_ready"))
        silu_ready, hid_ready, hid_turned, hh_ready, hl_ready = (sem(n) for n in (
            "silu_ready", "hid_ready", "hid_turned", "hh_ready", "hl_ready"))
        y_left, y_stored, ids_ready = sem("y_left"), sem("y_stored"), sem("ids_ready")
        number = lambda eng: eng.value_load(S.n_items[0:1, 0:1], min_val=EXPERTS, max_val=ITEMS)
        final_of = lambda eng: eng.value_load(S.n_items[0:1, 1:2], min_val=EXPERTS - 1, max_val=ITEMS - 1)
        expert_of = lambda eng, i: eng.value_load(S.item_expert[0:1, bass.ds(i, 1)], min_val=0, max_val=EXPERTS - 1)
        kgu = PIECE // D_EXP
        kdn = PIECE // D
        with nc.Block() as block:

            @block.sync
            def _(sp):
                with sp.Fori(1, EXPERTS - 1) as e:
                    for s in GATE + UP:
                        load_piece(sp, S, s, e + 1, expert_piece(S, s, bass.ds(e + 1, 1)))
                    for s in DOWN:
                        load_piece(sp, S, s, e, expert_piece(S, s, bass.ds(e, 1)))
                for s in DOWN:
                    load_piece(sp, S, s, EXPERTS - 1, expert_piece(S, s, slice(EXPERTS - 1, EXPERTS)))
                for s in range(5):
                    w, k = (ple_gate, 2 * s) if s < 4 else (ple_proj, 0)
                    sp.wait_ge(w_split[s], EXPERTS + 1)
                    sp.dma_start(S.w_raw[s].rearrange("p (k n) -> p k n", n=D), w[:, k:k + 2, :]).then_inc(S.raw_loaded[s], 16)
                sp.wait_ge(S.raw_loaded[4], (EXPERTS + 1) * 16)

            @block.gpsimd
            def _(pool):
                n_items = number(pool)

                def fetch(i):
                    row = pool.value_load(S.item_row[0:1, bass.ds(i, 1)], min_val=0, max_val=EXPERTS * RANKS - P)
                    pool.dma_start(next_ids[:, :], S.table[bass.ds(row, P), :]).then_inc(ids_loaded, 16)

                def gather(i):
                    pool.wait_ge(ids_loaded, i * 16 + 16)
                    pool.sem_inc(S.waits_met, 1)
                    pool.tensor_copy(ids[:, :], next_ids[:, :]).then_inc(ids_ready, 1)
                    pool.wait_ge(ids_ready, i + 1)
                    pool.sem_inc(S.waits_met, 1)
                    pool.indirect_dma_start(out=x[:, :], out_offset=None, in_=S.h2_rows[:, :],
                                            in_offset=bass.IndirectOffsetOnAxis(ap=ids[:, :], axis=0)).then_inc(x_gathered, 16)

                fetch(0)
                gather(0)
                fetch(1)
                with pool.Fori(1, n_items) as i:
                    pool.wait_ge(x_gathered, i * 16)
                    pool.wait_ge(x_turned, i)
                    gather(i)
                    fetch(i + 1)
                    e, last = expert_of(pool, i), expert_of(pool, i - 1)
                    with pool.If(e != last):
                        piece_lo(pool, S, e, 3)
                pool.wait_ge(ids_loaded, n_items * 16 + 16)
                pool.sem_inc(S.waits_met, 1)
                piece_lo(pool, S, EXPERTS, 3)

            @block.scalar
            def _(act):
                end = final_of(act)

                def take_hi(now, before, slots, items):
                    with act.If(now != before):
                        for s in slots:
                            piece_hi(act, S, now, s, items)

                def x_to_hi(i):
                    act.wait_ge(x_turned, i + 1)
                    act.activation(x_hi[:, :, :], ps_x[:, :, :], ACT.Copy).then_inc(xh_ready, 1)

                def leave_y(i):
                    act.wait_ge(w_used[5], i + 1)
                    act.wait_ge(y_stored, i * 16 + 16)
                    act.activation(y[:, :], ps_y[:, :], ACT.Copy).then_inc(y_left, 1)
                    act.wait_ge(y_left, i + 2)
                    act.dma_start(S.y_rows[bass.ds(i * P, P), :], y[:, :]).then_inc(y_stored, 16)

                def iteration(i, first=False, final=False):
                    act.wait_ge(w_used[1], i + 1)
                    act.activation(act_g[:, :], ps_g[:, :], ACT.Silu).then_inc(silu_ready, 1)
                    e = 0 if first else expert_of(act, i)
                    if final:
                        for s in GATE + UP:
                            piece_hi(act, S, EXPERTS, s, i + 1)
                    else:
                        take_hi(expert_of(act, i + 1), e, GATE + UP, i + 1)
                        x_to_hi(i + 1)
                    if first:
                        for s in DOWN:
                            piece_hi(act, S, 0, s, None)
                    else:
                        take_hi(e, expert_of(act, i - 1), DOWN, i)
                        leave_y(i - 1)
                    act.wait_ge(hid_turned, i + 1)
                    act.activation(h_hi[:, :, :], ps_h[:, :, :], ACT.Copy).then_inc(hh_ready, 1)

                act.sem_inc(y_left, 1)
                act.sem_inc(y_stored, 16)
                x_to_hi(0)
                iteration(0, first=True)
                with act.Fori(1, end) as i:
                    iteration(i)
                iteration(end, final=True)
                leave_y(end)
                act.wait_ge(y_stored, end * 16 + 32)
                act.sem_inc(S.waits_met, 1)

            @block.vector
            def _(dve):
                end = final_of(dve)

                def take_lo(now, before, slots):
                    with dve.If(now != before):
                        for s in slots:
                            piece_lo(dve, S, now, s)

                def x_to_lo(i):
                    dve.wait_ge(xh_ready, i + 1)
                    dve.tensor_tensor(x_lo[:, :, :], ps_x[:, :, :], x_hi[:, :, :].bitcast(F32), ALU.subtract)\
                       .then_inc(xl_ready, 1)

                def iteration(i, first=False, final=False):
                    e = 0 if first else expert_of(dve, i)
                    if final:
                        for s in (0, 1, 2):
                            piece_lo(dve, S, EXPERTS, s)
                    else:
                        take_lo(expert_of(dve, i + 1), e, (0, 1, 2))
                    dve.wait_ge(silu_ready, i + 1)
                    dve.wait_ge(w_used[3], i + 1)
                    dve.tensor_tensor(hid[:, :], ps_u[:, :], act_g[:, :], ALU.mult).then_inc(hid_ready, 1)
                    if not final:
                        x_to_lo(i + 1)
                    if first:
                        for s in DOWN:
                            piece_lo(dve, S, 0, s)
                    else:
                        take_lo(e, expert_of(dve, i - 1), DOWN)
                    dve.wait_ge(hh_ready, i + 1)
                    dve.tensor_tensor(h_lo[:, :, :], ps_h[:, :, :], h_hi[:, :, :].bitcast(F32), ALU.subtract)\
                       .then_inc(hl_ready, 1)

                x_to_lo(0)
                iteration(0, first=True)
                with dve.Fori(1, end) as i:
                    iteration(i)
                iteration(end, final=True)

            @block.tensor
            def _(pe):
                end = final_of(pe)

                def turn_x(i):
                    pe.wait_ge(x_gathered, i * 16 + 16)
                    for k in range(KD):
                        last = pe.transpose(ps_x[:, k, :], x[:, k * P:(k + 1) * P], S.ident[:, :])
                    last.then_inc(x_turned, 1)

                def gate_up(i, e):
                    pe.wait_ge(xl_ready, i + 1)
                    for slots, ps in ((GATE, ps_g), (UP, ps_u)):
                        for s in slots:
                            pe.wait_ge(w_split[s], e + 2)
                            for j in range(kgu):
                                k = (s % 2) * kgu + j
                                cols = slice(j * D_EXP, (j + 1) * D_EXP)
                                last = matmul3(pe, ps[:, :], x_hi[:, k, :], x_lo[:, k, :], w_hi[s][:, cols],
                                               w_lo[s][:, cols], k == 0, k == KD - 1)
                            last.then_inc(w_used[s], 1)

                def down(i, e):
                    pe.wait_ge(hl_ready, i + 1)
                    pe.wait_ge(y_left, i + 1)
                    for s in DOWN:
                        pe.wait_ge(w_split[s], e + 2)
                        for j in range(kdn):
                            k = (s % 2) * kdn + j
                            for h in range(2):
                                cols = slice(j * D + h * 512, j * D + (h + 1) * 512)
                                last = matmul3(pe, ps_y[:, h * 512:(h + 1) * 512], h_hi[:, k, :], h_lo[:, k, :],
                                               w_hi[s][:, cols], w_lo[s][:, cols], k == 0, k == KE - 1)
                        last.then_inc(w_used[s], 1)

                def turn_hid(i):
                    pe.wait_ge(hid_ready, i + 1)
                    for k in range(KE):
                        last = pe.transpose(ps_h[:, k, :], hid[:, k * P:(k + 1) * P], S.ident[:, :])
                    last.then_inc(hid_turned, 1)

                turn_x(0)
                gate_up(0, 0)
                turn_x(1)
                turn_hid(0)
                with pe.Fori(1, end) as i:
                    gate_up(i, expert_of(pe, i))
                    turn_x(i + 1)
                    down(i - 1, expert_of(pe, i - 1))
                    turn_hid(i)
                gate_up(end, EXPERTS - 1)
                down(end - 1, expert_of(pe, end - 1))
                turn_hid(end)
                down(end, EXPERTS - 1)


def embedding_gate(nc, S, p_prompt, p_sample, g_ple, b_ple_gate, g_final, y_prompt, y_sample):
    KP = PLE // P
    HALF = KD // 2
    with ExitStack() as ctx:
        sb = lambda n, s, d=F32: ctx.enter_context(nc.sbuf_tensor(n, s, d))
        sem = lambda n: S.stack.enter_context(nc.semaphore(n))
        room = [S.w_raw[s][:, h * D:(h + 1) * D] for s in (0, 1, 2, 3, 5) for h in range(2)]
        x2, y1, y2, x3, x3b, h3, sgm, x4, out, b_rows = room
        junk1, junk2, g_rows, f_rows = (sb(n, [P, D]) for n in ("junk61", "junk62", "g_ple_rows", "g_final_rows"))
        p_in = sb("p_in", [P, PLE])
        h_hi, h_lo = sb("h3t_hi", [P, KD, P], F32R), sb("h3t_lo", [P, KD, P], F32R)
        p_hi, p_lo = sb("pt_hi", [P, KP, P], F32R), sb("pt_lo", [P, KP, P], F32R)
        rows = sb("gather_rows", [P, 2], I32)
        gate = sb("gate_cols", [P, 2])
        ss, ms, rstd = sb("ss6", [P, 2]), sb("ms6", [P, 2]), sb("rstd6", [P, 2])
        psum = lambda n, s: ctx.enter_context(nc.psum_tensor(n, s, F32))
        ps_g, ps_p, ps_h, ps_pt = psum("ps_gate", [P, D]), psum("ps_proj", [P, D]), psum("ps_h3t", [P, KD, P]), psum("ps_pt", [P, KP, P])
        rows_loaded, proj_hi_ready, proj_ready = sem("rows_loaded"), sem("proj_hi_ready"), sem("proj_ready")
        x2_loaded, p_loaded, y1_in, y2_in, picked = (sem(n) for n in ("x2_in_loaded", "p_loaded", "y1_gathered", "y2_gathered", "picked"))
        x3_part, x3_ready, x3_kept, h3_ready, turned, p_turned = (sem(n) for n in (
            "x3_part", "x3_ready", "x3_kept_ready", "h3_ready", "h3_turned", "p_turned"))
        hi_ready, lo_ready, p_hi_ready, p_lo_ready = (sem(n) for n in ("h3_hi", "h3_lo", "p_hi_ready", "p_lo_ready"))
        squared, mean_ready, rstd_ready = ([sem(f"{n}{i}") for i in range(2)] for n in ("sq6_", "ms6_", "rstd6_"))
        gates, biased, sig_ready, projected, scaled = (sem(n) for n in ("gates_ready", "biased", "sig6_ready", "projected", "scaled6"))
        x4_ready, out_ready, out_stored = sem("x4_ready"), sem("out_ready"), sem("out_stored")

        def weights(halves, k, half):
            return halves[k // 2][:, (k % 2) * D + half.start:(k % 2) * D + half.stop]

        with nc.Block() as block:

            @block.sync
            def _(sp):
                def loads(t, p_src, rows_of):
                    sp.wait_ge(x3_part, t)
                    sp.dma_start(x2[:, :], S.x2_rows[bass.ds(t * P, P), :]).then_inc(x2_loaded, 16)
                    sp.wait_ge(p_turned, t)
                    sp.dma_start(p_in[rows_of, :], p_src).then_inc(p_loaded, 16)

                def store(t, dst, rows_of):
                    sp.wait_ge(out_ready, t + 1)
                    sp.dma_start(dst, out[rows_of, :]).then_inc(out_stored, 16)

                whole, sample = slice(0, P), slice(GAP, GAP + DEC)
                sp.sem_inc(out_stored, 16)
                sp.dma_start(x2[:, :], S.x2_rows[0:P, :]).then_inc(x2_loaded, 16)
                sp.dma_start(p_in[:, :], p_prompt[0, 0, 0:P, :]).then_inc(p_loaded, 16)
                loads(1, p_prompt[0, 0, P:2 * P, :], whole)
                with sp.Fori(0, TILES - 3) as t:
                    loads(t + 2, p_prompt[0, 0, bass.ds(t * P + 2 * P, P), :], whole)
                    store(t, y_prompt[0, bass.ds(t * P, P), :], whole)
                loads(TILES - 1, p_sample[0, 0], sample)
                for t in (TILES - 3, TILES - 2):
                    store(t, y_prompt[0, t * P:(t + 1) * P, :], whole)
                store(TILES - 1, y_sample[0], sample)
                sp.wait_ge(out_stored, 16 * (TILES + 1))

            @block.gpsimd
            def _(pool):
                def fetch(t):
                    pool.tensor_copy(rows[:, :], S.out_row[:, :, bass.ds(t, 1)])
                    pool.tensor_copy(gate[:, :], S.gate[:, :, bass.ds(t, 1)]).then_inc(picked, 1)
                    pool.wait_ge(picked, t + 1)
                    pool.sem_inc(S.waits_met, 1)
                    for k, (dst, got) in enumerate(((y1, y1_in), (y2, y2_in))):
                        pool.indirect_dma_start(out=dst[:, :], out_offset=None, in_=S.y_rows[:, :],
                                                in_offset=bass.IndirectOffsetOnAxis(ap=rows[:, k:k + 1], axis=0)).then_inc(got, 16)

                def norm1(t):
                    pool.wait_ge(mean_ready[0], t + 1)
                    pool.tensor_tensor(rstd[:, 0:1], ms[:, 0:1], S.minus_half[:, 0:1], ALU.pow).then_inc(rstd_ready[0], 1)

                def keep(t):
                    pool.wait_ge(x4_ready, t + 1)
                    pool.wait_ge(x3_ready, t + 1)
                    pool.sem_inc(S.waits_met, 1)
                    pool.tensor_copy(x3b[:, :], x3[:, :]).then_inc(x3_kept, 1)

                def norm2(t):
                    pool.wait_ge(mean_ready[1], t + 1)
                    pool.tensor_tensor(rstd[:, 1:2], ms[:, 1:2], S.minus_half[:, 0:1], ALU.pow).then_inc(rstd_ready[1], 1)

                def refetch(t):
                    pool.wait_ge(y1_in, t * 16)
                    pool.wait_ge(y2_in, t * 16)
                    pool.wait_ge(x3_ready, t)
                    pool.sem_inc(S.waits_met, 1)
                    fetch(t)

                fetch(0)
                norm1(0)
                refetch(1)
                keep(0)
                with pool.Fori(0, TILES - 2) as t:
                    norm1(t + 1)
                    refetch(t + 2)
                    norm2(t)
                    keep(t + 1)
                norm1(TILES - 1)
                norm2(TILES - 2)
                keep(TILES - 1)
                norm2(TILES - 1)

            @block.scalar
            def _(act):
                for dst, src in ((g_rows, g_ple[0]), (b_rows, b_ple_gate[0]), (f_rows, g_final)):
                    act.dma_start(dst[:, :], src.partition_broadcast(P)).then_inc(rows_loaded, 16)

                def square(t, j):
                    if type(t) is not int or t > 0:
                        act.wait_ge(squared[j], t)
                    act.wait_ge((x3_ready, x4_ready)[j], t + 1 + j)
                    act.activation((junk1, junk2)[j][:, :], (x3, x4)[j][:, :], ACT.Square, accum_out=ss[:, j:j + 1])\
                       .then_inc(squared[j], 1)

                def to_hi(t):
                    act.wait_ge(turned, t + 1)
                    act.activation(h_hi[:, :, :], ps_h[:, :, :], ACT.Copy).then_inc(hi_ready, 1)
                    act.wait_ge(p_turned, t + 1)
                    if type(t) is not int or t > 0:
                        act.wait_ge(projected, t)
                    act.activation(p_hi[:, :, :], ps_pt[:, :, :], ACT.Copy).then_inc(p_hi_ready, 1)

                def sigmoid(t):
                    act.wait_ge(biased, t + 1)
                    act.activation(sgm[:, :], sgm[:, :], ACT.Sigmoid).then_inc(sig_ready, 1)

                act.activation(S.w_hi[4][:, :], S.w_raw[4], ACT.Copy).then_inc(proj_hi_ready, 1)
                square(0, 0)
                to_hi(0)
                def iteration(t):
                    square(t + 1, 0)
                    sigmoid(t)
                    to_hi(t + 1)
                    square(t, 1)

                iteration(0)
                with act.Fori(1, TILES - 1) as t:
                    iteration(t)
                sigmoid(TILES - 1)
                square(TILES - 1, 1)

            @block.vector
            def _(dve):
                def combine(t):
                    dve.wait_ge(picked, t + 1)
                    dve.wait_ge(x2_loaded, t * 16 + 16)
                    dve.wait_ge(y1_in, t * 16 + 16)
                    if type(t) is not int or t > 0:
                        dve.wait_ge(x3_kept, t)
                    dve.scalar_tensor_tensor(x3[:, :], y1[:, :], gate[:, 0:1], x2[:, :], ALU.mult, ALU.add).then_inc(x3_part, 1)
                    dve.wait_ge(y2_in, t * 16 + 16)
                    dve.wait_ge(x3_part, t + 1)
                    dve.scalar_tensor_tensor(x3[:, :], y2[:, :], gate[:, 1:2], x3[:, :], ALU.mult, ALU.add).then_inc(x3_ready, 1)

                def mean(t, j):
                    dve.wait_ge(squared[j], t + 1)
                    dve.tensor_scalar(ms[:, j:j + 1], ss[:, j:j + 1], 1.0 / D, EPS, ALU.mult, ALU.add).then_inc(mean_ready[j], 1)
                    dve.wait_ge(rstd_ready[j], t + 1)

                def norm(t):
                    mean(t, 0)
                    dve.scalar_tensor_tensor(h3[:, :], x3[:, :], rstd[:, 0:1], g_rows[:, :], ALU.mult, ALU.mult)\
                       .then_inc(h3_ready, 1)

                def to_lo(t):
                    dve.wait_ge(hi_ready, t + 1)
                    dve.tensor_tensor(h_lo[:, :, :], ps_h[:, :, :], h_hi[:, :, :].bitcast(F32), ALU.subtract).then_inc(lo_ready, 1)

                def p_to_lo(t):
                    dve.wait_ge(p_hi_ready, t + 1)
                    dve.tensor_tensor(p_lo[:, :, :], ps_pt[:, :, :], p_hi[:, :, :].bitcast(F32), ALU.subtract).then_inc(p_lo_ready, 1)

                def bias(t):
                    dve.wait_ge(gates, t + 1)
                    dve.tensor_tensor(sgm[:, :], ps_g[:, :], b_rows[:, :], ALU.add).then_inc(biased, 1)

                def finish(t):
                    dve.wait_ge(sig_ready, t + 1)
                    dve.wait_ge(projected, t + 1)
                    dve.tensor_tensor(x4[:, :], ps_p[:, :], sgm[:, :], ALU.mult).then_inc(scaled, 1)
                    dve.wait_ge(scaled, t + 1)
                    dve.wait_ge(x3_kept, t + 1)
                    dve.tensor_tensor(x4[:, :], x4[:, :], x3b[:, :], ALU.add).then_inc(x4_ready, 1)

                def final(t):
                    mean(t, 1)
                    dve.wait_ge(out_stored, t * 16 + 16)
                    dve.scalar_tensor_tensor(out[:, :], x4[:, :], rstd[:, 1:2], f_rows[:, :], ALU.mult, ALU.mult)\
                       .then_inc(out_ready, 1)

                dve.sem_inc(x4_ready, 1)
                combine(0)
                dve.wait_ge(rows_loaded, 48)
                norm(0)
                to_lo(0)
                dve.wait_ge(proj_hi_ready, 1)
                dve.tensor_tensor(S.w_lo[4][:, :], S.w_raw[4], S.w_hi[4][:, :].bitcast(F32), ALU.subtract)\
                   .then_inc(proj_ready, 1)
                p_to_lo(0)
                with dve.Fori(0, TILES - 1) as t:
                    combine(t + 1)
                    norm(t + 1)
                    bias(t)
                    to_lo(t + 1)
                    finish(t)
                    p_to_lo(t + 1)
                    final(t)
                bias(TILES - 1)
                finish(TILES - 1)
                final(TILES - 1)

            @block.tensor
            def _(pe):
                def turn(t):
                    pe.wait_ge(h3_ready, t + 1)
                    for k in range(KD):
                        last = pe.transpose(ps_h[:, k, :], h3[:, k * P:(k + 1) * P], S.ident[:, :])
                    last.then_inc(turned, 1)
                    pe.wait_ge(p_loaded, t * 16 + 16)
                    for k in range(KP):
                        last = pe.transpose(ps_pt[:, k, :], p_in[:, k * P:(k + 1) * P], S.ident[:, :])
                    last.then_inc(p_turned, 1)

                def gate_products(t):
                    pe.wait_ge(lo_ready, t + 1)
                    for k in range(KD):
                        for h in range(2):
                            half = slice(h * 512, (h + 1) * 512)
                            last = matmul3(pe, ps_g[:, half], h_hi[:, k, :], h_lo[:, k, :],
                                           weights(S.w_hi, k, half), weights(S.w_lo, k, half), k == 0, k == KD - 1)
                    last.then_inc(gates, 1)

                def proj_products(t):
                    pe.wait_ge(p_lo_ready, t + 1)
                    for k in range(KP):
                        for h in range(2):
                            half = slice(h * 512, (h + 1) * 512)
                            last = matmul3(pe, ps_p[:, half], p_hi[:, k, :], p_lo[:, k, :],
                                           weights(S.w_hi, KD + k, half), weights(S.w_lo, KD + k, half), k == 0, k == KP - 1)
                    last.then_inc(projected, 1)

                turn(0)
                pe.wait_ge(proj_ready, 1)
                with pe.Fori(0, TILES - 1) as t:
                    gate_products(t)
                    turn(t + 1)
                    proj_products(t)
                gate_products(TILES - 1)
                proj_products(TILES - 1)


def build(nc, i, o):
    S = Shared()
    S.x2_rows = nc.dram_tensor("x2_rows", [ROWS, D], F32).ap()
    S.h2_rows = nc.dram_tensor("h2_rows", [ROWS, D], F32).ap()
    S.y_rows = nc.dram_tensor("y_rows", [ITEMS * P, D], F32).ap()
    S.table = nc.dram_tensor("token_table", [TABLE, 1], I32).ap()
    S.conv_p, S.pool_p, S.conv_s, S.pool_s = o["conv_p"], o["pool_p"], o["conv_s"], o["pool_s"]
    with ExitStack() as whole:
        S.stack = whole
        sb = lambda n, s, d=F32, at=whole: at.enter_context(nc.sbuf_tensor(n, s, d))
        S.ident, S.ones, S.minus_half = sb("ident", [P, P]), sb("ones", [P, P]), sb("minus_half", [P, 4])
        S.zero = sb("zero_rows", [P, P])
        S.gate, S.out_row = sb("gates", [P, 2, TILES]), sb("out_rows", [P, 2, TILES], I32)
        S.n_items, S.item_expert, S.item_row = sb("n_items", [P, 2], I32), sb("item_expert", [P, ITEMS + 1], I32), sb("item_row", [P, ITEMS + 1], I32)
        S.mix_w_loaded = whole.enter_context(nc.semaphore("mix_w_loaded"))
        S.waits_met = whole.enter_context(nc.semaphore("waits_met"))
        S.routed = whole.enter_context(nc.semaphore("routed"))
        S.raw_loaded, S.w_hi_ready, S.w_split, S.w_used = (
            [whole.enter_context(nc.semaphore(f"{n}{s}")) for s in range(6)] for n in
            ("raw_loaded", "w_hi_ready", "w_split", "w_used"))
        S.w_experts = (i["w_exp_gate"], i["w_exp_up"], i["w_exp_down"])
        S.par = sb("par", [P, KC, P_ALL])
        region = sb("mixer_or_raw_weights", [P, 6 * PIECE])
        at = [0]

        def part(width, *shape):
            flat = region[:, at[0]:at[0] + width * shape[0]]
            at[0] += width * shape[0]
            return flat.rearrange("p (k n) -> p k n", n=width)

        S.conv, S.pooled = part(COLS, KC), part(COLS, KC)
        S.w_pw, S.w_pool = part(CH, KC), part(P, KC)
        assert at[0] <= 6 * PIECE
        S.w_raw = [region[:, s * PIECE:(s + 1) * PIECE] for s in range(6)]
        with ExitStack() as hs:
            S.h_hi, S.h_lo = sb("h_hi", [P, KD, ROWS], F32R, hs), sb("h_lo", [P, KD, ROWS], F32R, hs)
            constants_and_norm(nc, S, i["x_prompt"], i["x_sample"], i["state_conv"], i["state_pool"], i["g_mix"],
                               i["w_dw"], i["b_dw"], i["g_conv_ln"], i["b_conv_ln"], i["b_pw"], i["pool_scale"])
            in_projection_conv_pool(nc, S, i["w_in"], i["w_pw"], i["w_pool"])
        with ExitStack() as routed:
            with ExitStack() as back:
                S.o = sb("o_channels", [P, KD, ROWS], F32, back)
                S.wo_hi, S.wo_lo = sb("w_out_hi", [P, KD, D], F32R, back), sb("w_out_lo", [P, KD, D], F32R, back)
                mixer_outputs(nc, S, i["w_out"])
                S.ps_route = routed.enter_context(nc.psum_tensor("ps_route", [P, TILES, GROUPS + EXPERTS], F32))
                out_projection(nc, S, i["x_prompt"], i["x_sample"], i["g_ffn"], i["w_route_group"], i["w_route_expert"])
            S.w_hi = [sb(f"w_hi{s}", [P, PIECE], F32R) for s in range(6)]
            S.w_lo = [sb(f"w_lo{s}", [P, PIECE], F32R) for s in range(6)]
            routing(nc, S, i["b_route_group"], i["b_route_expert"])
        blocks = lambda w: w[0].rearrange("(k p) n -> p k n", p=P)
        experts(nc, S, blocks(i["w_ple_gate"]), blocks(i["w_ple_proj"]))
        embedding_gate(nc, S, i["p_prompt"], i["p_sample"], i["g_ple"], i["b_ple_gate"], i["g_final"],
                       o["y_prompt"], o["y_sample"])


_OUTS = {
    "y_prompt": (1, SEQ, D), "y_sample": (1, DEC, D), "conv_p": (1, 1, CONV_HIST, CH), "pool_p": (1, 1, POOL_HIST, CH),
    "conv_s": (1, 1, CONV_HIST, CH), "pool_s": (1, 1, POOL_HIST, CH),
}


def kernel(**inputs):
    import numpy as np
    import concourse.bacc as bacc
    from concourse.bass_utils import run_bass_kernel_spmd

    nc = bacc.Bacc("TRN2", target_bir_lowering=False, num_devices=1)
    arrays = {n: np.ascontiguousarray(a) for n, a in inputs.items()}
    ins = {n: nc.dram_tensor(n, a.shape, mybir.dt.from_np(a.dtype), kind="ExternalInput").ap() for n, a in arrays.items()}
    outs = {n: nc.dram_tensor(n, s, F32, kind="ExternalOutput").ap() for n, s in _OUTS.items()}
    build(nc, ins, outs)
    r = run_bass_kernel_spmd(nc, [arrays], core_ids=[0])
    return tuple(r.results[0][n] for n in _OUTS)
```

```python
from contextlib import ExitStack

import concourse.bass as bass
from concourse import mybir

F32, F32R = mybir.dt.float32, mybir.dt.float32r
BF16, I32 = mybir.dt.bfloat16, mybir.dt.int32
ACT, ALU, AX = mybir.ActivationFunctionType, mybir.AluOpType, mybir.AxisListType

P = 128
D, SEQ, DEC, CH = 1024, 1024, 32, 512
PLE, TAPS, POOL_HIST, POOL_GROUPS = 256, 31, 15, 4
POOL_TAPS = 6
CONV_HIST = TAPS - 1
GROUPS, PER_GROUP, D_EXP = 4, 8, 512
EXPERTS = GROUPS * PER_GROUP
EPS = 1e-6

KD = D // P
KE = D_EXP // P
KC = CH // P
GAP = 32
SAMPLE = SEQ + GAP
TILES = (SAMPLE + DEC + P - 1) // P
ROWS = TILES * P
CHUNKS = 3
CHUNK = 364
COLS = CHUNKS * CHUNK
assert COLS >= SAMPLE + DEC and CHUNK <= 512 and GAP >= CONV_HIST

P_BDW, P_GLN, P_BLN, P_BPW, P_SCALE = TAPS, TAPS + 1, TAPS + 2, TAPS + 3, TAPS + 4
P_CHIST = TAPS + 5
P_PHIST = P_CHIST + CONV_HIST
P_ALL = P_PHIST + POOL_HIST

MAX_BLOCKS = (SEQ + DEC + P - 1) // P
MAX_EXTRA = 2 * (SEQ + DEC) // P
ITEMS = EXPERTS + MAX_EXTRA
PIECE = 2048


def matmul3(pe, out, x_hi, x_lo, w_hi, w_lo, start, stop):
    pe.matmul(out, x_hi, w_hi, start=start, stop=False)
    pe.matmul(out, x_hi, w_lo, start=False, stop=False)
    return pe.matmul(out, x_lo, w_hi, start=False, stop=stop)


GATE, UP, DOWN = (0, 1), (2, 3), (4, 5)


def load_piece(eng, S, s, n, src):
    cols = D if s in DOWN else D_EXP
    eng.wait_ge(S.w_split[s], n + 1)
    eng.dma_start(S.w_raw[s].rearrange("p (k n) -> p k n", n=cols), src).then_inc(S.raw_loaded[s], 16)


def expert_piece(S, s, e):
    w = S.w_experts[s // 2]
    half = w.shape[2] // 2
    rows = slice((s % 2) * half, (s % 2 + 1) * half)
    return w[0, e, rows, :].rearrange("o (k p) n -> p (o k) n", p=P)


def piece_hi(act, S, n, s, items):
    act.wait_ge(S.raw_loaded[s], n * 16 + 16)
    if items is not None:
        act.wait_ge(S.w_used[s], items)
    act.activation(S.w_hi[s][:, :], S.w_raw[s], ACT.Copy).then_inc(S.w_hi_ready[s], 1)


def piece_lo(eng, S, n, s):
    eng.wait_ge(S.w_hi_ready[s], n + 1)
    eng.tensor_tensor(S.w_lo[s][:, :], S.w_raw[s], S.w_hi[s][:, :].bitcast(F32), ALU.subtract)\
       .then_inc(S.w_split[s], 1)


def gather_tokens(pool, S, i):
    pool.tensor_copy(S.ids[:, :], S.item_tokens[:, bass.ds(i, 1)]).then_inc(S.ids_ready, 1)
    pool.wait_ge(S.ids_ready, i + 1)
    pool.sem_inc(S.waits_met, 1)
    pool.indirect_dma_start(out=S.x_tokens[:, :], out_offset=None, in_=S.h2_rows[:, :],
                            in_offset=bass.IndirectOffsetOnAxis(ap=S.ids[:, :], axis=0)).then_inc(S.x_gathered, 16)


class Shared:
    pass


PARTS = 3


def load_w_in(sp, S, c, s):
    sp.dma_start(S.w_in_raw[s][:, :, :], S.w_in[:, :, bass.ds(c * P + s * CH, P)]).then_inc(S.w_in_loaded[s], 16)


def constants_and_norm(nc, S, x_prompt, x_sample, state_conv, state_pool, g_mix, w_dw, b_dw,
                       g_conv_ln, b_conv_ln, b_pw, pool_scale):
    BATCH, DEEP = 3, 6
    BATCHES = TILES // BATCH
    with ExitStack() as ctx:
        sb = lambda n, s, d=F32: ctx.enter_context(nc.sbuf_tensor(n, s, d))
        sem = lambda n: S.stack.enter_context(nc.semaphore(n))
        x, xn = S.room[0:DEEP], S.room[DEEP:2 * DEEP]
        gain = sb("g_mix_rows", [P, D])
        ss, ms, rstd = sb("ss1", [P, TILES]), sb("ms1", [P, TILES]), sb("rstd1", [P, TILES])
        rows = sb("param_rows", [P_ALL, CH])
        ps_t = [ctx.enter_context(nc.psum_tensor(f"ps_t{j}", [P, KD, P], F32)) for j in range(BATCH)]
        ps_par = ctx.enter_context(nc.psum_tensor("ps_par", [P, KC, P_ALL], F32))
        x_loaded = [sem(f"x_loaded{j}") for j in range(BATCH)]
        par_loaded, gain_loaded = sem("par_loaded"), sem("gain_loaded")
        const_set = sem("const_set")
        squared, mean_ready, rstd_ready = sem("squared"), sem("mean_ready"), sem("rstd_ready")
        norm_ready, turned, hi_ready, lo_ready = sem("norm_ready"), sem("turned"), sem("h_hi_ready"), sem("h_lo_ready")
        par_turned, par_ready = sem("par_turned"), sem("par_ready")
        of_batch = lambda b: slice(b * BATCH, (b + 1) * BATCH)
        tiles = lambda b: range(b * BATCH, (b + 1) * BATCH)
        with nc.Block() as block:

            @block.sync
            def _(sp):
                for t in range(TILES):
                    if t == BATCH:
                        sp.dma_start(gain[:, :], g_mix[0].partition_broadcast(P)).then_inc(gain_loaded, 16)
                    if t == DEEP:
                        for at, part in ((0, w_dw[0]), (P_BDW, b_dw), (P_GLN, g_conv_ln), (P_BLN, b_conv_ln),
                                         (P_BPW, b_pw), (P_SCALE, pool_scale), (P_CHIST, state_conv[0, 0]),
                                         (P_PHIST, state_pool[0, 0])):
                            sp.dma_start(rows[at:at + part.shape[0], :], part).then_inc(par_loaded, 16)
                        for s in range(PARTS):
                            load_w_in(sp, S, 0, s)
                    if t >= DEEP:
                        sp.wait_ge(norm_ready, t - DEEP + 1)
                    if t >= BATCH:
                        sp.wait_ge(x_loaded[t % BATCH], 16 * (t // BATCH))
                    if t < TILES - 1:
                        sp.dma_start(x[t % DEEP], x_prompt[0, t * P:(t + 1) * P, :]).then_inc(x_loaded[t % BATCH], 16)
                    else:
                        sp.dma_start(x[t % DEEP][GAP:GAP + DEC, :], x_sample[0]).then_inc(x_loaded[t % BATCH], 16)

            @block.gpsimd
            def _(pool):
                pool.memset(S.ident[:, :], 0.0).then_inc(const_set, 1)
                pool.wait_ge(const_set, 1)
                pool.affine_select(out=S.ident[:, :], in_=S.ident[:, :], compare_op=ALU.not_equal, fill=1.0,
                                   base=0, pattern=[[-1, P]], channel_multiplier=1).then_inc(const_set, 1)
                pool.memset(S.ones[:, :], 1.0)
                pool.memset(S.zero[:, :], 0.0)
                pool.memset(S.minus_half[:, :], -0.5).then_inc(const_set, 1)
                pool.wait_ge(const_set, 3)
                for b in range(BATCHES):
                    pool.wait_ge(mean_ready, b + 1)
                    pool.tensor_tensor(rstd[:, of_batch(b)], ms[:, of_batch(b)], S.minus_half[:, 0:BATCH], ALU.pow)\
                        .then_inc(rstd_ready, 1)
                for s in range(PARTS):
                    w_in_lo(pool, S, 0, s)

            @block.scalar
            def _(act):
                def square(b):
                    for t in tiles(b):
                        act.wait_ge(x_loaded[t % BATCH], 16 * (t // BATCH) + 16)
                        if t >= DEEP:
                            act.wait_ge(turned, t - DEEP + 1)
                        act.activation(xn[t % DEEP], x[t % DEEP], ACT.Square, accum_out=ss[:, t:t + 1]).then_inc(squared, 1)

                def take_hi(b):
                    for t in tiles(b):
                        act.wait_ge(turned, t + 1)
                        act.activation(S.h_hi[:, :, t * P:(t + 1) * P], ps_t[t % BATCH][:, :, :], ACT.Copy)\
                           .then_inc(hi_ready, 1)

                square(0)
                for b in range(BATCHES):
                    if b + 1 < BATCHES:
                        square(b + 1)
                    if b + 1 == BATCHES:
                        for s in range(PARTS):
                            w_in_hi(act, S, 0, s)
                        act.wait_ge(par_turned, 1)
                        act.activation(S.par[:, :, :], ps_par[:, :, :], ACT.Copy).then_inc(par_ready, 1)
                    take_hi(b)

            @block.vector
            def _(dve):
                def norm(b):
                    dve.wait_ge(squared, b * BATCH + BATCH)
                    dve.tensor_scalar(ms[:, of_batch(b)], ss[:, of_batch(b)], 1.0 / D, EPS, ALU.mult, ALU.add)\
                       .then_inc(mean_ready, 1)
                    dve.wait_ge(rstd_ready, b + 1)
                    for t in tiles(b):
                        dve.scalar_tensor_tensor(xn[t % DEEP], x[t % DEEP], rstd[:, t:t + 1], gain[:, :],
                                                 ALU.mult, ALU.mult).then_inc(norm_ready, 1)

                def take_lo(b):
                    for t in tiles(b):
                        dve.wait_ge(hi_ready, t + 1)
                        cols = slice(t * P, (t + 1) * P)
                        dve.tensor_tensor(S.h_lo[:, :, cols], ps_t[t % BATCH][:, :, :], S.h_hi[:, :, cols].bitcast(F32),
                                          ALU.subtract).then_inc(lo_ready, 1)

                dve.wait_ge(gain_loaded, 16)
                norm(0)
                for b in range(BATCHES):
                    if b + 1 < BATCHES:
                        norm(b + 1)
                    take_lo(b)

            @block.tensor
            def _(pe):
                pe.wait_ge(const_set, 2)
                for t in range(TILES):
                    if t == DEEP:
                        pe.wait_ge(par_loaded, 8 * 16)
                        for c in range(KC):
                            last = pe.transpose(ps_par[:, c, :], rows[:, c * P:(c + 1) * P], S.ident[0:P_ALL, 0:P_ALL])
                        last.then_inc(par_turned, 1)
                    pe.wait_ge(norm_ready, t + 1)
                    if t >= BATCH:
                        pe.wait_ge(lo_ready, t - BATCH + 1)
                    for k in range(KD):
                        last = pe.transpose(ps_t[t % BATCH][:, k, :], xn[t % DEEP][:, k * P:(k + 1) * P], S.ident[:, :])
                    last.then_inc(turned, 1)


def w_in_hi(act, S, c, s):
    act.wait_ge(S.w_in_loaded[s], c * 16 + 16)
    act.activation(S.w_in_hi[s][:, :, :], S.w_in_raw[s][:, :, :], ACT.Copy).then_inc(S.w_in_hi_ready[s], 1)


def w_in_lo(pool, S, c, s):
    pool.wait_ge(S.w_in_hi_ready[s], c + 1)
    pool.tensor_tensor(S.w_in_lo[s][:, :, :], S.w_in_raw[s][:, :, :], S.w_in_hi[s][:, :, :].bitcast(F32),
                       ALU.subtract).then_inc(S.w_in_split[s], 1)


def in_projection_conv_pool(nc, S, w_pw, w_pool):
    A_PAD, U_PAD = CONV_HIST, POOL_HIST
    with ExitStack() as ctx:
        sb = lambda n, s, d=F32: ctx.enter_context(nc.sbuf_tensor(n, s, d))
        sem = lambda n: S.stack.enter_context(nc.semaphore(n))
        w_hi, w_lo, w_split = S.w_in_hi, S.w_in_lo, S.w_in_split
        a_ext, u_ext = sb("a_ext", [P, A_PAD + COLS]), sb("u_ext", [P, U_PAD + COLS])
        sums = [sb(f"window_sum{i}", [P, U_PAD + COLS]) for i in range(2)]
        sig = sb("sigmoid_gate", [P, CHUNKS, CHUNK])
        product = [sb(f"tap_product{i}", [P, COLS]) for i in range(2)]
        odd, late = sb("conv_odd_taps", [P, COLS]), sb("conv_late_taps", [P, COLS])
        window, inv = sb("windows", [P, KC]), sb("window_by_count", [P, POOL_GROUPS, 16])
        count = sb("count", [P, 16])
        tail = sb("state_tail", [P, KC, 90])
        state_rows = S.state_rows
        bank = [ctx.enter_context(nc.psum_tensor(f"z_bank{b}", [P, 512], F32)) for b in range(8)]
        a_bank, g_bank, u_bank = bank[0:3], bank[3:6], [bank[6], bank[7], bank[3]]
        z_ready = [sem(f"z_ready{s}") for s in range(PARTS)]
        sig_ready, a_ready, a_whole, conv_step = sem("sig_ready"), sem("a_ready"), sem("a_whole"), sem("conv_step")
        u_ready, group_done, pool_step = sem("u_ready"), sem("group_done"), sem("pool_step")
        padded, inv_step, tail_turned, tail_ready = sem("padded"), sem("inv_step"), sem("tail_turned"), sem("tail_ready")
        tail_read, product_ready, product_added, conv_done = (sem(n) for n in (
            "tail_read", "product_ready", "product_added", "conv_done"))
        with nc.Block() as block:

            @block.sync
            def _(sp):
                with sp.Fori(1, KC) as c:
                    for s in range(PARTS):
                        sp.wait_ge(w_split[s], c)
                        load_w_in(sp, S, c, s)
                sp.dma_start(S.w_pw[:, :, :], w_pw[0].rearrange("(k p) n -> p k n", p=P)).then_inc(S.mix_w_loaded, 16)
                sp.dma_start(S.w_pool[:, :, :], w_pool[0].rearrange("g c d -> c g d")).then_inc(S.mix_w_loaded, 16)
                with sp.Fori(EXPERTS, ITEMS) as i:
                    sp.dma_start(S.y_rows[bass.ds(i * P, P), :].rearrange("p (j n) -> p j n", n=P),
                                 S.zero[:, :].unsqueeze(1).to_broadcast([P, KD, P])).then_inc(S.y_cleared, 16)
                sp.wait_ge(tail_ready, 1)
                for at, n, out in ((0, CONV_HIST, S.conv_p), (CONV_HIST, CONV_HIST, S.conv_s),
                                   (2 * CONV_HIST, POOL_HIST, S.pool_p), (2 * CONV_HIST + POOL_HIST, POOL_HIST, S.pool_s)):
                    sp.dma_start(out[0, 0], state_rows[at:at + n, :]).then_inc(S.state_stored, 16)

            @block.scalar
            def _(act):
                def gates(c):
                    for n in range(CHUNKS):
                        act.wait_ge(z_ready[1], c * CHUNKS + (n + 1))
                        act.activation(sig[:, n, :], g_bank[n][:, 0:CHUNK], ACT.Sigmoid).then_inc(sig_ready, 1)

                def us(c):
                    act.wait_ge(group_done, c + 1)
                    for n in range(CHUNKS):
                        act.wait_ge(z_ready[2], c * CHUNKS + (n + 1))
                        act.activation(S.pooled[:, bass.ds(c, 1), n * CHUNK:(n + 1) * CHUNK], u_bank[n][:, 0:CHUNK],
                                       ACT.Copy, scale=window[:, bass.ds(c, 1)])
                        act.activation(u_ext[:, U_PAD + n * CHUNK:U_PAD + (n + 1) * CHUNK], u_bank[n][:, 0:CHUNK],
                                       ACT.Copy).then_inc(u_ready, 1)

                def products(c):
                    act.wait_ge(a_whole, c + 1)
                    for j in range(POOL_TAPS):
                        k = TAPS - POOL_TAPS + j
                        act.wait_ge(product_added, c * POOL_TAPS + (j + 1))
                        act.activation(product[j % 2][:, :], a_ext[:, k:k + COLS], ACT.Copy,
                                       scale=S.par[:, bass.ds(c, 1), k:k + 1]).then_inc(product_ready, 1)

                act.sem_inc(product_added, 2)
                act.sem_inc(product_ready, 1)
                act.sem_inc(u_ready, CHUNKS)
                act.wait_ge(padded, 3)
                with act.Fori(0, KC - 1) as c:
                    act.wait_ge(z_ready[0], c * CHUNKS + CHUNKS)
                    w_in_hi(act, S, c + 1, 0)
                    gates(c)
                    w_in_hi(act, S, c + 1, 1)
                    us(c)
                    w_in_hi(act, S, c + 1, 2)
                    products(c)
                gates(KC - 1)
                us(KC - 1)
                products(KC - 1)
                act.wait_ge(tail_turned, 1)
                act.activation(state_rows, bank[0][0:90, :], ACT.Copy).then_inc(tail_ready, 1)

            @block.gpsimd
            def _(pool):
                steps = [0]

                def step(ins):
                    steps[0] += 1
                    ins.then_inc(pool_step, 1)
                    pool.wait_ge(pool_step, steps[0])

                def add_products(c):
                    first = c * POOL_TAPS
                    pool.wait_ge(product_ready, first + 3)
                    pool.wait_ge(conv_done, c + 1)
                    pool.tensor_tensor(late[:, :], product[0][:, :], product[1][:, :], ALU.add).then_inc(product_added, 2)
                    for j in range(2, POOL_TAPS):
                        pool.wait_ge(product_ready, first + j + 2)
                        pool.wait_ge(product_added, first + j + 2)
                        pool.tensor_tensor(late[:, :], late[:, :], product[j % 2][:, :], ALU.add).then_inc(product_added, 1)

                pool.sem_inc(group_done, 1)
                pool.sem_inc(tail_read, 1)
                pool.memset(a_ext[:, 0:A_PAD], 0.0).then_inc(padded, 1)
                pool.memset(u_ext[:, 0:U_PAD], 0.0).then_inc(padded, 1)
                for c in range(KC):
                    pool.memset(window[:, c:c + 1], float(2 << c))
                pool.memset(sums[0][:, 0:16], 0.0)
                pool.memset(sums[1][:, 0:16], 0.0).then_inc(padded, 1)
                pool.iota(count[:, :], pattern=[[1, 16]], base=1, channel_multiplier=0,
                          allow_small_or_imprecise_dtypes=True).then_inc(inv_step, 1)
                for c in range(KC):
                    pool.tensor_scalar(S.par[:, c, P_SCALE:P_SCALE + 1], S.par[:, c, P_SCALE:P_SCALE + 1],
                                       1.0 / (2 << c), None, ALU.mult)
                pool.wait_ge(inv_step, 2 + 2 * POOL_GROUPS)

                def windows(c):
                    pool.wait_ge(u_ready, (c + 2) * CHUNKS)
                    step(pool.tensor_copy(u_ext[:, SAMPLE:SAMPLE + POOL_HIST], S.par[:, c, P_PHIST:P_ALL]))
                    pool.tensor_copy(tail[:, c, 2 * CONV_HIST:2 * CONV_HIST + POOL_HIST], u_ext[:, SEQ:SEQ + POOL_HIST])
                    pool.tensor_copy(tail[:, c, 2 * CONV_HIST + POOL_HIST:90],
                                     u_ext[:, SAMPLE + DEC:SAMPLE + DEC + POOL_HIST])
                    src = u_ext
                    for i in range(c + 1):
                        d = 1 << i
                        first = 2 * d - 1
                        dst = sums[i % 2]
                        step(pool.tensor_tensor(dst[:, first:], src[:, first:], src[:, first - d:U_PAD + COLS - d], ALU.add))
                        src = dst
                    step(pool.tensor_tensor(src[:, U_PAD:U_PAD + 16], src[:, U_PAD:U_PAD + 16], inv[:, c, :], ALU.mult))
                    pool.tensor_tensor(S.pooled[:, c, :], src[:, U_PAD:], S.pooled[:, c, :], ALU.subtract)\
                        .then_inc(group_done, 1)

                for c in range(KC):
                    if c + 1 < KC:
                        for s in range(PARTS):
                            w_in_lo(pool, S, c + 1, s)
                    pool.wait_ge(a_whole, c + 1)
                    pool.tensor_copy(tail[:, c, 0:CONV_HIST], a_ext[:, SEQ:SEQ + CONV_HIST])
                    pool.tensor_copy(tail[:, c, CONV_HIST:2 * CONV_HIST],
                                     a_ext[:, SAMPLE + DEC:SAMPLE + DEC + CONV_HIST]).then_inc(tail_read, 1)
                    add_products(c)
                    windows(c)

            @block.vector
            def _(dve):
                STEPS = TAPS - POOL_TAPS + 1
                dve.sem_inc(a_ready, CHUNKS)
                dve.sem_inc(conv_done, 1)
                dve.wait_ge(inv_step, 1)
                for g in range(POOL_GROUPS):
                    dve.tensor_scalar(inv[:, g, :], count[:, :], float(2 << g), None, ALU.min).then_inc(inv_step, 1)
                dve.wait_ge(inv_step, 1 + POOL_GROUPS)
                dve.reciprocal(inv[:, :, :], inv[:, :, :]).then_inc(inv_step, 1)
                dve.wait_ge(inv_step, 2 + POOL_GROUPS)
                for g in range(POOL_GROUPS):
                    dve.tensor_scalar(inv[:, g, :], inv[:, g, :], float(2 << g), None, ALU.mult).then_inc(inv_step, 1)
                dve.wait_ge(padded, 1)
                with dve.Fori(0, KC) as c:
                    dve.wait_ge(tail_read, c + 1)
                    dve.wait_ge(product_ready, c * POOL_TAPS + 1)
                    for n in range(CHUNKS):
                        dve.wait_ge(sig_ready, c * CHUNKS + (n + 1))
                        dve.tensor_tensor(a_ext[:, A_PAD + n * CHUNK:A_PAD + (n + 1) * CHUNK], a_bank[n][:, 0:CHUNK],
                                          sig[:, n, :], ALU.mult).then_inc(a_ready, 1)
                    dve.wait_ge(a_ready, c * CHUNKS + 2 * CHUNKS)
                    dve.tensor_copy(a_ext[:, SAMPLE:SAMPLE + CONV_HIST],
                                    S.par[:, bass.ds(c, 1), P_CHIST:P_PHIST]).then_inc(a_whole, 1)
                    dve.wait_ge(a_whole, c + 1)
                    even = S.conv[:, bass.ds(c, 1), :]
                    dve.tensor_scalar(even, a_ext[:, 0:COLS], S.par[:, bass.ds(c, 1), 0:1],
                                      S.par[:, bass.ds(c, 1), P_BDW:P_BDW + 1], ALU.mult, ALU.add).then_inc(conv_step, 1)
                    dve.tensor_scalar(odd[:, :], a_ext[:, 1:1 + COLS], S.par[:, bass.ds(c, 1), 1:2],
                                      None, ALU.mult).then_inc(conv_step, 1)
                    for k in range(2, TAPS - POOL_TAPS):
                        out = even if k % 2 == 0 else odd[:, :]
                        dve.wait_ge(conv_step, c * STEPS + k - 1)
                        dve.scalar_tensor_tensor(out, a_ext[:, k:k + COLS], S.par[:, bass.ds(c, 1), k:k + 1], out,
                                                 ALU.mult, ALU.add).then_inc(conv_step, 1)
                    dve.wait_ge(conv_step, c * STEPS + STEPS - 1)
                    dve.tensor_tensor(even, even, odd[:, :], ALU.add).then_inc(conv_step, 1)
                    dve.wait_ge(conv_step, c * STEPS + STEPS)
                    dve.wait_ge(product_added, c * POOL_TAPS + POOL_TAPS + 2)
                    dve.tensor_tensor(even, even, late[:, :], ALU.add).then_inc(conv_done, 1)
                    dve.wait_ge(conv_done, c + 2)

            @block.tensor
            def _(pe):
                with pe.Fori(0, KC) as c:
                    for s, banks in ((0, a_bank), (1, g_bank), (2, u_bank)):
                        pe.wait_ge(w_split[s], c + 1)
                        for n in range(CHUNKS):
                            if s == 0:
                                pe.wait_ge(a_ready, c * CHUNKS + (n + 1))
                            if s == 1 and n == 0:
                                pe.wait_ge(u_ready, c * CHUNKS + CHUNKS)
                            if s == 2 and n == 2:
                                pe.wait_ge(sig_ready, c * CHUNKS + 1)
                            cols = slice(n * CHUNK, (n + 1) * CHUNK)
                            for k in range(KD):
                                last = matmul3(pe, banks[n][:, 0:CHUNK], w_hi[s][:, k, :], w_lo[s][:, k, :],
                                               S.h_hi[:, k, cols], S.h_lo[:, k, cols], k == 0, k == KD - 1)
                            last.then_inc(z_ready[s], 1)
                pe.wait_ge(group_done, KC + 1)
                for c in range(KC):
                    last = pe.transpose(bank[0][0:90, c * P:(c + 1) * P], tail[:, c, :], S.ident[:, :])
                last.then_inc(tail_turned, 1)


def mixer_outputs(nc, S, w_out):
    with ExitStack() as ctx:
        sb = lambda n, s, d=F32: ctx.enter_context(nc.sbuf_tensor(n, s, d))
        sem = lambda n: S.stack.enter_context(nc.semaphore(n))
        sq = sb("conv_sq", [P, KC, COLS])
        var, rstd = sb("conv_var", [P, CHUNKS, CHUNK]), sb("conv_rstd", [P, CHUNKS, CHUNK])
        root, fix = sb("conv_root", [P, CHUNKS, CHUNK]), sb("conv_fix", [P, CHUNKS, CHUNK])
        raw = [sb(f"w_out_raw{i}", [P, 2, D]) for i in range(2)]
        bank = [ctx.enter_context(nc.psum_tensor(f"mix_bank{b}", [P, 512], F32)) for b in range(8)]
        raw_loaded = [sem(f"w_out_loaded{i}") for i in range(2)]
        w_hi_ready, w_lo_ready = sem("w_out_hi_ready"), sem("w_out_lo_ready")
        sum_ready, centred, sq_ready = sem("sum_ready"), sem("centred"), sem("sq_ready")
        varsum_ready, var_ready, rstd_ready, root_ready = sem("varsum_ready"), sem("var_ready"), sem("conv_rstd_step"), sem("root_ready")
        scaled, c_ready, o_ready, o_left = sem("scaled"), sem("c_ready"), sem("o_product"), sem("o_left")
        cols = [slice(n * CHUNK, (n + 1) * CHUNK) for n in range(CHUNKS)]
        outs = [(KC + g, n) for g in range(KC) for n in range(CHUNKS)] + [(c, n) for n in range(CHUNKS) for c in range(KC)]
        o_bank = lambda i: bank[3 + i % 5][:, 0:CHUNK]
        w_view = w_out[0].rearrange("(k p) n -> p k n", p=P)
        with nc.Block() as block:

            @block.sync
            def _(sp):
                for i in range(KD // 2):
                    if i >= 2:
                        sp.wait_ge(w_lo_ready, i - 1)
                    sp.dma_start(raw[i % 2][:, :, :], w_view[:, 2 * i:2 * i + 2, :]).then_inc(raw_loaded[i % 2], 16)

            @block.gpsimd
            def _(pool):
                def take_lo(i):
                    pool.wait_ge(w_hi_ready, i + 1)
                    pool.tensor_tensor(S.wo_lo[:, 2 * i:2 * i + 2, :], raw[i % 2][:, :, :],
                                       S.wo_hi[:, 2 * i:2 * i + 2, :].bitcast(F32), ALU.subtract).then_inc(w_lo_ready, 1)

                pool.memset(S.o[:, :, COLS:ROWS], 0.0)
                for i in range(KD // 2):
                    take_lo(i)

            @block.scalar
            def _(act):
                def take_hi(i):
                    act.wait_ge(raw_loaded[i % 2], 16 * (i // 2) + 16)
                    act.activation(S.wo_hi[:, 2 * i:2 * i + 2, :], raw[i % 2][:, :, :], ACT.Copy).then_inc(w_hi_ready, 1)

                def leave(i):
                    act.wait_ge(o_ready, i + 1)
                    block_of, n = outs[i]
                    if block_of >= KC:
                        g = block_of - KC
                        act.activation(S.o[:, block_of, cols[n]], o_bank(i), ACT.Copy, scale=S.par[:, g, P_SCALE:P_SCALE + 1])\
                           .then_inc(o_left, 1)
                    else:
                        act.activation(S.o[:, block_of, cols[n]], o_bank(i), ACT.Identity,
                                       bias=S.par[:, block_of, P_BPW:P_BPW + 1]).then_inc(o_left, 1)

                take_hi(0)
                take_hi(1)
                for n in range(CHUNKS):
                    act.wait_ge(centred, n + 1)
                    act.activation(sq[:, :, cols[n]], S.conv[:, :, cols[n]], ACT.Square).then_inc(sq_ready, 1)
                for i in range(KC * CHUNKS):
                    leave(i)
                    if CHUNKS <= i < 2 * CHUNKS:
                        n = i - CHUNKS
                        act.wait_ge(var_ready, n + 1)
                        act.activation(root[:, n, :], var[:, n, :], ACT.Sqrt).then_inc(root_ready, 1)
                        if n == 2:
                            take_hi(2)
                            take_hi(3)
                for n in range(CHUNKS):
                    act.wait_ge(scaled, n + 1)
                    for c in range(KC):
                        act.activation(S.conv[:, c, cols[n]], S.conv[:, c, cols[n]], ACT.Silu,
                                       bias=S.par[:, c, P_BLN:P_BLN + 1], scale=S.par[:, c, P_GLN:P_GLN + 1])\
                           .then_inc(c_ready, 1)
                    if n >= 1:
                        for i in range(KC):
                            leave(KC * CHUNKS + (n - 1) * KC + i)
                for i in range(KC):
                    leave(KC * CHUNKS + (CHUNKS - 1) * KC + i)

            @block.vector
            def _(dve):
                steps = [0]

                def step(ins):
                    steps[0] += 1
                    ins.then_inc(rstd_ready, 1)
                    dve.wait_ge(rstd_ready, steps[0])

                for n in range(CHUNKS):
                    dve.wait_ge(sum_ready, n + 1)
                    dve.scalar_tensor_tensor(S.conv[:, :, cols[n]],
                                             bank[n][:, 0:CHUNK].unsqueeze(1).to_broadcast([P, KC, CHUNK]), -1.0 / CH,
                                             S.conv[:, :, cols[n]], ALU.mult, ALU.add).then_inc(centred, 1)
                def variance(n):
                    dve.wait_ge(varsum_ready, n + 1)
                    dve.tensor_scalar(var[:, n, :], bank[n][:, 0:CHUNK], 1.0 / CH, EPS, ALU.mult, ALU.add)\
                       .then_inc(var_ready, 1)

                variance(0)
                for n in range(CHUNKS):
                    dve.wait_ge(root_ready, n + 1)
                    step(dve.reciprocal(rstd[:, n, :], root[:, n, :]))
                    if n == 0:
                        variance(1)
                    step(dve.tensor_tensor(fix[:, n, :], rstd[:, n, :], rstd[:, n, :], ALU.mult))
                    step(dve.scalar_tensor_tensor(fix[:, n, :], fix[:, n, :], -0.5, var[:, n, :], ALU.mult, ALU.mult))
                    step(dve.scalar_tensor_tensor(rstd[:, n, :], fix[:, n, :], 1.5, rstd[:, n, :], ALU.add, ALU.mult))
                    if n == 0:
                        variance(2)
                    dve.tensor_tensor(S.conv[:, :, cols[n]], S.conv[:, :, cols[n]],
                                      rstd[:, n, :].unsqueeze(1).to_broadcast([P, KC, CHUNK]), ALU.mult).then_inc(scaled, 1)

            @block.tensor
            def _(pe):
                for n in range(CHUNKS):
                    for c in range(KC):
                        last = pe.matmul(bank[n][:, 0:CHUNK], S.ones[:, :], S.conv[:, c, cols[n]],
                                         start=(c == 0), stop=(c == KC - 1))
                    last.then_inc(sum_ready, 1)
                pe.wait_ge(S.mix_w_loaded, 32)
                i = 0
                for g in range(KC):
                    for n in range(CHUNKS):
                        if i >= 5:
                            pe.wait_ge(o_left, i - 4)
                        pe.matmul(o_bank(i), S.w_pool[:, g, :], S.pooled[:, g, cols[n]], start=True, stop=True)\
                          .then_inc(o_ready, 1)
                        i += 1
                        if g == 1:
                            pe.wait_ge(sq_ready, n + 1)
                            for c in range(KC):
                                last = pe.matmul(bank[n][:, 0:CHUNK], S.ones[:, :], sq[:, c, cols[n]],
                                                 start=(c == 0), stop=(c == KC - 1))
                            last.then_inc(varsum_ready, 1)
                for n in range(CHUNKS):
                    pe.wait_ge(c_ready, KC * (n + 1))
                    for c in range(KC):
                        pe.wait_ge(o_left, i - 4)
                        for k in range(KC):
                            last = pe.matmul(o_bank(i), S.w_pw[:, k, c * P:(c + 1) * P], S.conv[:, k, cols[n]],
                                             start=(k == 0), stop=(k == KC - 1))
                        last.then_inc(o_ready, 1)
                        i += 1


def out_projection(nc, S, x_prompt, x_sample, g_ffn, w_rg, w_re):
    HALF = KD // 2
    with ExitStack() as ctx:
        sb = lambda n, s, d=F32: ctx.enter_context(nc.sbuf_tensor(n, s, d))
        sem = lambda n: S.stack.enter_context(nc.semaphore(n))
        x, x2, h2, junk, gain = (sb(n, [P, D]) for n in ("x_res", "x2_tile", "h2_tile", "sq_junk4", "g_ffn_rows"))
        o_hi, o_lo = sb("o_hi", [P, KD, P], F32R), sb("o_lo", [P, KD, P], F32R)
        h2_t = sb("h2_t", [P, KD, P])
        w_route = sb("w_route", [P, KD, GROUPS + EXPERTS])
        ss, ms, rstd = sb("ss4", [P, 1]), sb("ms4", [P, 1]), sb("rstd4", [P, 1])
        ps = [ctx.enter_context(nc.psum_tensor(f"ps_out{h}", [P, 512], F32)) for h in range(2)]
        ps_t = ctx.enter_context(nc.psum_tensor("ps_h2t", [P, KD, P], F32))
        x_loaded, gain_loaded, route_loaded = sem("x_loaded4"), sem("gain_loaded4"), sem("route_loaded")
        hi_ready, lo_ready, used, added = sem("o_hi_ready"), sem("o_lo_ready"), sem("o_used"), sem("added")
        squared, mean_ready, rstd_ready, h2_ready = sem("squared4"), sem("mean4"), sem("rstd_ready4"), sem("h2_ready")
        turned, h2t_ready = sem("h2_turned"), sem("h2t_ready")
        x2_stored, h2_stored = sem("x2_stored"), sem("h2_stored")
        with nc.Block() as block:

            @block.sync
            def _(sp):
                def store(t):
                    sp.wait_ge(added, t + 2)
                    sp.dma_start(S.x2_rows[bass.ds(t * P, P), :], x2[:, :]).then_inc(x2_stored, 16)

                def store_h(t):
                    sp.wait_ge(h2_ready, t + 1)
                    sp.dma_start(S.h2_rows[bass.ds(t * P, P), :], h2[:, :]).then_inc(h2_stored, 16)

                sp.sem_inc(x2_stored, 16)
                sp.sem_inc(h2_stored, 16)
                sp.dma_start(x[:, :], x_prompt[0, 0:P, :]).then_inc(x_loaded, 16)

                def tile(t):
                    store(t)
                    sp.dma_start(x[:, :], x_prompt[0, bass.ds(t * P + P, P), :]).then_inc(x_loaded, 16)
                    store_h(t)

                sp.wait_ge(S.state_stored, 4 * 16)
                for t in range(3):
                    tile(t)
                    for s in (2 * t, 2 * t + 1):
                        sp.sem_inc(S.w_split[s], 1)
                        load_piece(sp, S, s, 0, expert_piece(S, s, slice(0, 1)))
                with sp.Fori(3, TILES - 2) as t:
                    tile(t)
                store(TILES - 2)
                sp.dma_start(x[GAP:GAP + DEC, :], x_sample[0]).then_inc(x_loaded, 16)
                store_h(TILES - 2)
                store(TILES - 1)
                store_h(TILES - 1)
                sp.wait_ge(x2_stored, 16 * (TILES + 1))
                sp.wait_ge(h2_stored, 16 * (TILES + 1))

            @block.gpsimd
            def _(pool):
                with pool.Fori(0, TILES) as t:
                    pool.wait_ge(mean_ready, t + 1)
                    pool.tensor_tensor(rstd[:, :], ms[:, :], S.minus_half[:, 0:1], ALU.pow).then_inc(rstd_ready, 1)

            @block.scalar
            def _(act):
                act.dma_start(gain[:, :], g_ffn[0].partition_broadcast(P)).then_inc(gain_loaded, 16)
                act.dma_start(w_route[:, :, 0:GROUPS], w_rg[0].rearrange("(k p) n -> p k n", p=P)).then_inc(route_loaded, 16)
                act.dma_start(w_route[:, :, GROUPS:], w_re[0].rearrange("(k p) n -> p k n", p=P)).then_inc(route_loaded, 16)

                def take_hi(t, i):
                    ks = slice(i * HALF, (i + 1) * HALF)
                    act.activation(o_hi[:, ks, :], S.o[:, ks, bass.ds(t * P, P)], ACT.Copy).then_inc(hi_ready, 1)

                def next_hi(t):
                    for i in range(2):
                        act.wait_ge(used, 2 * t + (i - 1))
                        take_hi(t, i)

                def square(t):
                    if type(t) is not int or t > 0:
                        act.wait_ge(squared, t)
                    act.wait_ge(added, t + 2)
                    act.activation(junk[:, :], x2[:, :], ACT.Square, accum_out=ss[:, :]).then_inc(squared, 1)

                def leave(t):
                    act.wait_ge(turned, t + 2)
                    act.activation(h2_t[:, :, :], ps_t[:, :, :], ACT.Copy).then_inc(h2t_ready, 1)

                take_hi(0, 0)
                take_hi(0, 1)
                next_hi(1)
                square(0)
                with act.Fori(1, TILES - 1) as t:
                    next_hi(t + 1)
                    square(t)
                    leave(t - 1)
                square(TILES - 1)
                leave(TILES - 2)
                leave(TILES - 1)

            @block.vector
            def _(dve):
                def take_lo(t, i):
                    ks = slice(i * HALF, (i + 1) * HALF)
                    dve.wait_ge(hi_ready, t * 2 + (i + 1))
                    dve.tensor_tensor(o_lo[:, ks, :], S.o[:, ks, bass.ds(t * P, P)], o_hi[:, ks, :].bitcast(F32),
                                      ALU.subtract).then_inc(lo_ready, 1)

                def add(t):
                    dve.wait_ge(x_loaded, t * 16 + 16)
                    dve.wait_ge(x2_stored, t * 16 + 16)
                    dve.wait_ge(used, t * 2 + 2)
                    dve.tensor_tensor(x2[:, 0:512], ps[0][:, :], x[:, 0:512], ALU.add)
                    dve.tensor_tensor(x2[:, 512:D], ps[1][:, :], x[:, 512:D], ALU.add).then_inc(added, 1)

                def norm(t):
                    dve.wait_ge(squared, t + 1)
                    dve.tensor_scalar(ms[:, :], ss[:, :], 1.0 / D, EPS, ALU.mult, ALU.add).then_inc(mean_ready, 1)
                    dve.wait_ge(rstd_ready, t + 1)
                    dve.wait_ge(h2_stored, t * 16 + 16)
                    dve.wait_ge(turned, t + 1)
                    dve.scalar_tensor_tensor(h2[:, :], x2[:, :], rstd[:, :], gain[:, :], ALU.mult, ALU.mult)\
                       .then_inc(h2_ready, 1)
                    dve.wait_ge(h2_ready, t + 1)

                dve.sem_inc(added, 1)
                dve.wait_ge(gain_loaded, 16)
                take_lo(0, 0)
                take_lo(0, 1)
                with dve.Fori(0, TILES - 1) as t:
                    take_lo(t + 1, 0)
                    add(t)
                    take_lo(t + 1, 1)
                    norm(t)
                add(TILES - 1)
                norm(TILES - 1)

            @block.tensor
            def _(pe):
                def products(t):
                    pe.wait_ge(added, t + 1)
                    for i in range(2):
                        pe.wait_ge(lo_ready, t * 2 + (i + 1))
                        for k in range(i * HALF, (i + 1) * HALF):
                            for h in range(2):
                                half = slice(h * 512, (h + 1) * 512)
                                last = matmul3(pe, ps[h][:, :], o_hi[:, k, :], o_lo[:, k, :], S.wo_hi[:, k, half],
                                               S.wo_lo[:, k, half], k == 0, k == KD - 1)
                        last.then_inc(used, 1)

                def turn(t):
                    pe.wait_ge(h2_ready, t + 1)
                    for k in range(KD):
                        last = pe.transpose(ps_t[:, k, :], h2[:, k * P:(k + 1) * P], S.ident[:, :])
                    last.then_inc(turned, 1)

                def route(t):
                    pe.wait_ge(h2t_ready, t + 1)
                    for k in range(KD):
                        last = pe.matmul(S.ps_route[:, bass.ds(t, 1), :], h2_t[:, k, :], w_route[:, k, :],
                                         start=(k == 0), stop=(k == KD - 1))
                    last.then_inc(S.routed, 1)

                pe.sem_inc(turned, 1)
                products(0)
                products(1)
                turn(0)
                pe.wait_ge(route_loaded, 32)
                with pe.Fori(2, TILES) as t:
                    products(t)
                    route(t - 2)
                    turn(t - 1)
                route(TILES - 2)
                turn(TILES - 1)
                route(TILES - 1)


def routing(nc, S, b_rg, b_re):
    T, E, G, C8 = TILES, EXPERTS, GROUPS, PER_GROUP
    with ExitStack() as ctx:
        sb = lambda n, s, d=F32: ctx.enter_context(nc.sbuf_tensor(n, s, d))
        sem = lambda n: S.stack.enter_context(nc.semaphore(n))
        bias = sb("route_bias", [P, G + E])
        lg = sb("logits", [P, T, G + E])
        idx = sb("iota_experts", [P, E])
        valid = sb("valid_rows", [P, T])
        first_row = sb("first_rows", [P, 2, T])
        lane, tile_of = sb("iota_lanes", [P, P]), sb("tile_numbers", [P, 2, T])
        own_lane = sb("own_lane", [P, 1])
        at_row = sb("at_row", [P, 2 * T, P], BF16)
        at_item, token_parts = sb("at_item", [P, 2 * T, ITEMS], BF16), sb("token_parts", [P, 2 * T, 2, ITEMS], BF16)
        tri = sb("earlier", [P, P], BF16)
        ones_b = sb("ones_b", [P, P], BF16)
        best, gsel, gw = (sb(n, [P, T]) for n in ("best", "group", "group_weight"))
        g4, g4b = sb("group_work", [P, T, G]), sb("group_onehot", [P, T, G])
        e32, esel, e8, e8b = sb("e32", [P, T, G, C8]), sb("esel", [P, T, C8]), sb("e8", [P, T, C8]), sb("e8b", [P, T, C8])
        m1, m2 = sb("m1", [P, T]), sb("m2", [P, T])
        eid = sb("eid", [P, 2, T])
        oh = [sb(f"onehot{k}", [P, T, E]) for k in range(2)]
        ohs = sb("onehot_sum", [P, T, E], BF16)
        tot, base, rank = sb("tile_totals", [P, T, E]), sb("tile_base", [P, T + 1, E]), sb("rank", [P, T, E])
        t32 = sb("t32", [P, T, E])
        limit, further = sb("block_starts", [P, MAX_BLOCKS - 1]), sb("further_blocks", [P, E, MAX_BLOCKS - 1])
        tokens_low = sb("item_tokens_low", [P, ITEMS])
        over, cum, cum2 = sb("over", [P, E]), sb("cum", [P, E]), sb("cum2", [P, E])
        rk, osk, item, s18 = (sb(n, [P, 2, T]) for n in ("rk", "osk", "item", "s18"))
        blk, in_item = sb("rank_blocks", [P, 2, T]), sb("row_in_item", [P, 2, T])
        ended = sb("ended_experts", [P, ITEMS + 1, E])
        number, owner, n1 = sb("item_numbers", [P, ITEMS + 1]), sb("item_owners", [P, ITEMS + 1]), sb("n1", [P, 1])
        ps_rank = ctx.enter_context(nc.psum_tensor("ps_rank", [P, T, E], F32))
        ps_tot = ctx.enter_context(nc.psum_tensor("ps_tot", [P, T, E], F32))
        ps_items = ctx.enter_context(nc.psum_tensor("ps_items", [P, 2, ITEMS], F32))
        bias_loaded, made, exp_ready = sem("bias_loaded"), sem("tables_made"), sem("exp_ready")
        chain, to_exp, to_rank, ranked = sem("route_chain"), sem("to_exp"), sem("to_rank"), sem("ranked")
        to_place, placed = sem("to_place"), sem("placed")
        bc = lambda ap, shape: ap.to_broadcast(shape)
        with nc.Block() as block:

            @block.sync
            def _(sp):
                sp.dma_start(bias[:, 0:G], b_rg[0].partition_broadcast(P)).then_inc(bias_loaded, 16)
                sp.dma_start(bias[:, G:], b_re[0].partition_broadcast(P)).then_inc(bias_loaded, 16)
                for s in GATE + UP:
                    load_piece(sp, S, s, 1, expert_piece(S, s, slice(1, 2)))
                sp.wait_ge(S.y_cleared, 16 * (ITEMS - EXPERTS))

            @block.gpsimd
            def _(pool):
                pool.iota(idx[:, :], pattern=[[1, E]], base=0, channel_multiplier=0, allow_small_or_imprecise_dtypes=True)
                pool.iota(number[:, :], pattern=[[1, ITEMS + 1]], base=0, channel_multiplier=0,
                          allow_small_or_imprecise_dtypes=True)
                pool.iota(lane[:, :], pattern=[[1, P]], base=0, channel_multiplier=0, allow_small_or_imprecise_dtypes=True)
                pool.iota(limit[:, :], pattern=[[P, MAX_BLOCKS - 1]], base=P, channel_multiplier=0,
                          allow_small_or_imprecise_dtypes=True)
                pool.iota(own_lane[:, :], pattern=[[0, 1]], base=0, channel_multiplier=1,
                          allow_small_or_imprecise_dtypes=True)
                pool.iota(tile_of[:, :, :], pattern=[[0, 2], [1, T]], base=0, channel_multiplier=0,
                          allow_small_or_imprecise_dtypes=True)
                pool.memset(valid[:, :], 1.0)
                pool.memset(tri[:, :], 1.0)
                pool.memset(first_row[:, :, 0:T - 1], 0.0)
                pool.iota(first_row[:, :, T - 1], pattern=[[0, 2]], base=0, channel_multiplier=1,
                          allow_small_or_imprecise_dtypes=True)
                pool.memset(ones_b[:, :], 1.0).then_inc(made, 1)
                pool.wait_ge(made, 1)
                pool.affine_select(out=valid[:, T - 1:T], in_=valid[:, T - 1:T], compare_op=ALU.is_ge, fill=0.0,
                                   base=-GAP, pattern=[[0, 1]], channel_multiplier=1).then_inc(made, 1)
                pool.wait_ge(made, 2)
                pool.affine_select(out=valid[:, T - 1:T], in_=valid[:, T - 1:T], compare_op=ALU.is_ge, fill=0.0,
                                   base=GAP + DEC - 1, pattern=[[0, 1]], channel_multiplier=-1)
                pool.affine_select(out=tri[:, :], in_=tri[:, :], compare_op=ALU.is_gt, fill=0.0,
                                   base=0, pattern=[[1, P]], channel_multiplier=-1).then_inc(made, 1)
                for s in range(6):
                    piece_lo(pool, S, 0, s)
                pool.wait_ge(S.tokens_ready, 1)
                gather_tokens(pool, S, 0)

            @block.scalar
            def _(act):
                for s in GATE + UP:
                    piece_hi(act, S, 0, s, None)
                act.wait_ge(to_exp, 1)
                act.activation(g4[:, :, :], g4[:, :, :], ACT.Exp).then_inc(exp_ready, 1)
                act.wait_ge(to_exp, 2)
                act.activation(m2[:, :], m2[:, :], ACT.Exp).then_inc(exp_ready, 1)
                for s in DOWN:
                    piece_hi(act, S, 0, s, None)

            @block.tensor
            def _(pe):
                pe.wait_ge(made, 3)
                pe.wait_ge(to_rank, 1)
                pe.matmul(ps_tot[:, :, :], ones_b[:, :], ohs[:, :, :], start=True, stop=True)
                pe.matmul(ps_rank[:, :, :], tri[:, :], ohs[:, :, :], start=True, stop=True).then_inc(ranked, 1)
                pe.wait_ge(to_place, 1)
                for a in range(2 * T):
                    last = pe.matmul(ps_items[:, :, :], at_row[:, a, :], token_parts[:, a, :, :],
                                     start=(a == 0), stop=(a == 2 * T - 1))
                last.then_inc(placed, 1)

            @block.vector
            def _(dve):
                links = [0]

                def step(ins):
                    links[0] += 1
                    ins.then_inc(chain, 1)
                    dve.wait_ge(chain, links[0])

                tt = lambda o, a, b, op: step(dve.tensor_tensor(o, a, b, op))
                ts = lambda o, a, s1, s2, o1, o2=None: step(
                    dve.tensor_scalar(o, a, s1, s2, o1) if o2 is None else dve.tensor_scalar(o, a, s1, s2, o1, o2))
                red = lambda o, a, op: step(dve.tensor_reduce(o, a, AX.X, op))

                def argfirst(out, values, best, n, work):
                    tt(work, values, bc(best.unsqueeze(2), [P, T, n]), ALU.is_equal)
                    step(dve.scalar_tensor_tensor(work, bc(idx[:, 0:n].unsqueeze(1), [P, T, n]), -float(E), work,
                                                  ALU.add, ALU.mult))
                    red(out, work, ALU.min)
                    ts(out, out, float(E), None, ALU.add)

                dve.wait_ge(made, 3)
                dve.wait_ge(bias_loaded, 32)
                dve.wait_ge(S.routed, T)
                tt(lg[:, :, :], S.ps_route[:, :, :], bc(bias[:, :].unsqueeze(1), [P, T, G + E]), ALU.add)
                red(best[:, :], lg[:, :, 0:G], ALU.max)
                argfirst(gsel[:, :], lg[:, :, 0:G], best[:, :], G, g4[:, :, :])
                tt(g4[:, :, :], lg[:, :, 0:G], bc(best[:, :].unsqueeze(2), [P, T, G]), ALU.subtract)
                dve.sem_inc(to_exp, 1)
                tt(g4b[:, :, :], bc(idx[:, 0:G].unsqueeze(1), [P, T, G]), bc(gsel[:, :].unsqueeze(2), [P, T, G]), ALU.is_equal)
                tt(e32[:, :, :, :], lg[:, :, G:].rearrange("p t (g e) -> p t g e", g=G),
                   bc(g4b[:, :, :].unsqueeze(3), [P, T, G, C8]), ALU.mult)
                tt(esel[:, :, :], e32[:, :, 0, :], e32[:, :, 1, :], ALU.add)
                tt(esel[:, :, :], esel[:, :, :], e32[:, :, 2, :], ALU.add)
                tt(esel[:, :, :], esel[:, :, :], e32[:, :, 3, :], ALU.add)
                red(m1[:, :], esel[:, :, :], ALU.max)
                argfirst(eid[:, 0, :], esel[:, :, :], m1[:, :], C8, e8[:, :, :])
                tt(e8[:, :, :], bc(idx[:, 0:C8].unsqueeze(1), [P, T, C8]), bc(eid[:, 0, :].unsqueeze(2), [P, T, C8]),
                   ALU.is_equal)
                step(dve.scalar_tensor_tensor(e8b[:, :, :], e8[:, :, :], -1e30, esel[:, :, :], ALU.mult, ALU.add))
                red(m2[:, :], e8b[:, :, :], ALU.max)
                argfirst(eid[:, 1, :], e8b[:, :, :], m2[:, :], C8, e8[:, :, :])
                tt(m2[:, :], m2[:, :], m1[:, :], ALU.subtract)
                dve.sem_inc(to_exp, 1)
                for k in range(2):
                    step(dve.scalar_tensor_tensor(eid[:, k, :], gsel[:, :], float(C8), eid[:, k, :], ALU.mult, ALU.add))
                    step(dve.scalar_tensor_tensor(eid[:, k, :], eid[:, k, :], 1.0, valid[:, :], ALU.add, ALU.mult))
                    ts(eid[:, k, :], eid[:, k, :], -1.0, None, ALU.add)
                    tt(oh[k][:, :, :], bc(idx[:, :].unsqueeze(1), [P, T, E]), bc(eid[:, k, :].unsqueeze(2), [P, T, E]),
                       ALU.is_equal)
                tt(ohs[:, :, :], oh[0][:, :, :], oh[1][:, :, :], ALU.add)
                dve.sem_inc(to_rank, 1)
                dve.wait_ge(ranked, 1)
                step(dve.tensor_copy(tot[:, :, :], ps_tot[:, :, :]))
                step(dve.memset(base[:, 0, :], 0.0))
                for t in range(T):
                    tt(base[:, t + 1, :], base[:, t, :], tot[:, t, :], ALU.add)
                tt(rank[:, :, :], ps_rank[:, :, :], base[:, 0:T, :], ALU.add)
                for k in range(2):
                    tt(t32[:, :, :], oh[k][:, :, :], rank[:, :, :], ALU.mult)
                    red(rk[:, k, :], t32[:, :, :], ALU.add)
                total = base[:, T, :]
                more = [P, E, MAX_BLOCKS - 1]
                tt(further[:, :, :], bc(total.unsqueeze(2), more), bc(limit[:, :].unsqueeze(1), more), ALU.is_gt)
                red(over[:, :], further[:, :, :], ALU.add)
                ts(over[:, :], over[:, :], 1.0, None, ALU.add)
                src, dst, d = over, cum, 1
                while d < E:
                    tt(dst[:, d:], src[:, d:], src[:, 0:E - d], ALU.add)
                    step(dve.tensor_copy(dst[:, 0:d], src[:, 0:d]))
                    src, dst, d = dst, (cum2 if dst is cum else cum), 2 * d
                incl = src
                tt(over[:, :], incl[:, :], over[:, :], ALU.subtract)
                for k in range(2):
                    tt(t32[:, :, :], oh[k][:, :, :], bc(over[:, :].unsqueeze(1), [P, T, E]), ALU.mult)
                    red(osk[:, k, :], t32[:, :, :], ALU.add)
                shape = [P, 2 * T, MAX_BLOCKS - 1]
                ranks = rk[:, :, :].rearrange("p k t -> p (k t)").unsqueeze(2)
                tt(further[:, 0:2 * T, :], bc(ranks, shape), bc(limit[:, :].unsqueeze(1), shape), ALU.is_ge)
                red(blk[:, :, :].rearrange("p k t -> p (k t)"), further[:, 0:2 * T, :], ALU.add)
                step(dve.scalar_tensor_tensor(in_item[:, :, :], blk[:, :, :], -float(P), rk[:, :, :], ALU.mult, ALU.add))
                tt(item[:, :, :], osk[:, :, :], blk[:, :, :], ALU.add)
                v2 = bc(valid[:, :].unsqueeze(1), [P, 2, T])
                step(dve.scalar_tensor_tensor(item[:, :, :], item[:, :, :], 1.0, v2, ALU.add, ALU.mult))
                ts(item[:, :, :], item[:, :, :], -1.0, None, ALU.add)
                flat = lambda ap: ap.rearrange("p k t -> p (k t)").unsqueeze(2)
                tt(at_row[:, :, :], bc(lane[:, :].unsqueeze(1), [P, 2 * T, P]), bc(flat(in_item[:, :, :]), [P, 2 * T, P]),
                   ALU.is_equal)
                tt(at_item[:, :, :], bc(number[:, 0:ITEMS].unsqueeze(1), [P, 2 * T, ITEMS]),
                   bc(flat(item[:, :, :]), [P, 2 * T, ITEMS]), ALU.is_equal)
                ts(token_parts[:, :, 0, :], at_item[:, :, :], own_lane[:, :], None, ALU.mult)
                tt(token_parts[:, :, 1, :], at_item[:, :, :], bc(flat(tile_of[:, :, :]), [P, 2 * T, ITEMS]), ALU.mult)
                dve.sem_inc(to_place, 1)
                ts(n1[:, :], incl[:, E - 1:E], -1.0, None, ALU.add)
                step(dve.tensor_copy(S.last_item[:, :], n1[:, :]))
                dve.wait_ge(placed, 1)
                step(dve.tensor_copy(tokens_low[:, :], ps_items[:, 0, :]))
                step(dve.scalar_tensor_tensor(tokens_low[:, :], ps_items[:, 1, :], float(P), tokens_low[:, :],
                                              ALU.mult, ALU.add))
                step(dve.tensor_copy(S.item_tokens[:, :], tokens_low[:, :]))
                dve.sem_inc(S.tokens_ready, 1)
                step(dve.scalar_tensor_tensor(s18[:, :, :], osk[:, :, :], float(P), rk[:, :, :], ALU.mult, ALU.add))
                tt(s18[:, :, :], s18[:, :, :], v2, ALU.mult)
                tt(item[:, :, :], first_row[:, :, :], v2, ALU.mult)
                tt(item[:, :, :], first_row[:, :, :], item[:, :, :], ALU.subtract)
                tt(s18[:, :, :], s18[:, :, :], item[:, :, :], ALU.add)
                step(dve.tensor_copy(S.out_row[:, :, :], s18[:, :, :]))
                shape = [P, ITEMS + 1, E]
                tt(ended[:, :, :], bc(incl[:, :].unsqueeze(1), shape), bc(number[:, :].unsqueeze(2), shape), ALU.is_le)
                red(owner[:, :], ended[:, :, :], ALU.add)
                step(dve.tensor_copy(S.item_expert[:, :], owner[:, :]))
                dve.wait_ge(exp_ready, 2)
                red(gw[:, :], g4[:, :, :], ALU.add)
                step(dve.reciprocal(gw[:, :], gw[:, :]))
                ts(best[:, :], m2[:, :], 1.0, None, ALU.add)
                step(dve.reciprocal(best[:, :], best[:, :]))
                tt(S.gate[:, 0, :], best[:, :], gw[:, :], ALU.mult)
                tt(S.gate[:, 1, :], S.gate[:, 0, :], m2[:, :], ALU.mult)


def experts(nc, S, ple_gate, ple_proj, gains, p_prompt):
    with ExitStack() as ctx:
        sb = lambda n, s, d=F32: ctx.enter_context(nc.sbuf_tensor(n, s, d))
        sem = lambda n: S.stack.enter_context(nc.semaphore(n))
        w_hi, w_lo, w_split, w_used = S.w_hi, S.w_lo, S.w_split, S.w_used
        x = S.x_tokens
        x_hi, x_lo = sb("xt_hi", [P, KD, P], F32R), sb("xt_lo", [P, KD, P], F32R)
        act_g, hid = sb("act_gate", [P, D_EXP]), sb("hidden", [P, D_EXP])
        h_hi, h_lo = sb("ht_hi", [P, KE, P], F32R), sb("ht_lo", [P, KE, P], F32R)
        y = sb("y_tile", [P, D])
        psum = lambda n, s: ctx.enter_context(nc.psum_tensor(n, s, F32))
        ps_x, ps_g, ps_u, ps_h, ps_y = (psum("ps_x", [P, KD, P]), psum("ps_g", [P, D_EXP]), psum("ps_u", [P, D_EXP]),
                                        psum("ps_h", [P, KE, P]), psum("ps_y", [P, D]))
        x_gathered = S.x_gathered
        x_turned, xh_ready, xl_ready = (sem(n) for n in (
            "x_turned", "xh_ready", "xl_ready"))
        silu_ready, hid_ready, hid_turned, hh_ready, hl_ready = (sem(n) for n in (
            "silu_ready", "hid_ready", "hid_turned", "hh_ready", "hl_ready"))
        y_left, y_stored = sem("y_left"), sem("y_stored")
        final_of = lambda eng: eng.value_load(S.last_item[0:1, 0:1], min_val=EXPERTS - 1, max_val=ITEMS - 1)
        expert_of = lambda eng, i: eng.value_load(S.item_expert[0:1, bass.ds(i, 1)], min_val=0, max_val=EXPERTS - 1)
        kgu = PIECE // D_EXP
        kdn = PIECE // D
        with nc.Block() as block:

            @block.sync
            def _(sp):
                with sp.Fori(1, EXPERTS - 1) as e:
                    for s in GATE + UP:
                        load_piece(sp, S, s, e + 1, expert_piece(S, s, bass.ds(e + 1, 1)))
                    for s in DOWN:
                        load_piece(sp, S, s, e, expert_piece(S, s, bass.ds(e, 1)))
                for s in DOWN:
                    load_piece(sp, S, s, EXPERTS - 1, expert_piece(S, s, slice(EXPERTS - 1, EXPERTS)))
                for s in range(5):
                    w, k = (ple_gate, 2 * s) if s < 4 else (ple_proj, 0)
                    sp.wait_ge(w_split[s], EXPERTS + 1)
                    sp.dma_start(S.w_raw[s].rearrange("p (k n) -> p k n", n=D), w[:, k:k + 2, :]).then_inc(S.raw_loaded[s], 16)
                for rows, src in zip((S.g_ple_rows, S.b_ple_rows, S.g_final_rows), gains):
                    sp.dma_start(rows[:, :], src.partition_broadcast(P)).then_inc(S.ple_rows_loaded, 16)
                sp.dma_start(S.p_in[:, :], p_prompt[0, 0, 0:P, :]).then_inc(S.p_loaded, 16)
                sp.wait_ge(S.ple_rows_loaded, 48)
                sp.wait_ge(S.raw_loaded[4], (EXPERTS + 1) * 16)

            @block.gpsimd
            def _(pool):
                n_last = final_of(pool)

                def gather(i):
                    pool.wait_ge(S.x_gathered, i * 16)
                    pool.wait_ge(x_turned, i)
                    pool.sem_inc(S.waits_met, 1)
                    gather_tokens(pool, S, i)

                gather(1)
                with pool.Fori(1, n_last) as i:
                    gather(i + 1)
                    e, last = expert_of(pool, i), expert_of(pool, i - 1)
                    with pool.If(e != last):
                        piece_lo(pool, S, e, 3)
                with pool.If(expert_of(pool, n_last - 1) != EXPERTS - 1):
                    piece_lo(pool, S, EXPERTS - 1, 3)
                piece_lo(pool, S, EXPERTS, 3)

            @block.scalar
            def _(act):
                end = final_of(act)

                def take_hi(now, before, slots, items):
                    with act.If(now != before):
                        for s in slots:
                            piece_hi(act, S, now, s, items)

                def x_to_hi(i):
                    act.wait_ge(x_turned, i + 1)
                    act.activation(x_hi[:, :, :], ps_x[:, :, :], ACT.Copy).then_inc(xh_ready, 1)

                def leave_y(i):
                    act.wait_ge(w_used[5], i + 1)
                    act.wait_ge(y_stored, i * 16 + 16)
                    act.activation(y[:, :], ps_y[:, :], ACT.Copy).then_inc(y_left, 1)
                    act.wait_ge(y_left, i + 2)
                    act.dma_start(S.y_rows[bass.ds(i * P, P), :], y[:, :]).then_inc(y_stored, 16)

                def iteration(i, first=False, final=False):
                    if first:
                        take_hi(expert_of(act, 1), 0, GATE, 1)
                    act.wait_ge(w_used[1], i + 1)
                    act.activation(act_g[:, :], ps_g[:, :], ACT.Silu).then_inc(silu_ready, 1)
                    e = 0 if first else expert_of(act, i)
                    if final:
                        for s in GATE + UP:
                            piece_hi(act, S, EXPERTS, s, i + 1)
                    else:
                        take_hi(expert_of(act, i + 1), e, UP if first else GATE + UP, i + 1)
                        x_to_hi(i + 1)
                    if not first:
                        take_hi(e, expert_of(act, i - 1), DOWN, i)
                        leave_y(i - 1)
                    act.wait_ge(hid_turned, i + 1)
                    act.activation(h_hi[:, :, :], ps_h[:, :, :], ACT.Copy).then_inc(hh_ready, 1)

                act.sem_inc(y_left, 1)
                act.sem_inc(y_stored, 16)
                x_to_hi(0)
                iteration(0, first=True)
                with act.Fori(1, end) as i:
                    iteration(i)
                iteration(end, final=True)
                leave_y(end)
                act.wait_ge(y_stored, end * 16 + 32)
                act.sem_inc(S.waits_met, 1)

            @block.vector
            def _(dve):
                end = final_of(dve)

                def take_lo(now, before, slots):
                    with dve.If(now != before):
                        for s in slots:
                            piece_lo(dve, S, now, s)

                def x_to_lo(i):
                    dve.wait_ge(xh_ready, i + 1)
                    dve.tensor_tensor(x_lo[:, :, :], ps_x[:, :, :], x_hi[:, :, :].bitcast(F32), ALU.subtract)\
                       .then_inc(xl_ready, 1)

                def iteration(i, first=False, final=False):
                    e = 0 if first else expert_of(dve, i)
                    if final:
                        for s in (0, 1, 2):
                            piece_lo(dve, S, EXPERTS, s)
                    else:
                        take_lo(expert_of(dve, i + 1), e, (0, 1, 2))
                    dve.wait_ge(silu_ready, i + 1)
                    dve.wait_ge(w_used[3], i + 1)
                    dve.tensor_tensor(hid[:, :], ps_u[:, :], act_g[:, :], ALU.mult).then_inc(hid_ready, 1)
                    if not final:
                        x_to_lo(i + 1)
                    if not first:
                        take_lo(e, expert_of(dve, i - 1), DOWN)
                    dve.wait_ge(hh_ready, i + 1)
                    dve.tensor_tensor(h_lo[:, :, :], ps_h[:, :, :], h_hi[:, :, :].bitcast(F32), ALU.subtract)\
                       .then_inc(hl_ready, 1)

                x_to_lo(0)
                iteration(0, first=True)
                with dve.Fori(1, end) as i:
                    iteration(i)
                iteration(end, final=True)

            @block.tensor
            def _(pe):
                end = final_of(pe)

                def turn_x(i):
                    pe.wait_ge(x_gathered, i * 16 + 16)
                    for k in range(KD):
                        last = pe.transpose(ps_x[:, k, :], x[:, k * P:(k + 1) * P], S.ident[:, :])
                    last.then_inc(x_turned, 1)

                def gate_up(i, e):
                    pe.wait_ge(xl_ready, i + 1)
                    for slots, ps in ((GATE, ps_g), (UP, ps_u)):
                        for s in slots:
                            pe.wait_ge(w_split[s], e + 2)
                            for j in range(kgu):
                                k = (s % 2) * kgu + j
                                cols = slice(j * D_EXP, (j + 1) * D_EXP)
                                last = matmul3(pe, ps[:, :], x_hi[:, k, :], x_lo[:, k, :], w_hi[s][:, cols],
                                               w_lo[s][:, cols], k == 0, k == KD - 1)
                            last.then_inc(w_used[s], 1)

                def down(i, e):
                    pe.wait_ge(hl_ready, i + 1)
                    pe.wait_ge(y_left, i + 1)
                    for s in DOWN:
                        pe.wait_ge(w_split[s], e + 2)
                        for j in range(kdn):
                            k = (s % 2) * kdn + j
                            for h in range(2):
                                cols = slice(j * D + h * 512, j * D + (h + 1) * 512)
                                last = matmul3(pe, ps_y[:, h * 512:(h + 1) * 512], h_hi[:, k, :], h_lo[:, k, :],
                                               w_hi[s][:, cols], w_lo[s][:, cols], k == 0, k == KE - 1)
                        last.then_inc(w_used[s], 1)

                def turn_hid(i):
                    pe.wait_ge(hid_ready, i + 1)
                    for k in range(KE):
                        last = pe.transpose(ps_h[:, k, :], hid[:, k * P:(k + 1) * P], S.ident[:, :])
                    last.then_inc(hid_turned, 1)

                turn_x(0)
                gate_up(0, 0)
                turn_x(1)
                turn_hid(0)
                with pe.Fori(1, end) as i:
                    gate_up(i, expert_of(pe, i))
                    turn_x(i + 1)
                    down(i - 1, expert_of(pe, i - 1))
                    turn_hid(i)
                gate_up(end, EXPERTS - 1)
                down(end - 1, expert_of(pe, end - 1))
                turn_hid(end)
                down(end, EXPERTS - 1)


def embedding_gate(nc, S, p_prompt, p_sample, y_prompt, y_sample):
    KP = PLE // P
    with ExitStack() as ctx:
        sb = lambda n, s, d=F32: ctx.enter_context(nc.sbuf_tensor(n, s, d))
        sem = lambda n: S.stack.enter_context(nc.semaphore(n))
        x3_pair = S.w_raw[0].rearrange("p (j n) -> p j n", n=D)
        room = [S.w_raw[s][:, h * D:(h + 1) * D] for s in (1, 2, 3, 5) for h in range(2)]
        x3 = lambda t: x3_pair[:, t % 2, :] if type(t) is int else x3_pair[:, bass.ds(t % 2, 1), :]
        x2, y1, y2, h3, sgm, x4, out, junk1 = room
        junk2 = sb("junk62", [P, D])
        g_rows, b_rows, f_rows, p_in, p_loaded = S.g_ple_rows, S.b_ple_rows, S.g_final_rows, S.p_in, S.p_loaded
        h_hi, h_lo = sb("h3t_hi", [P, KD, P], F32R), sb("h3t_lo", [P, KD, P], F32R)
        p_hi, p_lo = sb("pt_hi", [P, KP, P], F32R), sb("pt_lo", [P, KP, P], F32R)
        rows = sb("gather_rows", [P, 2], I32)
        gate = sb("gate_cols", [P, 2])
        ss, ms, rstd = sb("ss6", [P, 2]), sb("ms6", [P, 2]), sb("rstd6", [P, 2])
        psum = lambda n, s: ctx.enter_context(nc.psum_tensor(n, s, F32))
        ps_g, ps_p, ps_h, ps_pt = psum("ps_gate", [P, D]), psum("ps_proj", [P, D]), psum("ps_h3t", [P, KD, P]), psum("ps_pt", [P, KP, P])
        proj_hi_ready, proj_ready = sem("proj_hi_ready"), sem("proj_ready")
        x2_loaded, y1_in, y2_in, picked = (sem(n) for n in ("x2_in_loaded", "y1_gathered", "y2_gathered", "picked"))
        x3_part, x3_ready, h3_ready, turned, p_turned = (sem(n) for n in (
            "x3_part", "x3_ready", "h3_ready", "h3_turned", "p_turned"))
        hi_ready, lo_ready, p_hi_ready, p_lo_ready = (sem(n) for n in ("h3_hi", "h3_lo", "p_hi_ready", "p_lo_ready"))
        squared, mean_ready, rstd_ready = ([sem(f"{n}{i}") for i in range(2)] for n in ("sq6_", "ms6_", "rstd6_"))
        gates, biased, sig_ready, projected, scaled = (sem(n) for n in ("gates_ready", "biased", "sig6_ready", "projected", "scaled6"))
        x4_ready, out_ready, out_stored = sem("x4_ready"), sem("out_ready"), sem("out_stored")

        def weights(halves, k, half):
            return halves[k // 2][:, (k % 2) * D + half.start:(k % 2) * D + half.stop]

        with nc.Block() as block:

            @block.sync
            def _(sp):
                def loads(t, p_src, rows_of):
                    sp.wait_ge(x3_part, t)
                    sp.dma_start(x2[:, :], S.x2_rows[bass.ds(t * P, P), :]).then_inc(x2_loaded, 16)
                    sp.wait_ge(p_turned, t)
                    sp.dma_start(p_in[rows_of, :], p_src).then_inc(p_loaded, 16)

                def store(t, dst, rows_of):
                    sp.wait_ge(out_ready, t + 1)
                    sp.dma_start(dst, out[rows_of, :]).then_inc(out_stored, 16)

                whole, sample = slice(0, P), slice(GAP, GAP + DEC)
                sp.sem_inc(out_stored, 16)
                sp.dma_start(x2[:, :], S.x2_rows[0:P, :]).then_inc(x2_loaded, 16)
                loads(1, p_prompt[0, 0, P:2 * P, :], whole)
                with sp.Fori(0, TILES - 3) as t:
                    loads(t + 2, p_prompt[0, 0, bass.ds(t * P + 2 * P, P), :], whole)
                    store(t, y_prompt[0, bass.ds(t * P, P), :], whole)
                loads(TILES - 1, p_sample[0, 0], sample)
                for t in (TILES - 3, TILES - 2):
                    store(t, y_prompt[0, t * P:(t + 1) * P, :], whole)
                store(TILES - 1, y_sample[0], sample)
                sp.wait_ge(out_stored, 16 * (TILES + 1))

            @block.gpsimd
            def _(pool):
                def fetch(t):
                    pool.tensor_copy(rows[:, :], S.out_row[:, :, bass.ds(t, 1)])
                    pool.tensor_copy(gate[:, :], S.gate[:, :, bass.ds(t, 1)]).then_inc(picked, 1)
                    pool.wait_ge(picked, t + 1)
                    pool.sem_inc(S.waits_met, 1)
                    for k, (dst, got) in enumerate(((y1, y1_in), (y2, y2_in))):
                        pool.indirect_dma_start(out=dst[:, :], out_offset=None, in_=S.y_rows[:, :],
                                                in_offset=bass.IndirectOffsetOnAxis(ap=rows[:, k:k + 1], axis=0)).then_inc(got, 16)

                def norm1(t):
                    pool.wait_ge(mean_ready[0], t + 1)
                    pool.tensor_tensor(rstd[:, 0:1], ms[:, 0:1], S.minus_half[:, 0:1], ALU.pow).then_inc(rstd_ready[0], 1)

                def norm2(t):
                    pool.wait_ge(mean_ready[1], t + 1)
                    pool.tensor_tensor(rstd[:, 1:2], ms[:, 1:2], S.minus_half[:, 0:1], ALU.pow).then_inc(rstd_ready[1], 1)

                def refetch(t):
                    pool.wait_ge(y1_in, t * 16)
                    pool.wait_ge(y2_in, t * 16)
                    pool.wait_ge(x3_ready, t)
                    pool.sem_inc(S.waits_met, 1)
                    fetch(t)

                fetch(0)
                norm1(0)
                refetch(1)
                with pool.Fori(0, TILES - 2) as t:
                    norm1(t + 1)
                    refetch(t + 2)
                    norm2(t)
                norm1(TILES - 1)
                norm2(TILES - 2)
                norm2(TILES - 1)

            @block.scalar
            def _(act):
                def square(t, j):
                    if type(t) is not int or t > 0:
                        act.wait_ge(squared[j], t)
                    act.wait_ge((x3_ready, x4_ready)[j], t + 1 + j)
                    act.activation((junk1, junk2)[j][:, :], (x3(t), x4[:, :])[j], ACT.Square, accum_out=ss[:, j:j + 1])\
                       .then_inc(squared[j], 1)

                def to_hi(t):
                    act.wait_ge(turned, t + 1)
                    act.activation(h_hi[:, :, :], ps_h[:, :, :], ACT.Copy).then_inc(hi_ready, 1)

                def p_to_hi(t):
                    act.wait_ge(p_turned, t + 1)
                    if type(t) is not int or t > 0:
                        act.wait_ge(projected, t)
                    act.activation(p_hi[:, :, :], ps_pt[:, :, :], ACT.Copy).then_inc(p_hi_ready, 1)

                def sigmoid(t):
                    act.wait_ge(biased, t + 1)
                    act.activation(sgm[:, :], sgm[:, :], ACT.Sigmoid).then_inc(sig_ready, 1)

                act.activation(S.w_hi[4][:, :], S.w_raw[4], ACT.Copy).then_inc(proj_hi_ready, 1)
                p_to_hi(0)
                square(0, 0)
                to_hi(0)
                def iteration(t):
                    square(t + 1, 0)
                    to_hi(t + 1)
                    sigmoid(t)
                    p_to_hi(t + 1)
                    square(t, 1)

                iteration(0)
                with act.Fori(1, TILES - 1) as t:
                    iteration(t)
                sigmoid(TILES - 1)
                square(TILES - 1, 1)

            @block.vector
            def _(dve):
                def combine(t):
                    dve.wait_ge(picked, t + 1)
                    dve.wait_ge(x2_loaded, t * 16 + 16)
                    dve.wait_ge(y1_in, t * 16 + 16)
                    if type(t) is not int or t > 0:
                        dve.wait_ge(x4_ready, t)
                    dve.scalar_tensor_tensor(x3(t), y1[:, :], gate[:, 0:1], x2[:, :], ALU.mult, ALU.add).then_inc(x3_part, 1)
                    dve.wait_ge(y2_in, t * 16 + 16)
                    dve.wait_ge(x3_part, t + 1)
                    dve.scalar_tensor_tensor(x3(t), y2[:, :], gate[:, 1:2], x3(t), ALU.mult, ALU.add).then_inc(x3_ready, 1)

                def mean(t, j):
                    dve.wait_ge(squared[j], t + 1)
                    dve.tensor_scalar(ms[:, j:j + 1], ss[:, j:j + 1], 1.0 / D, EPS, ALU.mult, ALU.add).then_inc(mean_ready[j], 1)
                    dve.wait_ge(rstd_ready[j], t + 1)

                def norm(t):
                    mean(t, 0)
                    dve.scalar_tensor_tensor(h3[:, :], x3(t), rstd[:, 0:1], g_rows[:, :], ALU.mult, ALU.mult)\
                       .then_inc(h3_ready, 1)

                def to_lo(t):
                    dve.wait_ge(hi_ready, t + 1)
                    dve.tensor_tensor(h_lo[:, :, :], ps_h[:, :, :], h_hi[:, :, :].bitcast(F32), ALU.subtract).then_inc(lo_ready, 1)

                def p_to_lo(t):
                    dve.wait_ge(p_hi_ready, t + 1)
                    dve.tensor_tensor(p_lo[:, :, :], ps_pt[:, :, :], p_hi[:, :, :].bitcast(F32), ALU.subtract).then_inc(p_lo_ready, 1)

                def bias(t):
                    dve.wait_ge(gates, t + 1)
                    dve.tensor_tensor(sgm[:, :], ps_g[:, :], b_rows[:, :], ALU.add).then_inc(biased, 1)

                def finish(t):
                    dve.wait_ge(sig_ready, t + 1)
                    dve.wait_ge(projected, t + 1)
                    dve.tensor_tensor(x4[:, :], ps_p[:, :], sgm[:, :], ALU.mult).then_inc(scaled, 1)
                    dve.wait_ge(scaled, t + 1)
                    dve.tensor_tensor(x4[:, :], x4[:, :], x3(t), ALU.add).then_inc(x4_ready, 1)

                def final(t):
                    mean(t, 1)
                    dve.wait_ge(out_stored, t * 16 + 16)
                    dve.scalar_tensor_tensor(out[:, :], x4[:, :], rstd[:, 1:2], f_rows[:, :], ALU.mult, ALU.mult)\
                       .then_inc(out_ready, 1)

                dve.sem_inc(x4_ready, 1)
                dve.wait_ge(proj_hi_ready, 1)
                dve.tensor_tensor(S.w_lo[4][:, :], S.w_raw[4], S.w_hi[4][:, :].bitcast(F32), ALU.subtract)\
                   .then_inc(proj_ready, 1)
                p_to_lo(0)
                combine(0)
                norm(0)
                to_lo(0)
                combine(1)

                def iteration(t, more=True):
                    norm(t + 1)
                    bias(t)
                    to_lo(t + 1)
                    finish(t)
                    p_to_lo(t + 1)
                    if more:
                        combine(t + 2)
                    final(t)

                with dve.Fori(0, TILES - 2) as t:
                    iteration(t)
                iteration(TILES - 2, more=False)
                bias(TILES - 1)
                finish(TILES - 1)
                final(TILES - 1)

            @block.tensor
            def _(pe):
                def turn_h(t):
                    pe.wait_ge(h3_ready, t + 1)
                    for k in range(KD):
                        last = pe.transpose(ps_h[:, k, :], h3[:, k * P:(k + 1) * P], S.ident[:, :])
                    last.then_inc(turned, 1)

                def turn_p(t):
                    pe.wait_ge(p_loaded, t * 16 + 16)
                    for k in range(KP):
                        last = pe.transpose(ps_pt[:, k, :], p_in[:, k * P:(k + 1) * P], S.ident[:, :])
                    last.then_inc(p_turned, 1)

                def gate_products(t):
                    pe.wait_ge(lo_ready, t + 1)
                    for k in range(KD):
                        for h in range(2):
                            half = slice(h * 512, (h + 1) * 512)
                            last = matmul3(pe, ps_g[:, half], h_hi[:, k, :], h_lo[:, k, :],
                                           weights(S.w_hi, k, half), weights(S.w_lo, k, half), k == 0, k == KD - 1)
                    last.then_inc(gates, 1)

                def proj_products(t):
                    pe.wait_ge(p_lo_ready, t + 1)
                    for k in range(KP):
                        for h in range(2):
                            half = slice(h * 512, (h + 1) * 512)
                            last = matmul3(pe, ps_p[:, half], p_hi[:, k, :], p_lo[:, k, :],
                                           weights(S.w_hi, KD + k, half), weights(S.w_lo, KD + k, half), k == 0, k == KP - 1)
                    last.then_inc(projected, 1)

                turn_p(0)
                pe.wait_ge(proj_ready, 1)
                proj_products(0)
                turn_h(0)
                gate_products(0)
                turn_h(1)
                turn_p(1)
                with pe.Fori(1, TILES - 1) as t:
                    gate_products(t)
                    turn_h(t + 1)
                    turn_p(t + 1)
                    proj_products(t)
                gate_products(TILES - 1)
                proj_products(TILES - 1)


def build(nc, i, o):
    S = Shared()
    S.x2_rows = nc.dram_tensor("x2_rows", [ROWS, D], F32).ap()
    S.h2_rows = nc.dram_tensor("h2_rows", [ROWS, D], F32).ap()
    S.y_rows = nc.dram_tensor("y_rows", [ITEMS * P, D], F32).ap()
    S.conv_p, S.pool_p, S.conv_s, S.pool_s = o["conv_p"], o["pool_p"], o["conv_s"], o["pool_s"]
    with ExitStack() as whole:
        S.stack = whole
        sb = lambda n, s, d=F32, at=whole: at.enter_context(nc.sbuf_tensor(n, s, d))
        S.ident, S.ones, S.minus_half = sb("ident", [P, P]), sb("ones", [P, P]), sb("minus_half", [P, 4])
        S.zero = sb("zero_rows", [P, P])
        S.gate, S.out_row = sb("gates", [P, 2, TILES]), sb("out_rows", [P, 2, TILES], I32)
        S.last_item, S.item_expert = sb("last_item", [P, 1], I32), sb("item_expert", [P, ITEMS + 1], I32)
        S.item_tokens = sb("item_tokens", [P, ITEMS], I32)
        S.mix_w_loaded = whole.enter_context(nc.semaphore("mix_w_loaded"))
        S.waits_met = whole.enter_context(nc.semaphore("waits_met"))
        S.routed = whole.enter_context(nc.semaphore("routed"))
        S.raw_loaded, S.w_hi_ready, S.w_split, S.w_used = (
            [whole.enter_context(nc.semaphore(f"{n}{s}")) for s in range(6)] for n in
            ("raw_loaded", "w_hi_ready", "w_split", "w_used"))
        S.w_experts = (i["w_exp_gate"], i["w_exp_up"], i["w_exp_down"])
        S.par = sb("par", [P, KC, P_ALL])
        region = sb("mixer_or_raw_weights", [P, 6 * PIECE])
        at = [0]

        def part(width, *shape):
            flat = region[:, at[0]:at[0] + width * shape[0]]
            at[0] += width * shape[0]
            return flat.rearrange("p (k n) -> p k n", n=width)

        S.conv, S.pooled = part(COLS, KC), part(COLS, KC)
        S.w_pw, S.w_pool = part(CH, KC), part(P, KC)
        S.state_rows = region[0:90, at[0]:at[0] + CH]
        assert at[0] + CH <= 6 * PIECE
        S.state_stored, S.y_cleared = (whole.enter_context(nc.semaphore(n)) for n in ("state_stored", "y_cleared"))
        S.w_raw = [region[:, s * PIECE:(s + 1) * PIECE] for s in range(6)]
        S.room = [S.w_raw[s][:, h * D:(h + 1) * D] for s in range(6) for h in range(2)]
        S.w_in = i["w_in"][0].rearrange("(k p) n -> p k n", p=P)
        S.w_in_loaded, S.w_in_hi_ready, S.w_in_split = (
            [whole.enter_context(nc.semaphore(f"{n}{s}")) for s in range(PARTS)] for n in
            ("w_in_loaded", "w_in_hi_ready", "w_in_split"))
        with ExitStack() as hs:
            S.w_in_raw = [sb(f"w_in_raw{s}", [P, KD, P], F32, hs) for s in range(PARTS)]
            S.w_in_hi = [sb(f"w_in_hi{s}", [P, KD, P], F32R, hs) for s in range(PARTS)]
            S.w_in_lo = [sb(f"w_in_lo{s}", [P, KD, P], F32R, hs) for s in range(PARTS)]
            S.h_hi, S.h_lo = sb("h_hi", [P, KD, ROWS], F32R, hs), sb("h_lo", [P, KD, ROWS], F32R, hs)
            constants_and_norm(nc, S, i["x_prompt"], i["x_sample"], i["state_conv"], i["state_pool"], i["g_mix"],
                               i["w_dw"], i["b_dw"], i["g_conv_ln"], i["b_conv_ln"], i["b_pw"], i["pool_scale"])
            in_projection_conv_pool(nc, S, i["w_pw"], i["w_pool"])
        with ExitStack() as routed:
            with ExitStack() as back:
                S.o = sb("o_channels", [P, KD, ROWS], F32, back)
                S.wo_hi, S.wo_lo = sb("w_out_hi", [P, KD, D], F32R, back), sb("w_out_lo", [P, KD, D], F32R, back)
                mixer_outputs(nc, S, i["w_out"])
                S.ps_route = routed.enter_context(nc.psum_tensor("ps_route", [P, TILES, GROUPS + EXPERTS], F32))
                out_projection(nc, S, i["x_prompt"], i["x_sample"], i["g_ffn"], i["w_route_group"], i["w_route_expert"])
            S.w_hi = [sb(f"w_hi{s}", [P, PIECE], F32R) for s in range(6)]
            S.w_lo = [sb(f"w_lo{s}", [P, PIECE], F32R) for s in range(6)]
            S.ids, S.x_tokens = sb("token_ids", [P, 1], I32), sb("x_tokens", [P, D])
            S.ids_ready, S.tokens_ready, S.x_gathered = (
                whole.enter_context(nc.semaphore(n)) for n in ("ids_ready", "tokens_ready", "x_gathered"))
            routing(nc, S, i["b_route_group"], i["b_route_expert"])
        blocks = lambda w: w[0].rearrange("(k p) n -> p k n", p=P)
        S.g_ple_rows, S.b_ple_rows, S.g_final_rows = (sb(n, [P, D]) for n in ("g_ple_rows", "b_ple_rows", "g_final_rows"))
        S.p_in = sb("p_in", [P, PLE])
        S.ple_rows_loaded, S.p_loaded = (whole.enter_context(nc.semaphore(n)) for n in ("ple_rows_loaded", "p_loaded"))
        experts(nc, S, blocks(i["w_ple_gate"]), blocks(i["w_ple_proj"]),
                (i["g_ple"][0], i["b_ple_gate"][0], i["g_final"]), i["p_prompt"])
        embedding_gate(nc, S, i["p_prompt"], i["p_sample"], o["y_prompt"], o["y_sample"])


_OUTS = {
    "y_prompt": (1, SEQ, D), "y_sample": (1, DEC, D), "conv_p": (1, 1, CONV_HIST, CH), "pool_p": (1, 1, POOL_HIST, CH),
    "conv_s": (1, 1, CONV_HIST, CH), "pool_s": (1, 1, POOL_HIST, CH),
}


def kernel(**inputs):
    import numpy as np
    import concourse.bacc as bacc
    from concourse.bass_utils import run_bass_kernel_spmd

    nc = bacc.Bacc("TRN2", target_bir_lowering=False, num_devices=1)
    arrays = {n: np.ascontiguousarray(a) for n, a in inputs.items()}
    ins = {n: nc.dram_tensor(n, a.shape, mybir.dt.from_np(a.dtype), kind="ExternalInput").ap() for n, a in arrays.items()}
    outs = {n: nc.dram_tensor(n, s, F32, kind="ExternalOutput").ap() for n, s in _OUTS.items()}
    build(nc, ins, outs)
    r = run_bass_kernel_spmd(nc, [arrays], core_ids=[0])
    return tuple(r.results[0][n] for n in _OUTS)
```
